# Optimizing a Trainium2 kernel written in Bass

```python
import math
import jax
import jax.numpy as jnp
from jax import lax
import numpy as np

D_MODEL = 1024
BATCH = 1
SEQ = 256
DEPTH = 1
DEC_BATCH = 8
DEC_SEQ = 8
PAST_LEN = 1024
PAGE_SIZE = 128

M_HEADS = 4
M_DV = 256
M_DQK = 128
M_WIDTH = M_HEADS * M_DV
M_CONV = 4
M_CHUNK = 64
N_HEADS = 16
N_KV = 2
N_HD = 64
N_HPG = N_HEADS // N_KV
N_WIDTH = N_HEADS * N_HD
KV_W = N_KV * N_HD
CMP_LEN = 32
CMP_STRIDE = 16
SLC_BLOCK = 64
N_SELECT = 16
WINDOW = 512
NSA_Q_BLOCK = 16
FORCE_BONUS = 1000.0
N_EXPERTS = 32
TOP_K = 4
D_EXPERT = 1024
SWIGLU_LIMIT = 7.0
SWIGLU_ALPHA = 1.702
MOE_BLOCK = 128
EPS = 1e-6
TINY = 1e-30

OFF_MX = 0
OFF_MV = OFF_MX + M_WIDTH
OFF_MO = OFF_MV + M_WIDTH
OFF_MI = OFF_MO + M_WIDTH
OFF_MF = OFF_MI + M_HEADS
OFF_NQ = OFF_MF + M_HEADS
OFF_NKV = OFF_NQ + N_WIDTH
OFF_NG = OFF_NKV + 6 * KV_W
OFF_BG = OFF_NG + 3 * N_HEADS
N_IN = OFF_BG + 2 * D_MODEL

kernel_name = 'mlstm_nsa_moe_hybrid_step'

def rmsnorm(x, g):
    xf = x.astype(jnp.float32)
    y = xf * lax.rsqrt(jnp.mean(xf * xf, axis=-1, keepdims=True) + EPS)
    return (y * g).astype(x.dtype)

def masked_softmax(s, mask, axes):
    s = jnp.where(mask, s, -jnp.inf)
    mx = jnp.max(s, axis=axes, keepdims=True)
    mx = jnp.where(jnp.isfinite(mx), mx, 0.0)
    p = jnp.exp(s - mx)
    return p / jnp.maximum(jnp.sum(p, axis=axes, keepdims=True), TINY)

def project_in(xn, w_in, b_in):
    z = xn @ w_in + b_in
    B, T = z.shape[:2]
    q = z[..., OFF_NQ:OFF_NKV].reshape(B, T, N_HEADS, N_HD)
    kv = z[..., OFF_NKV:OFF_NG].reshape(B, T, 6, N_KV, N_HD)
    gates = jax.nn.sigmoid(z[..., OFF_NG:OFF_BG].astype(jnp.float32)).reshape(B, T, N_HEADS, 3)
    return z, q, kv, gates

def causal_conv(x, buf, w, b):
    T = x.shape[1]
    xp = jnp.concatenate([buf, x], axis=1)
    y = sum(xp[:, j:j + T] * w[j] for j in range(M_CONV)) + b
    return y, xp[:, -(M_CONV - 1):]

def mlstm_scan(q, k, v, ig, lf, C0, n0, m0):
    B, T, H, _ = q.shape
    L = math.gcd(T, M_CHUNK)
    nc = T // L

    def to_chunks(a):
        return a.reshape((B, nc, L) + a.shape[2:]).swapaxes(0, 1)

    causal = jnp.tril(jnp.ones((L, L), dtype=bool))

    def step(carry, xs):
        C, n, m = carry
        qc, kc, vc, ic, fc = xs
        b = jnp.cumsum(fc, axis=1)
        a = b + m[:, None, :]
        dmat = b[:, :, None, :] - b[:, None, :, :] + ic[:, None, :, :]
        dmat = jnp.where(causal[None, :, :, None], dmat, -jnp.inf)
        mt = jnp.maximum(a, jnp.max(dmat, axis=2))
        w_intra = jnp.exp(dmat - mt[:, :, None, :])
        w_inter = jnp.exp(a - mt)
        qk = jnp.einsum('bthd,bshd->btsh', qc, kc) * w_intra
        num = jnp.einsum('btsh,bshv->bthv', qk, vc) + w_inter[..., None] * jnp.einsum('bthd,bhdv->bthv', qc, C)
        den = jnp.sum(qk, axis=2) + w_inter * jnp.einsum('bthd,bhd->bth', qc, n)
        h = num / jnp.maximum(jnp.abs(den), jnp.exp(-mt))[..., None]
        m_new = mt[:, -1]
        w_end = jnp.exp(dmat[:, -1] - m_new[:, None, :])
        decay = jnp.exp(a[:, -1] - m_new)
        C_new = decay[..., None, None] * C + jnp.einsum('bsh,bshd,bshv->bhdv', w_end, kc, vc)
        n_new = decay[..., None] * n + jnp.einsum('bsh,bshd->bhd', w_end, kc)
        return (C_new, n_new, m_new), h

    xs = (to_chunks(q), to_chunks(k), to_chunks(v), to_chunks(ig), to_chunks(lf))
    (C, n, m), h = lax.scan(step, (C0, n0, m0), xs)
    return h.swapaxes(0, 1).reshape(B, T, H, M_DV), C, n, m

def mlstm_branch(z, conv_buf, C0, n0, m0, w_conv, b_conv, w_mq, w_mk, g_mnorm):
    f32 = jnp.float32
    B, T = z.shape[:2]
    xm = z[..., OFF_MX:OFF_MV]
    v = z[..., OFF_MV:OFF_MO].reshape(B, T, M_HEADS, M_DV).astype(f32)
    o = jax.nn.sigmoid(z[..., OFF_MO:OFF_MI].astype(f32))
    ig = z[..., OFF_MI:OFF_MF].astype(f32)
    lf = jax.nn.log_sigmoid(z[..., OFF_MF:OFF_NQ].astype(f32))
    xc, new_buf = causal_conv(xm, conv_buf.astype(xm.dtype), w_conv, b_conv)
    xc = jax.nn.silu(xc.astype(f32)).reshape(B, T, M_HEADS, M_DV)
    q = jnp.einsum('bthc,hcd->bthd', xc, w_mq.astype(f32))
    k = jnp.einsum('bthc,hcd->bthd', xc, w_mk.astype(f32)) * (M_DQK ** -0.5)
    h, C, n, m = mlstm_scan(q, k, v, ig, lf, C0.astype(f32), n0.astype(f32), m0.astype(f32))
    hn = h * lax.rsqrt(jnp.mean(h * h, axis=-1, keepdims=True) + EPS) * g_mnorm
    return hn.reshape(B, T, M_WIDTH) * o, new_buf, C, n, m

def cmp_segments(rows, w):
    B, L = rows.shape[:2]
    R = CMP_LEN // CMP_STRIDE
    nseg = L // CMP_STRIDE
    seg = rows[:, :nseg * CMP_STRIDE].reshape(B, nseg, CMP_STRIDE, N_KV, N_HD)
    return jnp.einsum('bnsgd,rsde->rbnge', seg, w.reshape(R, CMP_STRIDE, N_HD, N_HD))

def cmp_blocks(segs, b):
    R = CMP_LEN // CMP_STRIDE
    nc = segs.shape[2] - R + 1
    return sum(segs[r, :, r:r + nc] for r in range(R)) + b

def cmp_to_slc_matrix(nc, ns):
    c0 = np.arange(nc)[:, None] * CMP_STRIDE
    s0 = np.arange(ns)[None, :] * SLC_BLOCK
    ov = np.clip(np.minimum(c0 + CMP_LEN, s0 + SLC_BLOCK) - np.maximum(c0, s0), 0, None)
    return jnp.asarray(ov / CMP_LEN, dtype=jnp.float32)

def to_blocks(a):
    B, L = a.shape[:2]
    ns = -(-L // SLC_BLOCK)
    a = jnp.pad(a, [(0, 0), (0, ns * SLC_BLOCK - L)] + [(0, 0)] * (a.ndim - 2))
    return a.reshape((B, ns, SLC_BLOCK) + a.shape[2:])

def nsa_attend(q, qpos, ck, cv, ns, gather_sel, wk, wv, wpos, gates):
    f32 = jnp.float32
    B, T = q.shape[:2]
    nc = ck.shape[1]
    qg = q.reshape(B, T, N_KV, N_HPG, N_HD).astype(f32) * (N_HD ** -0.5)
    c_end = jnp.arange(nc) * CMP_STRIDE + (CMP_LEN - 1)
    cmask = (c_end[None, :] <= qpos[:, None])[None, :, None, None, :]
    p_cmp = masked_softmax(jnp.einsum('btghd,bcgd->btghc', qg, ck.astype(f32)), cmask, (-1,))
    o_cmp = jnp.einsum('btghc,bcgd->btghd', p_cmp, cv.astype(f32))
    imp = jnp.einsum('btgc,cn->btgn', jnp.sum(p_cmp, axis=3), cmp_to_slc_matrix(nc, ns))
    blk = jnp.arange(ns)[None, :]
    cur = (qpos // SLC_BLOCK)[:, None]
    allowed = blk <= cur
    forced = (blk == 0) | (blk == cur) | (blk == cur - 1)
    score = jnp.where(allowed[None, :, None, :], imp + FORCE_BONUS * forced[None, :, None, :], -jnp.inf)
    top_s, idx = lax.top_k(score, min(N_SELECT, ns))
    idx = idx.transpose(0, 2, 1, 3)
    ok = jnp.isfinite(top_s).transpose(0, 2, 1, 3)
    ksel, vsel = gather_sel(idx)
    kpos = idx[..., None] * SLC_BLOCK + jnp.arange(SLC_BLOCK)
    smask = ((kpos <= qpos[None, None, :, None, None]) & ok[..., None])[:, :, :, None]
    s = jnp.einsum('btghd,bgtnkd->bgthnk', qg, ksel.astype(f32))
    p_slc = masked_softmax(s, smask, (-2, -1))
    o_slc = jnp.einsum('bgthnk,bgtnkd->btghd', p_slc, vsel.astype(f32))
    dpos = qpos[:, None] - wpos[None, :]
    wmask = ((wpos[None, :] >= 0) & (dpos >= 0) & (dpos < WINDOW))[None, :, None, None, :]
    p_win = masked_softmax(jnp.einsum('btghd,bwgd->btghw', qg, wk.astype(f32)), wmask, (-1,))
    o_win = jnp.einsum('btghw,bwgd->btghd', p_win, wv.astype(f32))
    g = gates.reshape(B, T, N_KV, N_HPG, 3)
    o = g[..., 0:1] * o_cmp + g[..., 1:2] * o_slc + g[..., 2:3] * o_win
    return o.reshape(B, T, N_WIDTH)

def nsa_prompt(q, kv, gates, w_cmp, b_cmp):
    B, S = q.shape[:2]
    ck = cmp_blocks(cmp_segments(kv[:, :, 0], w_cmp[0]), b_cmp[0])
    cv = cmp_blocks(cmp_segments(kv[:, :, 1], w_cmp[1]), b_cmp[1])
    blocks = to_blocks(kv[:, :, 2:4])
    b_ix = jnp.arange(B)[:, None, None, None]
    g_ix = jnp.arange(N_KV)[None, :, None, None]

    def gather_sel(idx):
        return blocks[b_ix, idx, :, 0, g_ix], blocks[b_ix, idx, :, 1, g_ix]

    pad = ((0, 0), (WINDOW, 0), (0, 0), (0, 0))
    wk = jnp.pad(kv[:, :, 4], pad)
    wv = jnp.pad(kv[:, :, 5], pad)
    qb = math.gcd(S, NSA_Q_BLOCK)

    def one(i):
        start = i * qb
        return nsa_attend(lax.dynamic_slice_in_dim(q, start, qb, 1), start + jnp.arange(qb), ck, cv,
                          blocks.shape[1], gather_sel,
                          lax.dynamic_slice_in_dim(wk, start, WINDOW + qb, 1),
                          lax.dynamic_slice_in_dim(wv, start, WINDOW + qb, 1),
                          start - WINDOW + jnp.arange(WINDOW + qb),
                          lax.dynamic_slice_in_dim(gates, start, qb, 1))

    o = lax.map(one, jnp.arange(S // qb))
    return o.swapaxes(0, 1).reshape(B, S, N_WIDTH)

def nsa_sample(q, kv, gates, cache_kv, layer, page_table, win_buf, w_cmp, b_cmp):
    B, T = q.shape[:2]
    past_len = page_table.shape[1] * PAGE_SIZE
    b_ix = jnp.arange(B)[:, None, None, None]
    g_ix = jnp.arange(N_KV)[None, :, None, None]

    def cmp_branch(c):
        past = cache_kv[page_table, :, layer, c].reshape(B, past_len, N_KV, N_HD)
        segs = jnp.concatenate([cmp_segments(past, w_cmp[c]), cmp_segments(kv[:, :, c], w_cmp[c])], axis=2)
        return cmp_blocks(segs, b_cmp[c])

    ck, cv = cmp_branch(0), cmp_branch(1)
    new_blocks = to_blocks(kv[:, :, 2:4])
    nnb = new_blocks.shape[1]
    npb = past_len // SLC_BLOCK
    bpp = PAGE_SIZE // SLC_BLOCK

    def gather_sel(idx):
        in_past = (idx < npb)[..., None, None]
        jc = jnp.minimum(idx, npb - 1)
        page = page_table[b_ix, jc // bpp]
        row = ((jc % bpp) * SLC_BLOCK)[..., None] + jnp.arange(SLC_BLOCK)
        loc = jnp.clip(idx - npb, 0, nnb - 1)

        def pick(c):
            past = cache_kv[page[..., None], row, layer, 2 + c, g_ix[..., None]]
            new = new_blocks[b_ix, loc, :, c, g_ix]
            return jnp.where(in_past, past, new.astype(past.dtype))

        return pick(0), pick(1)

    wb = win_buf.shape[1]
    win_all = jnp.concatenate([win_buf.astype(kv.dtype), kv[:, :, 4:]], axis=1)
    qpos = past_len + jnp.arange(T)
    wpos = past_len - wb + jnp.arange(wb + T)
    o = nsa_attend(q, qpos, ck, cv, npb + nnb, gather_sel, win_all[:, :, 0], win_all[:, :, 1], wpos, gates)
    return o, win_all[:, T:]

def merge(z, h_m, h_n, w_bm, w_bn, w_out):
    g = jax.nn.sigmoid(z[..., OFF_BG:N_IN].astype(jnp.float32))
    return (g[..., :D_MODEL] * (h_m @ w_bm) + g[..., D_MODEL:] * (h_n @ w_bn)) @ w_out

def expert_ffn(xe, wgu, bgu, wd, bd):
    gu = xe @ wgu + bgu
    gate = jnp.minimum(gu[..., :D_EXPERT], SWIGLU_LIMIT)
    up = jnp.clip(gu[..., D_EXPERT:], -SWIGLU_LIMIT, SWIGLU_LIMIT)
    glu = gate * jax.nn.sigmoid(gate * SWIGLU_ALPHA)
    return ((up + 1.0) * glu) @ wd + bd

def moe(x, w_router, b_router, w_gu, b_gu, w_dn, b_dn):
    B, T, D = x.shape
    N = B * T
    xf = x.reshape(N, D)
    logits = (xf @ w_router + b_router).astype(jnp.float32)
    top_v, top_e = lax.top_k(logits, TOP_K)
    top_w = jax.nn.softmax(top_v, axis=-1)
    nk = N * TOP_K
    flat_e = top_e.reshape(-1)
    order = jnp.argsort(flat_e)
    sorted_e = flat_e[order]
    counts = jnp.bincount(flat_e, length=N_EXPERTS)
    padded = (counts + MOE_BLOCK - 1) // MOE_BLOCK * MOE_BLOCK
    pad_end = jnp.cumsum(padded)
    pad_start = pad_end - padded
    grp_start = jnp.cumsum(counts) - counts
    dest = pad_start[sorted_e] + jnp.arange(nk) - grp_start[sorted_e]
    n_blocks = -(-(nk + N_EXPERTS * (MOE_BLOCK - 1)) // MOE_BLOCK)
    slots = n_blocks * MOE_BLOCK
    slot_tok = jnp.full((slots,), N, jnp.int32).at[dest].set((order // TOP_K).astype(jnp.int32))
    slot_w = jnp.zeros((slots,), jnp.float32).at[dest].set(top_w.reshape(-1)[order])
    blk_e = jnp.minimum(jnp.searchsorted(pad_end, jnp.arange(n_blocks) * MOE_BLOCK, side='right'), N_EXPERTS - 1)
    x_pad = jnp.concatenate([xf, jnp.zeros((1, D), xf.dtype)], axis=0)

    def run(args):
        tok, e = args
        return expert_ffn(x_pad[tok], w_gu[e], b_gu[e], w_dn[e], b_dn[e])

    y_slots = lax.map(run, (slot_tok.reshape(n_blocks, MOE_BLOCK), blk_e))
    y_slots = y_slots.reshape(slots, D) * slot_w[:, None].astype(y_slots.dtype)
    y = jax.ops.segment_sum(y_slots, slot_tok, num_segments=N + 1)[:N]
    return y.reshape(B, T, D)

def layer_prompt(x, lw):
    (n1, w_in, b_in, w_conv, b_conv, w_mq, w_mk, g_mnorm, w_cmp, b_cmp,
     w_bm, w_bn, w_out, n2, w_r, b_r, w_gu, b_gu, w_dn, b_dn) = lw
    B, S, _ = x.shape
    f32 = jnp.float32
    z, q, kv, gates = project_in(rmsnorm(x, n1), w_in, b_in)
    h_m, conv_new, C, n, m = mlstm_branch(
        z, jnp.zeros((B, M_CONV - 1, M_WIDTH), z.dtype), jnp.zeros((B, M_HEADS, M_DQK, M_DV), f32),
        jnp.zeros((B, M_HEADS, M_DQK), f32), jnp.zeros((B, M_HEADS), f32), w_conv, b_conv, w_mq, w_mk, g_mnorm)
    h_n = nsa_prompt(q, kv, gates, w_cmp, b_cmp)
    x = x + merge(z, h_m, h_n, w_bm, w_bn, w_out)
    x = x + moe(rmsnorm(x, n2), w_r, b_r, w_gu, b_gu, w_dn, b_dn)
    return x, (kv[:, :, :4], kv[:, -min(WINDOW, S):, 4:], conv_new, C, n, m)

def layer_sample(x, cache_kv, layer, page_table, win_buf, conv_buf, C0, n0, m0, lw):
    (n1, w_in, b_in, w_conv, b_conv, w_mq, w_mk, g_mnorm, w_cmp, b_cmp,
     w_bm, w_bn, w_out, n2, w_r, b_r, w_gu, b_gu, w_dn, b_dn) = lw
    z, q, kv, gates = project_in(rmsnorm(x, n1), w_in, b_in)
    h_m, conv_new, C, n, m = mlstm_branch(z, conv_buf, C0, n0, m0, w_conv, b_conv, w_mq, w_mk, g_mnorm)
    h_n, win_new = nsa_sample(q, kv, gates, cache_kv, layer, page_table, win_buf, w_cmp, b_cmp)
    x = x + merge(z, h_m, h_n, w_bm, w_bn, w_out)
    x = x + moe(rmsnorm(x, n2), w_r, b_r, w_gu, b_gu, w_dn, b_dn)
    return x, (kv[:, :, :4], win_new, conv_new, C, n, m)

def setup_inputs(seed: int = 0) -> dict:
    key = jax.random.key(seed)
    keys = iter(jax.random.split(key, 48))
    f32 = jnp.float32

    def nrm(shape, scale):
        return jax.random.normal(next(keys), shape, f32) * scale

    def gain(shape):
        return 1.0 + nrm(shape, 0.02)

    n_pages = PAST_LEN // PAGE_SIZE
    n_pool = (5 * DEC_BATCH * n_pages + 3) // 4
    wb = min(WINDOW, PAST_LEN)
    x_prompt = nrm((BATCH, SEQ, D_MODEL), 1.0)
    x_sample = nrm((DEC_BATCH, DEC_SEQ, D_MODEL), 1.0)
    cache_kv = nrm((n_pool, PAGE_SIZE, DEPTH, 4, N_KV, N_HD), 1.0)
    cache_win_kv = nrm((DEPTH, DEC_BATCH, wb, 2, N_KV, N_HD), 1.0)
    state_conv = nrm((DEPTH, DEC_BATCH, M_CONV - 1, M_WIDTH), 1.0)
    state_C = nrm((DEPTH, DEC_BATCH, M_HEADS, M_DQK, M_DV), 0.1)
    state_n = nrm((DEPTH, DEC_BATCH, M_HEADS, M_DQK), 0.1)
    state_m = nrm((DEPTH, DEC_BATCH, M_HEADS), 1.0)
    perm = jax.random.permutation(next(keys), n_pool)
    page_table = perm[:DEC_BATCH * n_pages].reshape(DEC_BATCH, n_pages).astype(jnp.int32)
    b_in = nrm((DEPTH, N_IN), 0.02)
    b_in = b_in.at[:, OFF_MF:OFF_NQ].add(jax.random.uniform(next(keys), (DEPTH, M_HEADS), f32, 3.0, 6.0))
    return {
        'x_prompt': x_prompt,
        'x_sample': x_sample,
        'cache_kv': cache_kv,
        'cache_win_kv': cache_win_kv,
        'state_conv': state_conv,
        'state_C': state_C,
        'state_n': state_n,
        'state_m': state_m,
        'page_table': page_table,
        'norm1_g': gain((DEPTH, D_MODEL)),
        'w_in': nrm((DEPTH, D_MODEL, N_IN), D_MODEL ** -0.5),
        'b_in': b_in,
        'w_conv': nrm((DEPTH, M_CONV, M_WIDTH), M_CONV ** -0.5),
        'b_conv': nrm((DEPTH, M_WIDTH), 0.02),
        'w_mq': nrm((DEPTH, M_HEADS, M_DV, M_DQK), M_DV ** -0.5),
        'w_mk': nrm((DEPTH, M_HEADS, M_DV, M_DQK), M_DV ** -0.5),
        'g_mnorm': gain((DEPTH, M_HEADS, M_DV)),
        'w_cmp': nrm((DEPTH, 2, CMP_LEN, N_HD, N_HD), (CMP_LEN * N_HD) ** -0.5),
        'b_cmp': nrm((DEPTH, 2, N_HD), 0.02),
        'w_branch_m': nrm((DEPTH, M_WIDTH, D_MODEL), M_WIDTH ** -0.5),
        'w_branch_n': nrm((DEPTH, N_WIDTH, D_MODEL), N_WIDTH ** -0.5),
        'w_out': nrm((DEPTH, D_MODEL, D_MODEL), D_MODEL ** -0.5),
        'norm2_g': gain((DEPTH, D_MODEL)),
        'w_router': nrm((DEPTH, D_MODEL, N_EXPERTS), D_MODEL ** -0.5),
        'b_router': nrm((DEPTH, N_EXPERTS), 0.01),
        'w_gu': nrm((DEPTH, N_EXPERTS, D_MODEL, 2 * D_EXPERT), D_MODEL ** -0.5),
        'b_gu': nrm((DEPTH, N_EXPERTS, 2 * D_EXPERT), 0.02),
        'w_dn': nrm((DEPTH, N_EXPERTS, D_EXPERT, D_MODEL), D_EXPERT ** -0.5),
        'b_dn': nrm((DEPTH, N_EXPERTS, D_MODEL), 0.02),
        'normf_g': gain((D_MODEL,)),
    }

def reference(x_prompt, x_sample, cache_kv, cache_win_kv, state_conv, state_C, state_n, state_m, page_table,
              norm1_g, w_in, b_in, w_conv, b_conv, w_mq, w_mk, g_mnorm, w_cmp, b_cmp,
              w_branch_m, w_branch_n, w_out, norm2_g, w_router, b_router, w_gu, b_gu, w_dn, b_dn, normf_g):
    xp, xs = x_prompt, x_sample
    st_p, st_s = [], []
    for l in range(DEPTH):
        lw = (norm1_g[l], w_in[l], b_in[l], w_conv[l], b_conv[l], w_mq[l], w_mk[l], g_mnorm[l], w_cmp[l], b_cmp[l],
              w_branch_m[l], w_branch_n[l], w_out[l], norm2_g[l], w_router[l], b_router[l], w_gu[l], b_gu[l],
              w_dn[l], b_dn[l])
        xp, sp = layer_prompt(xp, lw)
        xs, ss = layer_sample(xs, cache_kv, l, page_table, cache_win_kv[l], state_conv[l], state_C[l],
                              state_n[l], state_m[l], lw)
        st_p.append(sp)
        st_s.append(ss)
    y_prompt = rmsnorm(xp, normf_g)
    y_sample = rmsnorm(xs, normf_g)
    new_kv_p = jnp.stack([s[0] for s in st_p], axis=2)
    new_win_p = jnp.stack([s[1] for s in st_p])
    new_conv_p = jnp.stack([s[2] for s in st_p])
    new_C_p = jnp.stack([s[3] for s in st_p])
    new_n_p = jnp.stack([s[4] for s in st_p])
    new_m_p = jnp.stack([s[5] for s in st_p])
    new_kv_s = jnp.stack([s[0] for s in st_s], axis=2)
    new_win_s = jnp.stack([s[1] for s in st_s])
    new_conv_s = jnp.stack([s[2] for s in st_s])
    new_C_s = jnp.stack([s[3] for s in st_s])
    new_n_s = jnp.stack([s[4] for s in st_s])
    new_m_s = jnp.stack([s[5] for s in st_s])
    return (y_prompt, y_sample, new_kv_p, new_win_p, new_conv_p, new_C_p, new_n_p, new_m_p,
            new_kv_s, new_win_s, new_conv_s, new_C_s, new_n_s, new_m_s)


_drawn_inputs = setup_inputs


def setup_inputs(seed=0):
    import zlib

    import numpy as np

    out = dict(_drawn_inputs(seed))
    spreads = {}
    factors = {'b_gu': 5.33, 'b_dn': 6.082, 'normf_g': 2.767}
    for name, (base, spread) in spreads.items():
        noise = np.random.default_rng([zlib.crc32(name.encode()), seed]).standard_normal(out[name].shape)
        drawn = base * np.exp(spread * noise) if base else spread * noise
        out[name] = jnp.asarray(drawn.astype(out[name].dtype))
    for name, factor in factors.items():
        out[name] = (out[name] * factor).astype(out[name].dtype)
    return out
```

```python
import concourse.bass as bass
from concourse import mybir
from contextlib import ExitStack

FP = mybir.dt.float32
I32 = mybir.dt.int32
U32 = mybir.dt.uint32
ALU = mybir.AluOpType
ACT = mybir.ActivationFunctionType
AX = mybir.AxisListType

D = 1024
SEQ = 256
NB = 8
TS = 8
NTOK = SEQ + NB * TS
KD = D // 128
TILE_ROWS = [128, 128, 64]
NT = len(TILE_ROWS)
EPS = 1e-6
TINY = 1e-30
NEG = -1e30
NEG_CLAMP = -1e29

MH = 4
DV = 256
DQK = 128
VX = DV + 1
HD = 64
KVC = 768
PAST = 1024
PAGE = 128
NPG = PAST // PAGE
WIN = 512
CMP = 32
CST = 16
NC_P = SEQ // CST - 1
NC_S = PAST // CST - 1
NE = 32
FE = 1024
SLOT = 64
N_OVER = 20
NITEM = NE + N_OVER

OFF_MX, OFF_MV, OFF_MO, OFF_MI, OFF_MF, OFF_NQ = 0, 1024, 2048, 3072, 3076, 3080
OFF_NKV, OFF_NG, OFF_BG = 4104, 4872, 4920


class Link:

    def __init__(self, eng, sem):
        self.eng, self.sem, self.base, self.n = eng, sem, 0, 0

    def go(self, ins):
        ins.then_inc(self.sem, 1)
        self.n += 1

    def wait(self):
        self.eng.wait_ge(self.sem, self.base + self.n)

    def __call__(self, ins):
        self.go(ins)
        self.wait()

    def loop(self, i, per):
        if isinstance(i, int) and i > 0:
            assert self.n == per, (self.n, per)
            self.base, self.n = i * per + self.before, 0
        else:
            self.before, self.per, self.base, self.n = self.n, per, i * per + self.n, 0

    def done(self, turns):
        assert self.n == self.per, (self.n, self.per)
        self.base, self.n = 0, self.before + turns * self.per


class Mem:
    pass


def make_consts(nc, m):
    s0, s1, s2 = m.sem("const_fill"), m.sem("const_sel"), m.sem("const_sel2")
    s_pe, s_ev = m.sem("const_pe"), m.sem("const_ev")
    with nc.Block() as block:
        @block.gpsimd
        def _(pool):
            fills = [(m.ident, 0.0), (m.ones, 1.0), (m.tri, 1.0), (m.causal_st, 0.0), (m.causal_tk, 0.0),
                     (m.same_seq, 0.0), (m.seg_mul, 1.0), (m.seg_add, 0.0), (m.seq_onehot, 1.0),
                     (m.cmp_mask, 0.0), (m.period, 1.0), (m.new8, 0.0), (m.win8, 0.0)]
            for t, v in fills:
                pool.memset(t[:], v).then_inc(s0, 1)
            pool.iota(m.blk_idx[:], [[1, 16]], base=0, channel_multiplier=0,
                      allow_small_or_imprecise_dtypes=True).then_inc(s0, 1)
            pool.iota(m.slot_idx[:], [[1, SLOT]], base=0, channel_multiplier=0,
                      allow_small_or_imprecise_dtypes=True).then_inc(s0, 1)
            pool.iota(m.exp_idx[:], [[1, NE]], base=0, channel_multiplier=0,
                      allow_small_or_imprecise_dtypes=True).then_inc(s0, 1)
            pool.iota(m.over_idx[:], [[1, N_OVER], [0, NE]], base=0, channel_multiplier=0,
                      allow_small_or_imprecise_dtypes=True).then_inc(s0, 1)
            pool.wait_ge(s0, len(fills) + 4)

            def sel(t, pattern, base, cm, op, fill, sem=s1):
                pool.affine_select(out=t, in_=t, pattern=pattern, compare_op=op, fill=fill,
                                   base=base, channel_multiplier=cm).then_inc(sem, 1)

            sel(m.ident[:], [[-1, 128]], 0, 1, ALU.not_equal, 1.0)
            sel(m.tri[:], [[1, 128]], 0, -1, ALU.is_gt, 0.0)
            sel(m.causal_st[:], [[1, 128]], 0, -1, ALU.is_ge, NEG)
            sel(m.causal_tk[:], [[-1, 128]], 0, 1, ALU.is_ge, NEG)
            sel(m.same_seq[:], [[1, 64]], 0, -1, ALU.is_ge, NEG)
            sel(m.seg_mul[:, SEQ:], [[0, NB], [1, TS]], 0, 0, ALU.is_gt, 0.0)
            sel(m.seg_add[:, SEQ:], [[0, NB], [1, TS]], 0, 0, ALU.is_gt, NEG)
            sel(m.seq_onehot[:], [[-TS, NB]], 0, 1, ALU.is_ge, 0.0)
            for t in range(2):
                sel(m.cmp_mask[:, t, :], [[-CST, NC_P]], 128 * t - (CMP - 1), 1, ALU.is_ge, NEG)
            sel(m.period[:], [[0, 16], [-1, TS]], 0, 1, ALU.is_equal, 0.0)
            sel(m.new8[:], [[0, NB], [0, NB], [-1, TS]], 0, 1, ALU.is_ge, NEG)
            sel(m.win8[:], [[1, WIN]], 0, -1, ALU.is_gt, NEG)
            pool.wait_ge(s1, 13)
            sel(m.same_seq[:], [[-TS, NB], [0, TS]], 0, 1, ALU.is_ge, NEG, s2)
            sel(m.seq_onehot[:], [[TS, NB]], TS - 1, -1, ALU.is_ge, 0.0, s2)
            sel(m.new8[:], [[1, NB], [-1, NB], [0, TS]], 0, 0, ALU.is_equal, NEG, s2)

        @block.tensor
        def _(pe):
            pe.wait_ge(s2, 3)
            pe.matmul(m.bank[0][:, :], m.period[:], m.new8[:], start=True, stop=True).then_inc(s_pe, 1)
            pe.matmul(m.bank[1][:, :], m.period[:], m.win8[:], start=True, stop=True).then_inc(s_pe, 1)
            pe.matmul(m.bank[2][:, 0:128], m.period[:], m.period[:], start=True, stop=True).then_inc(s_pe, 1)

        @block.vector
        def _(dve):
            dve.wait_ge(s_pe, 3)
            dve.tensor_copy(m.new_mask[:], m.bank[0][:, :])
            dve.tensor_copy(m.win_mask[:], m.bank[1][:, :])
            dve.tensor_copy(m.peer[:], m.bank[2][:, 0:128]).then_inc(s_ev, 1)
            dve.wait_ge(s_ev, 1)
            dve.memset(m.peer[0:64, 64:128], 0.0)
            dve.memset(m.peer[64:128, 0:64], 0.0)


def norm_in(nc, m, a):
    s_x, s_p, s_v = m.sem("x_in"), m.sem("params_in"), m.sem("vec_in")
    s_tp, s_ev, s_chain = m.sem("tp_done"), m.sem("tp_evicted"), m.sem("norm1_dve")
    s_ms, s_sq, s_r = m.sem("norm1_ms"), m.sem("norm1_sqrt"), m.sem("norm1_rstd")
    s_xn = m.sem("norm1_scaled")
    xp = a.x_prompt.rearrange("b (t p) d -> p (b t) d", p=128)
    xs = a.x_sample.rearrange("b t d -> (b t) d")
    with ExitStack() as c:
        xn = c.enter_context(nc.sbuf_tensor("xn1", [128, NT, D], FP))
        junk = c.enter_context(nc.sbuf_tensor("junk1", [128, D], FP))
        ss = c.enter_context(nc.sbuf_tensor("ss1", [128, NT], FP))
        prow = c.enter_context(nc.sbuf_tensor("prow", [12, D], FP))
        pcol = c.enter_context(nc.sbuf_tensor("pcol", [128, KD, 12], FP))
        block = c.enter_context(nc.Block())

        @block.sync
        def _(sp):
            sp.dma_start(m.x[:, 0:2, :], xp).then_inc(s_x, 16)
            sp.dma_start(m.x[0:64, 2, :], xs).then_inc(s_x, 16)

        @block.scalar
        def _(act):
            b_in = a.b_in
            act.dma_start(prow[0:4, :], a.w_conv[0]).then_inc(s_p, 16)
            act.dma_start(prow[4:5, :], a.b_conv).then_inc(s_p, 16)
            act.dma_start(prow[5:6, :], a.g_mnorm.rearrange("l h v -> l (h v)")).then_inc(s_p, 16)
            act.dma_start(prow[6:7, :], a.norm1_g).then_inc(s_p, 16)
            act.dma_start(prow[7:8, :], b_in[:, OFF_MX:OFF_MX + D]).then_inc(s_p, 16)
            act.dma_start(prow[8:9, :], b_in[:, OFF_MO:OFF_MO + D]).then_inc(s_p, 16)
            act.dma_start(prow[9:10, :], b_in[:, OFF_BG:OFF_BG + D]).then_inc(s_p, 16)
            act.dma_start(prow[10:11, :], b_in[:, OFF_BG + D:OFF_BG + 2 * D]).then_inc(s_p, 16)
            for g in range(2):
                act.dma_start(prow[11:12, :].rearrange("p (j g d) -> p g j d", g=2, d=HD)[:, g],
                              b_in[:, OFF_NQ + g * 512:OFF_NQ + (g + 1) * 512].rearrange("l (j d) -> l j d", d=HD)).then_inc(s_p, 16)
            act.dma_start(m.bias_tok[:, 0:D], b_in[:, OFF_MV:OFF_MV + D].to_broadcast((128, D))).then_inc(s_v, 16)
            act.dma_start(m.bias_tok[:, D:], b_in[:, OFF_NKV:OFF_BG].to_broadcast((128, OFF_BG - OFF_NKV))).then_inc(s_v, 16)
            act.dma_start(m.gate_bias[:, 0:1], b_in[:, OFF_MI:OFF_MF].rearrange("l h -> h l")).then_inc(s_v, 16)
            act.dma_start(m.gate_bias[:, 1:2], b_in[:, OFF_MF:OFF_NQ].rearrange("l h -> h l")).then_inc(s_v, 16)
            act.wait_ge(s_ms, 1)
            act.activation(ss[:, :], ss[:, :], ACT.Sqrt).then_inc(s_sq, 1)
            act.wait_ge(s_v, 64)

        @block.vector
        def _(dve):
            link = Link(dve, s_chain)
            link(dve.memset(ss[:, :], 1.0))
            dve.wait_ge(s_x, 32)
            for t, n in enumerate(TILE_ROWS):
                link(dve.tensor_tensor_reduce(out=junk[0:n, :], in0=m.x[0:n, t, :], in1=m.x[0:n, t, :], scale=1.0,
                                              scalar=0.0, op0=ALU.mult, op1=ALU.add, accum_out=ss[0:n, t:t + 1]))
            dve.tensor_scalar(ss[:, :], ss[:, :], 1.0 / D, EPS, ALU.mult, ALU.add).then_inc(s_ms, 1)
            dve.wait_ge(s_sq, 1)
            link(dve.reciprocal(ss[:, :], ss[:, :]))
            for t, n in enumerate(TILE_ROWS):
                dve.tensor_scalar(xn[0:n, t, :], m.x[0:n, t, :], ss[0:n, t:t + 1], None, ALU.mult).then_inc(s_xn, 1)
            dve.wait_ge(s_tp, 1)
            link(dve.tensor_copy(pcol[:, :, :], m.bank[0][:, 0:KD * 12].rearrange("p (k r) -> p k r", r=12)))
            dve.tensor_copy(m.par[:, :, :], pcol[:, :, 0:7].rearrange("p k r -> p r k"))
            dve.tensor_copy(m.bias_feat[:, :].rearrange("p (r k) -> p r k", k=KD), pcol[:, :, 7:12].rearrange("p k r -> p r k"))
            for k in range(KD):
                dve.wait_ge(s_tp, 2 + k)
                dve.tensor_scalar(m.uT[:, k, :], m.bank[1 + k % 2][:, 0:NTOK], pcol[:, k, 6:7], None,
                                  ALU.mult).then_inc(s_ev, 1)

        @block.tensor
        def _(pe):
            pe.wait_ge(s_p, 160)
            for k in range(KD):
                last = pe.transpose(m.bank[0][:, k * 12:(k + 1) * 12], prow[:, k * 128:(k + 1) * 128], m.ident[0:12, 0:12])
            last.then_inc(s_tp, 1)
            pe.wait_ge(s_xn, NT)
            for k in range(KD):
                if k >= 2:
                    pe.wait_ge(s_ev, k - 1)
                for t, n in enumerate(TILE_ROWS):
                    last = pe.transpose(m.bank[1 + k % 2][:, t * 128:t * 128 + n], xn[0:n, t, k * 128:(k + 1) * 128],
                                        m.ident[0:n, 0:n])
                last.then_inc(s_tp, 1)


def project(nc, m, a):
    NCH = 8
    NSL = 4
    s_w = [m.sem(f"win_slot{i}") for i in range(NSL)]
    s_wg, s_pe = m.sem("wgate_in"), m.sem("proj_done")
    s_ev, s_pt, s_et = m.sem("proj_evicted"), m.sem("ptok_done"), m.sem("ptok_evicted")
    s_pg, s_sg, s_pq, s_eq = m.sem("pgate_done"), m.sem("sigmoid_gates"), m.sem("pq_done"), m.sem("pq_evicted")
    w_v = a.w_in[0].rearrange("(k p) n -> p k n", p=128)
    feat_off = [OFF_MX, OFF_MX + 512, OFF_MO, OFF_MO + 512] + [OFF_BG + 512 * i for i in range(4)]
    tok_cols = [(OFF_MV, 512, 0), (OFF_MV + 512, 512, 512), (OFF_NKV, 512, 1024), (OFF_NKV + 512, 304, 1536)]
    with ExitStack() as c:
        w = c.enter_context(nc.sbuf_tensor("w_slots", [128, NSL, KD, 512], FP))
        wg = c.enter_context(nc.sbuf_tensor("w_gates", [128, KD, 8], FP))
        block = c.enter_context(nc.Block())

        @block.sync
        def _(sp):
            sp.dma_start(wg[:, :, :], w_v[:, :, OFF_MI:OFF_NQ]).then_inc(s_wg, 16)
            loads = [(o, 512) for o in feat_off] + [(OFF_NQ, 512), (OFF_NQ + 512, 512)] + [(o, n) for o, n, _ in tok_cols]
            for i, (o, n) in enumerate(loads):
                before = i - NSL
                if before >= NCH:
                    sp.wait_ge(s_pq, KD)
                elif before >= 0:
                    sp.wait_ge(s_pe, 4 * (before + 1))
                sp.dma_start(w[:, i % NSL, :, 0:n], w_v[:, :, o:o + n]).then_inc(s_w[i % NSL], 16)

        @block.tensor
        def _(pe):
            pe.wait_ge(s_wg, 16)
            for r in range(2):
                for k in range(KD):
                    last = pe.matmul(m.bank[4 + r][0:MH, 0:NTOK], wg[:, k, MH * r:MH * (r + 1)], m.uT[:, k, :],
                                     start=(k == 0), stop=(k == KD - 1))
            last.then_inc(s_pg, 1)
            with pe.Fori(0, NCH // NSL) as i:
                for s in range(NSL):
                    pe.wait_ge(s_w[s], 16 * i + 16)
                    for j in range(4):
                        pe.wait_ge(s_ev, NSL * 4 * i + 4 * s + j + 1)
                        for k in range(KD):
                            last = pe.matmul(m.bank[j][:, 0:NTOK], w[:, s, k, j * 128:(j + 1) * 128], m.uT[:, k, :],
                                             start=(k == 0), stop=(k == KD - 1))
                        last.then_inc(s_pe, 1)
            for s in range(2):
                pe.wait_ge(s_w[s], 16 * 3)
            for j in range(KD):
                pe.wait_ge(s_ev, 4 + 32 - 3 + j) if j < 4 else pe.wait_ge(s_eq, j - 3)
                for g in range(2):
                    for k in range(KD):
                        last = pe.matmul(m.bank[j % 4][g * HD:(g + 1) * HD, 0:NTOK], w[:, g, k, j * HD:(j + 1) * HD],
                                         m.uT[:, k, :], start=(k == 0), stop=(k == KD - 1))
                last.then_inc(s_pq, 1)
            n = 0
            for i, (_, width, _) in enumerate(tok_cols):
                s = (10 + i) % NSL
                pe.wait_ge(s_w[s], 16 * (3 if i < 2 else 4))
                for t, rows in enumerate(TILE_ROWS):
                    pe.wait_ge(s_eq, n + 5) if n < 4 else pe.wait_ge(s_et, n - 3)
                    for k in range(KD):
                        last = pe.matmul(m.bank[n % 4][0:rows, 0:width], m.uT[:, k, t * 128:t * 128 + rows],
                                         w[:, s, k, 0:width], start=(k == 0), stop=(k == KD - 1))
                    last.then_inc(s_pt, 1)
                    n += 1

        @block.scalar
        def _(act):
            act.sem_inc(s_ev, 4)
            act.wait_ge(s_pg, 1)
            for r in range(2):
                act.activation(m.gate_rows[:, r, :], m.bank[4 + r][0:MH, 0:NTOK], ACT.Identity, bias=m.gate_bias[:, r:r + 1])
            with act.Fori(0, NCH) as i:
                for j in range(4):
                    act.wait_ge(s_pe, 4 * i + j + 1)
                    act.activation(m.zf[:, bass.ds(4 * i + j, 1), :], m.bank[j][:, 0:NTOK], ACT.Identity,
                                   bias=m.bias_feat[:, bass.ds(4 * i + j, 1)]).then_inc(s_ev, 1)
            for j in range(KD):
                act.wait_ge(s_pq, j + 1)
                act.activation(m.zf[:, 32 + j, :], m.bank[j % 4][:, 0:NTOK], ACT.Identity,
                               bias=m.bias_feat[:, 32 + j:33 + j]).then_inc(s_eq, 1)
            act.wait_ge(s_ev, 36)
            act.activation(m.zf[:, 8:32, :], m.zf[:, 8:32, :], ACT.Sigmoid)
            act.wait_ge(s_eq, 8)
            act.activation(m.zf[:, 32:40, :], m.zf[:, 32:40, :], ACT.Copy, scale=HD ** -0.5)
            act.wait_ge(s_et, 12)
            act.activation(m.ngate[:, 0:2, :], m.ngate[:, 0:2, :], ACT.Sigmoid)
            act.activation(m.ngate[0:64, 2, :], m.ngate[0:64, 2, :], ACT.Sigmoid)

        @block.vector
        def _(dve):
            dve.memset(m.v[:, :, :, DV:VX], 1.0)
            n = 0
            for i, (_, width, off) in enumerate(tok_cols):
                for t, rows in enumerate(TILE_ROWS):
                    dve.wait_ge(s_pt, n + 1)
                    ps = m.bank[n % 4]
                    bias = m.bias_tok[0:rows, off:off + width]
                    if i < 2:
                        dve.tensor_tensor(m.v[0:rows, t, 2 * i:2 * i + 2, 0:DV],
                                          ps[0:rows, 0:512].rearrange("p (h v) -> p h v", v=DV),
                                          bias.rearrange("p (h v) -> p h v", v=DV), ALU.add).then_inc(s_et, 1)
                    elif i == 2:
                        dve.tensor_tensor(m.kv[0:rows, t, 0:512], ps[0:rows, 0:512], bias, ALU.add).then_inc(s_et, 1)
                    else:
                        dve.tensor_tensor(m.kv[0:rows, t, 512:KVC], ps[0:rows, 0:256], bias[:, 0:256], ALU.add)
                        dve.tensor_tensor(m.ngate[0:rows, t, :], ps[0:rows, 256:304], bias[:, 256:304],
                                          ALU.add).then_inc(s_et, 1)
                    n += 1

def conv_silu(nc, m, a):
    s_in, s_tp, s_pad, s_last = m.sem("conv_state_in"), m.sem("conv_state_T"), m.sem("conv_padded"), m.sem("conv_last")
    s_lt, s_le, s_out = m.sem("conv_last_T"), m.sem("conv_last_ev"), m.sem("conv_out")
    s_chain, s_acc, s_sig, s_zero = m.sem("conv_dve"), m.sem("conv_acc"), m.sem("conv_sig"), m.sem("conv_zero")
    R = NB * 3
    with ExitStack() as c:
        state = c.enter_context(nc.sbuf_tensor("conv_state", [R, D], FP))
        xp = c.enter_context(nc.sbuf_tensor("conv_xp", [128, KD, SEQ + 3], FP))
        xs = c.enter_context(nc.sbuf_tensor("conv_xs", [128, KD, NB, TS + 3], FP))
        last3 = c.enter_context(nc.sbuf_tensor("conv_last3", [128, KD, R + 3], FP))
        rows = c.enter_context(nc.sbuf_tensor("conv_rows", [R + 3, D], FP))
        sig = c.enter_context(nc.sbuf_tensor("conv_sigm", [128, KD, NTOK], FP))
        block = c.enter_context(nc.Block())

        @block.sync
        def _(sp):
            sp.dma_start(state[:, :], a.state_conv[0].rearrange("b r d -> (b r) d")).then_inc(s_in, 16)
            sp.wait_ge(s_le, 2)
            sp.dma_start(a.new_conv_p[0, 0], rows[0:3, :]).then_inc(s_out, 16)
            sp.dma_start(a.new_conv_s[0].rearrange("b r d -> (b r) d"), rows[3:R + 3, :]).then_inc(s_out, 16)
            sp.wait_ge(s_out, 32)

        @block.tensor
        def _(pe):
            pe.wait_ge(s_in, 16)
            for k in range(KD):
                last = pe.transpose(m.bank[0][:, k * R:(k + 1) * R], state[:, k * 128:(k + 1) * 128], m.ident[0:R, 0:R])
            last.then_inc(s_tp, 1)
            pe.wait_ge(s_last, 1)
            for k in range(KD):
                last = pe.transpose(m.bank[1 + k // 4][0:R + 3, (k % 4) * 128:(k % 4 + 1) * 128], last3[:, k, :], m.ident[:, :])
                if k % 4 == 3:
                    last.then_inc(s_lt, 1)

        @block.gpsimd
        def _(pool):
            pool.memset(xp[:, :, 0:3], 0.0)
            pool.tensor_copy(xp[:, :, 3:], m.zf[:, 0:KD, 0:SEQ]).then_inc(s_zero, 1)

        @block.vector
        def _(dve):
            link = Link(dve, s_chain)
            link.go(dve.tensor_copy(xs[:, :, :, 3:], m.zf[:, 0:KD, SEQ:].rearrange("p k (b t) -> p k b t", t=TS)))
            dve.wait_ge(s_tp, 1)
            link(dve.tensor_copy(xs[:, :, :, 0:3], m.bank[0][:, 0:KD * R].rearrange("p (k b r) -> p k b r", b=NB, r=3)))
            dve.wait_ge(s_zero, 1)
            link.go(dve.tensor_copy(last3[:, :, 0:3], xp[:, :, SEQ:SEQ + 3]))
            link(dve.tensor_copy(last3[:, :, 3:].rearrange("p k (b r) -> p k b r", r=3), xs[:, :, :, TS:TS + 3]))
            dve.sem_inc(s_last, 1)
            with dve.Fori(0, KD) as k:
                link.loop(k, 8)
                w = [m.par[:, j, bass.ds(k, 1)] for j in range(5)]
                yp = m.xc[:, bass.ds(k, 1), 0:SEQ]
                ys = m.xc[:, bass.ds(k, 1), SEQ:].rearrange("p k (b t) -> p (k b) t", t=TS)
                for j in range(4):
                    inp = xp[:, bass.ds(k, 1), j:j + SEQ]
                    ins = xs[:, bass.ds(k, 1), :, j:j + TS].rearrange("p k b t -> p (k b) t")
                    if j == 0:
                        link.go(dve.tensor_scalar(yp, inp, w[0], w[4], ALU.mult, ALU.add))
                        link(dve.tensor_scalar(ys, ins, w[0], w[4], ALU.mult, ALU.add))
                    else:
                        link.go(dve.scalar_tensor_tensor(yp, inp, w[j], yp, ALU.mult, ALU.add))
                        link(dve.scalar_tensor_tensor(ys, ins, w[j], ys, ALU.mult, ALU.add))
            link.done(KD)
            dve.sem_inc(s_acc, 1)
            for i in range(2):
                dve.wait_ge(s_lt, i + 1)
                dve.tensor_copy(rows[:, i * 512:(i + 1) * 512], m.bank[1 + i][0:R + 3, :]).then_inc(s_le, 1)
            dve.wait_ge(s_sig, 1)
            dve.tensor_tensor(m.xc[:, :, :], m.xc[:, :, :], sig[:, :, :], ALU.mult)

        @block.scalar
        def _(act):
            act.wait_ge(s_acc, 1)
            act.activation(sig[:, :, :], m.xc[:, :, :], ACT.Sigmoid).then_inc(s_sig, 1)


def mlstm_gates(nc, m, a):
    s_w, s_m0, s_qk, s_ev = m.sem("wqk_in"), m.sem("m0_in"), m.sem("qk_done"), m.sem("qk_evicted")
    s_abs, s_e, s_ln, s_lf = m.sem("g_abs"), m.sem("g_exp"), m.sem("g_ln"), m.sem("g_dve")
    s_mt, s_wi, s_we, s_cols = m.sem("g_mt"), m.sem("g_winter"), m.sem("g_wend"), m.sem("g_cols_T")
    s_mo, s_out, s_dec = m.sem("g_mout"), m.sem("g_m_stored"), m.sem("g_decay")
    with ExitStack() as c:
        wq = c.enter_context(nc.sbuf_tensor("wq", [128, 2 * MH, DQK], FP))
        wk = c.enter_context(nc.sbuf_tensor("wk", [128, 2 * MH, DQK], FP))
        lf = c.enter_context(nc.sbuf_tensor("g_lf", [MH, NTOK], FP))
        t0 = c.enter_context(nc.sbuf_tensor("g_t0", [MH, NTOK], FP))
        t1 = c.enter_context(nc.sbuf_tensor("g_t1", [MH, NTOK], FP))
        bsum = c.enter_context(nc.sbuf_tensor("g_b", [MH, NTOK], FP))
        mrow = c.enter_context(nc.sbuf_tensor("g_m", [MH, NTOK], FP))
        m0 = c.enter_context(nc.sbuf_tensor("g_m0", [MH, NTOK], FP))
        m0s = c.enter_context(nc.sbuf_tensor("g_m0s", [MH, NB], FP))
        mt = c.enter_context(nc.sbuf_tensor("g_mtrow", [MH, NTOK], FP))
        wa = c.enter_context(nc.sbuf_tensor("g_wa", [MH, 64], FP))
        we = c.enter_context(nc.sbuf_tensor("g_we", [MH, 64], FP))
        crow = c.enter_context(nc.sbuf_tensor("g_crow", [MH, 3, NTOK], FP))
        mout = c.enter_context(nc.sbuf_tensor("g_mo", [MH, 1 + NB], FP))
        block = c.enter_context(nc.Block())
        r = crow[:, 0, :]

        @block.sync
        def _(sp):
            sp.dma_start(wq[:, :, :], a.w_mq[0].rearrange("h (c p) d -> p (h c) d", p=128)).then_inc(s_w, 16)
            sp.dma_start(wk[:, :, :], a.w_mk[0].rearrange("h (c p) d -> p (h c) d", p=128)).then_inc(s_w, 16)
            sp.dma_start(m0s[:, :], a.state_m[0].rearrange("b h -> h b"), allow_slow_non_contiguous=True).then_inc(s_m0, 16)
            sp.wait_ge(s_mo, 1)
            sp.dma_start(a.new_m_p[0].rearrange("b h -> h b"), mout[:, 0:1], allow_slow_non_contiguous=True).then_inc(s_out, 16)
            sp.dma_start(a.new_m_s[0].rearrange("b h -> h b"), mout[:, 1:], allow_slow_non_contiguous=True).then_inc(s_out, 16)
            sp.wait_ge(s_out, 32)

        @block.tensor
        def _(pe):
            pe.wait_ge(s_w, 32)
            for h in range(MH):
                pe.wait_ge(s_ev, 3 * h + 1)
                for i in range(2):
                    last = pe.matmul(m.bank[0][:, 0:NTOK], wq[:, bass.ds(2 * h + i, 1), :], m.xc[:, bass.ds(2 * h + i, 1), :],
                                     start=(i == 0), stop=(i == 1))
                last.then_inc(s_qk, 1)
                pe.wait_ge(s_ev, 3 * h + 2)
                for i in range(2):
                    last = pe.matmul(m.bank[1][:, 0:NTOK], wk[:, bass.ds(2 * h + i, 1), :], m.xc[:, bass.ds(2 * h + i, 1), :],
                                     start=(i == 0), stop=(i == 1))
                last.then_inc(s_qk, 1)
                pe.wait_ge(s_ev, 3 * h + 3)
                for t, n in enumerate(TILE_ROWS):
                    for i in range(2):
                        last = pe.matmul(m.bank[2][0:n, t * 128:(t + 1) * 128], m.xc[:, bass.ds(2 * h + i, 1), t * 128:t * 128 + n],
                                         wk[:, bass.ds(2 * h + i, 1), :], start=(i == 0), stop=(i == 1))
                last.then_inc(s_qk, 1)
            pe.wait_ge(s_we, 2)
            pe.wait_ge(s_e, 2)
            for t, n in enumerate(TILE_ROWS):
                for q in range(3):
                    last = pe.transpose(m.bank[3][0:n, (t * 3 + q) * MH:(t * 3 + q + 1) * MH],
                                        crow[:, q, t * 128:t * 128 + n], m.ident[0:MH, 0:MH])
            last.then_inc(s_cols, 1)

        @block.scalar
        def _(act):
            act.sem_inc(s_ev, 3)
            act.activation(t0[:, :], m.gate_rows[:, 1, :], ACT.Abs).then_inc(s_abs, 1)
            act.wait_ge(s_abs, 1)
            act.activation(t0[:, :], t0[:, :], ACT.Exp, scale=-1.0).then_inc(s_e, 1)
            act.wait_ge(s_e, 1)
            act.activation(t1[:, :], t0[:, :], ACT.Ln, bias=1.0).then_inc(s_ln, 1)
            act.wait_ge(s_mt, 1)
            act.activation(crow[:, 1, :], mt[:, :], ACT.Exp, scale=-1.0).then_inc(s_e, 1)
            act.activation(m.grow[:, NTOK:NTOK + 64], wa[:, :], ACT.Exp).then_inc(s_wi, 1)
            act.activation(crow[:, 2, 0:SEQ], r[:, 0:SEQ], ACT.Exp, bias=m.grow[:, SEQ - 1:SEQ]).then_inc(s_we, 1)
            act.activation(crow[:, 2, SEQ:], we[:, :], ACT.Exp).then_inc(s_we, 1)
            for h in range(MH):
                act.wait_ge(s_qk, 3 * h + 1)
                act.activation(m.mqT[:, bass.ds(h, 1), :], m.bank[0][:, 0:NTOK], ACT.Copy).then_inc(s_ev, 1)
                act.wait_ge(s_qk, 3 * h + 2)
                act.activation(m.mkT[:, bass.ds(h, 1), :], m.bank[1][:, 0:NTOK], ACT.Copy, scale=DQK ** -0.5).then_inc(s_ev, 1)
                act.wait_ge(s_qk, 3 * h + 3)
                act.activation(m.mk[:, bass.ds(h, 1), 0:2 * DQK], m.bank[2][:, 0:2 * DQK], ACT.Copy, scale=DQK ** -0.5)
                act.activation(m.mk[0:64, bass.ds(h, 1), 2 * DQK:], m.bank[2][0:64, 2 * DQK:3 * DQK], ACT.Copy,
                               scale=DQK ** -0.5).then_inc(s_ev, 1)

        @block.vector
        def _(dve):
            link = Link(dve, s_lf)
            link(dve.memset(m0[:, 0:SEQ], 0.0))
            dve.wait_ge(s_m0, 16)
            link(dve.tensor_copy(m0[:, SEQ:].rearrange("p (b t) -> p b t", t=TS), m0s[:, :].unsqueeze(2).to_broadcast((MH, NB, TS))))
            dve.wait_ge(s_ln, 1)
            link(dve.scalar_tensor_tensor(lf[:, :], m.gate_rows[:, 1, :], 0.0, t1[:, :], ALU.min, ALU.subtract))
            link(dve.tensor_tensor_scan(bsum[:, :], m.seg_mul[:, :], lf[:, :], 0.0, ALU.mult, ALU.add))
            link(dve.tensor_tensor(r, m.gate_rows[:, 0, :], bsum[:, :], ALU.subtract))
            link(dve.tensor_tensor_scan(mrow[:, :], m.seg_add[:, :], r, NEG, ALU.add, ALU.max))
            link(dve.tensor_tensor(mrow[:, :], mrow[:, :], m0[:, :], ALU.max))
            link(dve.tensor_scalar(m.grow[:, 0:NTOK], mrow[:, :], -1.0, None, ALU.mult))
            link(dve.tensor_tensor(mt[:, :], bsum[:, :], mrow[:, :], ALU.add))
            link(dve.tensor_tensor(wa[:, :], m0[:, SEQ:], mrow[:, SEQ:], ALU.subtract))
            negm_end = m.grow[:, SEQ:NTOK].rearrange("p (b t) -> p b t", t=TS)[:, :, TS - 1:TS]
            link(dve.tensor_tensor(we[:, :].rearrange("p (b t) -> p b t", t=TS), r[:, SEQ:].rearrange("p (b t) -> p b t", t=TS),
                                   negm_end.to_broadcast((MH, NB, TS)), ALU.add))
            dve.sem_inc(s_mt, 1)
            link.go(dve.tensor_copy(mout[:, 0:1], mt[:, SEQ - 1:SEQ]))
            link(dve.tensor_copy(mout[:, 1:].unsqueeze(2), mt[:, SEQ:].rearrange("p (b t) -> p b t", t=TS)[:, :, TS - 1:TS]))
            dve.sem_inc(s_mo, 1)
            dve.wait_ge(s_wi, 1)
            dve.tensor_copy(m.grow[:, NTOK + 64:NTOK + 64 + NB].unsqueeze(2),
                            m.grow[:, NTOK:NTOK + 64].rearrange("p (b t) -> p b t", t=TS)[:, :, TS - 1:TS])
            dve.wait_ge(s_cols, 1)
            dve.tensor_copy(m.gcol[:, 0:2, :, :], m.bank[3][:, 0:24].rearrange("p (t q h) -> p t q h", q=3, h=MH))
            dve.tensor_copy(m.gcol[0:64, 2, :, :], m.bank[3][0:64, 24:36].rearrange("p (q h) -> p q h", h=MH))


def mlstm_heads(nc, m, a):
    s_c0, s_n0, s_nT, s_n0e = m.sem("C0_in"), m.sem("n0_in"), m.sem("n0_T"), m.sem("n0_ev")
    s_nb, s_s, s_arg, s_w = m.sem("bcast_done"), m.sem("qk_scores"), m.sem("warg"), m.sem("wexp")
    s_nbf, s_pt, s_kw, s_num = m.sem("bcast_read"), m.sem("pt_ready"), m.sem("kw_ready"), m.sem("num_done")
    s_cp, s_cpe, s_cs, s_cse = m.sem("Cp_done"), m.sem("Cp_evicted"), m.sem("Cs_done"), m.sem("Cs_evicted")
    s_h, s_sq, s_numf, s_chain = m.sem("h_ready"), m.sem("h_sq"), m.sem("num_read"), m.sem("heads_dve")
    s_out, s_qm, s_rt, s_hn = m.sem("C_out"), m.sem("qm_zero"), m.sem("hrms_sqrt"), m.sem("hn_ready")
    s_hT, s_hTe, s_rs, s_nc, s_nct, s_nce = (m.sem("hT"), m.sem("hT_ev"), m.sem("hrms_ms"), m.sem("ncol"),
                                             m.sem("ncol_T"), m.sem("ncol_ev"))
    QW = 136
    with ExitStack() as c:
        def sb(name, shape):
            return c.enter_context(nc.sbuf_tensor(name, shape, FP))

        ce = sb("state_ce", [128, NB, MH, VX])
        cp = sb("prompt_c", [128, MH, VX])
        n0 = sb("n0_rows", [NB * MH, DQK])
        ncol = sb("ncols", [128, MH + NB * MH])
        nrow = sb("nrows", [MH + NB * MH, DQK])
        wi = sb("w_intra", [128, 3 * 128])
        wis = sb("w_intra_s", [64, 64])
        pt = sb("pt", [128, 3 * 128])
        pts = sb("pt_s", [64, 128])
        qm = sb("qm", [128, NB * QW])
        dec = sb("decay", [128, NB])
        kw = sb("kw", [128, 2, DQK])
        wem = sb("wend_m", [64, NB])
        kws = sb("kw_s", [64, NB, DQK])
        den = sb("den", [128, NT])
        ht = sb("h_tok", [128, NT, MH, DV])
        junk = sb("h_junk", [128, DV])
        ss = sb("h_ss", [128, NT, MH])
        block = c.enter_context(nc.Block())

        @block.sync
        def _(sp):
            sp.dma_start(n0[:, :], a.state_n[0].rearrange("b h d -> (b h) d")).then_inc(s_n0, 16)
            for b in range(NB):
                sp.dma_start(ce[:, b, :, 0:DV], a.state_C[0, b].rearrange("h d v -> d h v")).then_inc(s_c0, 16)
            for h in range(MH):
                sp.wait_ge(s_cpe, h + 2)
                sp.dma_start(a.new_C_p[0, 0, h], cp[:, h, 0:DV]).then_inc(s_out, 16)
                sp.wait_ge(s_cse, 2 + NB * (h + 1))
                sp.dma_start(a.new_C_s[0, :, h].rearrange("b d v -> d b v"), ce[:, :, h, 0:DV]).then_inc(s_out, 16)
            sp.wait_ge(s_nce, 1)
            sp.dma_start(a.new_n_p[0, 0], nrow[0:MH, :]).then_inc(s_out, 16)
            sp.dma_start(a.new_n_s[0].rearrange("b h d -> (b h) d"), nrow[MH:, :]).then_inc(s_out, 16)
            sp.wait_ge(s_out, 16 * (2 * MH + 2))

        @block.tensor
        def _(pe):
            pe.wait_ge(s_n0, 16)
            pe.transpose(m.bank[5][:, 0:NB * MH], n0[:, :], m.ident[0:NB * MH, 0:NB * MH]).then_inc(s_nT, 1)
            pe.wait_ge(s_n0e, 1)
            pe.wait_ge(s_c0, 16 * NB)
            pe.wait_ge(s_qm, 1)
            for h in range(MH):
                v = [m.v[0:n, t, bass.ds(h, 1), :] for t, n in enumerate(TILE_ROWS)]
                pe.wait_ge(s_nbf, h + 1)
                pe.matmul(m.bank[0][:, 0:392], m.ident[0:MH, bass.ds(h, 1)].to_broadcast((MH, 128)), m.grow[:, :],
                          start=True, stop=True).then_inc(s_nb, 1)
                pe.wait_ge(s_pt, h + 1)
                for o, k0, kn, q0, qn in ((0, 0, 128, 0, 256), (256, 128, 128, 128, 128), (384, 256, 64, 256, 64)):
                    last = pe.matmul(m.bank[1][0:kn, o:o + qn], m.mkT[:, bass.ds(h, 1), k0:k0 + kn],
                                     m.mqT[:, bass.ds(h, 1), q0:q0 + qn], start=True, stop=True)
                last.then_inc(s_s, 1)
                pe.wait_ge(s_pt, h + 2)
                pe.wait_ge(s_numf, 3 * h + 3)
                pe.matmul(m.bank[2][:, 0:VX], pt[:, 0:128], v[0], start=True, stop=True).then_inc(s_num, 1)
                pe.matmul(m.bank[3][:, 0:VX], pt[:, 128:256], v[0], start=True, stop=False)
                pe.matmul(m.bank[3][:, 0:VX], pt[:, 256:384], v[1], start=False, stop=True).then_inc(s_num, 1)
                pe.matmul(m.bank[4][:, 0:VX], pts[:, :], v[2], start=True, stop=False)
                for b in range(NB):
                    last = pe.matmul(m.bank[4][:, 0:VX], qm[:, 128 * b:128 * b + 128], ce[:, b, bass.ds(h, 1), :],
                                     start=False, stop=(b == NB - 1))
                last.then_inc(s_num, 1)
                pe.wait_ge(s_kw, h + 1)
                pe.wait_ge(s_cpe, h + 1)
                for t in range(2):
                    last = pe.matmul(m.bank[5][:, 0:VX], kw[:, t, :], v[t], start=(t == 0), stop=(t == 1))
                last.then_inc(s_cp, 1)
                for b in range(NB):
                    pe.wait_ge(s_cse, NB * h + b + 1)
                    pe.matmul(m.bank[6 + b % 2][:, 0:VX], kws[:, b, :], v[2], start=True, stop=True).then_inc(s_cs, 1)
            pe.wait_ge(s_nc, 1)
            pe.transpose(m.bank[0][0:MH + NB * MH, 0:128], ncol[:, :], m.ident[:, :]).then_inc(s_nct, 1)
            pe.wait_ge(s_hn, 1)
            for k in range(KD):
                if k >= 2:
                    pe.wait_ge(s_hTe, k - 1)
                for t, n in enumerate(TILE_ROWS):
                    last = pe.transpose(m.bank[2 + k % 2][:, t * 128:t * 128 + n],
                                        ht[0:n, t, k // 2, (k % 2) * 128:(k % 2 + 1) * 128], m.ident[0:n, 0:n])
                last.then_inc(s_hT, 1)

        @block.scalar
        def _(act):
            act.sem_inc(s_cpe, 1)
            act.wait_ge(s_nT, 1)
            act.activation(ce[:, :, :, DV:VX].rearrange("p b h o -> p (b h) o"), m.bank[5][:, 0:NB * MH].unsqueeze(2),
                           ACT.Copy).then_inc(s_n0e, 1)
            for h in range(MH):
                act.wait_ge(s_arg, h + 1)
                act.activation(wi[:, :], wi[:, :], ACT.Exp)
                act.activation(wis[:, :], wis[:, :], ACT.Exp).then_inc(s_w, 1)
                act.wait_ge(s_cp, h + 1)
                act.activation(cp[:, bass.ds(h, 1), :], m.bank[5][:, 0:VX], ACT.Copy)
                act.activation(ncol[:, bass.ds(h, 1)], m.bank[5][:, DV:VX], ACT.Copy).then_inc(s_cpe, 1)
                act.wait_ge(s_h, h + 1)
                for t, n in enumerate(TILE_ROWS):
                    if h + t > 0:
                        act.wait_ge(s_sq, NT * h + t)
                    act.activation(junk[0:n, :], ht[0:n, t, bass.ds(h, 1), :], ACT.Square,
                                   accum_out=ss[0:n, t, bass.ds(h, 1)]).then_inc(s_sq, 1)
            act.wait_ge(s_rs, 1)
            act.activation(ss[:, :, :], ss[:, :, :], ACT.Sqrt).then_inc(s_rt, 1)

        @block.vector
        def _(dve):
            link = Link(dve, s_chain)
            dve.sem_inc(s_nbf, 1)
            dve.sem_inc(s_numf, 3)
            dve.sem_inc(s_pt, 1)
            dve.sem_inc(s_cse, 2)
            link.go(dve.memset(ss[:, :, :], 1.0))
            link.go(dve.memset(pts[:, :], 0.0))
            link(dve.memset(qm[:, :], 0.0))
            dve.sem_inc(s_qm, 1)
            for h in range(MH):
                link.loop(h, 25 + NB)
                col = lambda n, t, q: m.gcol[0:n, t, q, bass.ds(h, 1)]
                link(dve.tensor_scalar(wem[:, :], m.seq_onehot[:, :], col(64, 2, 2), None, ALU.mult))
                dve.wait_ge(s_cpe, h + 1)
                for t in range(2):
                    link.go(dve.tensor_scalar(kw[:, t, :], m.mk[:, bass.ds(h, 1), t * DQK:(t + 1) * DQK], col(128, t, 2), None, ALU.mult))
                link(dve.tensor_tensor(kws[:, :, :], m.mk[0:64, bass.ds(h, 1), 2 * DQK:].to_broadcast((64, NB, DQK)),
                                       wem[:, :].unsqueeze(2).to_broadcast((64, NB, DQK)), ALU.mult))
                dve.sem_inc(s_kw, 1)
                dve.wait_ge(s_nb, h + 1)
                nb = m.bank[0]
                link.go(dve.scalar_tensor_tensor(wi[:, 0:128], nb[:, 0:128], col(128, 0, 0), m.causal_st[:, :], ALU.add, ALU.add))
                link.go(dve.tensor_scalar(wi[:, 128:256], nb[:, 128:256], col(128, 0, 0), None, ALU.add))
                link.go(dve.scalar_tensor_tensor(wi[:, 256:384], nb[:, 128:256], col(128, 1, 0), m.causal_st[:, :], ALU.add, ALU.add))
                link(dve.scalar_tensor_tensor(wis[:, :], nb[0:64, 256:320], col(64, 2, 0), m.same_seq[:, :], ALU.add, ALU.add))
                dve.sem_inc(s_arg, 1)
                link.go(dve.tensor_tensor(qm[:, :].rearrange("p (b x) -> p b x", x=QW)[:, :, 0:TS],
                                          m.mqT[:, bass.ds(h, 1), SEQ:].rearrange("p h (b t) -> p (h b) t", t=TS),
                                          nb[:, NTOK:NTOK + 64].rearrange("p (b t) -> p b t", t=TS), ALU.mult))
                link(dve.tensor_copy(dec[:, :], nb[:, NTOK + 64:NTOK + 64 + NB]))
                dve.sem_inc(s_nbf, 1)
                dve.wait_ge(s_w, h + 1)
                dve.wait_ge(s_s, h + 1)
                link.go(dve.tensor_tensor(pt[:, :], m.bank[1][:, 0:384], wi[:, :], ALU.mult))
                link(dve.tensor_tensor(pts[:, 0:64], m.bank[1][0:64, 384:448], wis[:, :], ALU.mult))
                dve.sem_inc(s_pt, 1)
                for t, n in enumerate(TILE_ROWS):
                    dve.wait_ge(s_num, 3 * h + t + 1)
                    ps = m.bank[2 + t]
                    link(dve.scalar_tensor_tensor(den[0:n, t:t + 1], ps[0:n, DV:VX], -1.0, col(n, t, 1), ALU.mult, ALU.max))
                    link(dve.tensor_tensor(den[0:n, t:t + 1], ps[0:n, DV:VX], den[0:n, t:t + 1], ALU.max))
                    link(dve.reciprocal(den[0:n, t:t + 1], den[0:n, t:t + 1]))
                    link(dve.tensor_scalar(ht[0:n, t, bass.ds(h, 1), :], ps[0:n, 0:DV], den[0:n, t:t + 1], None, ALU.mult))
                    dve.sem_inc(s_numf, 1)
                dve.sem_inc(s_h, 1)
                for b in range(NB):
                    dve.wait_ge(s_cs, NB * h + b + 1)
                    st = ce[:, b, bass.ds(h, 1), :]
                    link(dve.scalar_tensor_tensor(st, st, dec[:, b:b + 1], m.bank[6 + b % 2][:, 0:VX], ALU.mult, ALU.add))
                    dve.sem_inc(s_cse, 1)
                link.go(dve.tensor_copy(ncol[:, MH:].rearrange("p (b h) -> p b h", h=MH)[:, :, bass.ds(h, 1)],
                                        ce[:, :, bass.ds(h, 1), DV:VX].rearrange("p b h o -> p b (h o)")))
            link.done(MH)
            link.wait()
            dve.wait_ge(s_cpe, MH + 1)
            dve.sem_inc(s_nc, 1)
            dve.wait_ge(s_sq, 3 * MH)
            link(dve.tensor_scalar(ss[:, :, :], ss[:, :, :], 1.0 / DV, EPS, ALU.mult, ALU.add))
            dve.sem_inc(s_rs, 1)
            dve.wait_ge(s_rt, 1)
            link(dve.reciprocal(ss[:, :, :], ss[:, :, :]))
            for t, n in enumerate(TILE_ROWS):
                for h in range(MH):
                    link.go(dve.tensor_scalar(ht[0:n, t, h, :], ht[0:n, t, h, :], ss[0:n, t, h:h + 1], None, ALU.mult))
            link.wait()
            dve.sem_inc(s_hn, 1)
            dve.wait_ge(s_nct, 1)
            dve.tensor_copy(nrow[:, :], m.bank[0][0:MH + NB * MH, 0:128]).then_inc(s_nce, 1)
            for k in range(KD):
                dve.wait_ge(s_hT, k + 1)
                dve.scalar_tensor_tensor(m.hmT[:, k, :], m.bank[2 + k % 2][:, 0:NTOK], m.par[:, 5, k:k + 1],
                                         m.zf[:, KD + k, :], ALU.mult, ALU.mult).then_inc(s_hTe, 1)


def nsa_prepare(nc, m, a):
    s_w, s_z, s_b, s_g1, s_g2 = m.sem("wcmp_in"), m.sem("wcmp_zero"), m.sem("bcmp_in"), m.sem("gate_out"), m.sem("gate_in")
    s_t, s_te, s_c, s_ce, s_ct, s_cte = (m.sem("kT_done"), m.sem("kT_ev"), m.sem("cmpp_done"), m.sem("cmpp_ev"),
                                         m.sem("cvp_T"), m.sem("cvp_ev"))
    s_out, s_pt = m.sem("kv_out"), m.sem("pages_in")
    gates = nc.dram_tensor("gates_scratch", (NB * TS, 48), FP).ap()
    with ExitStack() as c:
        ccp = c.enter_context(nc.sbuf_tensor("ccp", [128, 2, NC_P], FP))
        block = c.enter_context(nc.Block())

        @block.sync
        def _(sp):
            sp.wait_ge(s_z, 1)
            for g in range(2):
                for i in range(2):
                    sp.dma_start(m.wc[g * HD:(g + 1) * HD, i * CMP:(i + 1) * CMP, g * HD:(g + 1) * HD],
                                 a.w_cmp[0, i].rearrange("r d e -> d r e")).then_inc(s_w, 16)
            sp.dma_start(gates, m.ngate[0:64, 2, :]).then_inc(s_g1, 16)
            sp.wait_ge(s_g1, 16)
            for h in range(16):
                sp.dma_start(m.gate_s[h * TS:(h + 1) * TS, :, :],
                             gates.rearrange("(b t) (h r) -> h t b r", t=TS, r=3)[h]).then_inc(s_g2, 16)
            sp.wait_ge(s_g2, 256)

        @block.scalar
        def _(act):
            for g in range(2):
                act.dma_start(m.bcmp[g * HD:(g + 1) * HD, :], a.b_cmp[0].rearrange("c e -> e c"),
                              allow_slow_non_contiguous=True).then_inc(s_b, 16)
            act.dma_start(m.pages[:, :], a.page_table.rearrange("(o b) n -> o (b n)", o=1)).then_inc(s_pt, 16)
            kvp = a.new_kv_p.rearrange("o (t p) l c g d -> t p (o l c g d)", p=128)
            wnp = a.new_win_p.rearrange("l o (t p) c g d -> t p (l o c g d)", p=128)
            for t in range(2):
                act.dma_start(kvp[t], m.kv[:, t, 0:512]).then_inc(s_out, 16)
                act.dma_start(wnp[t], m.kv[:, t, 512:KVC]).then_inc(s_out, 16)
            act.dma_start(a.new_kv_s.rearrange("b t l c g d -> (b t) (l c g d)"), m.kv[0:64, 2, 0:512]).then_inc(s_out, 16)
            nws = a.new_win_s[0].rearrange("b w c g d -> b w (c g d)")
            act.dma_start(nws[:, 0:WIN - TS, :], a.cache_win_kv[0].rearrange("b w c g d -> b w (c g d)")[:, TS:, :]).then_inc(s_out, 16)
            for b in range(NB):
                act.dma_start(nws[b, WIN - TS:, :], m.kv[b * TS:(b + 1) * TS, 2, 512:KVC]).then_inc(s_out, 16)
            act.wait_ge(s_out, 16 * (6 + NB))
            act.wait_ge(s_pt, 16)
            act.wait_ge(s_b, 32)
            for i in range(2):
                act.wait_ge(s_c, i + 1)
                act.activation(ccp[:, i, :], m.bank[4 + i][:, 0:NC_P], ACT.Identity, bias=m.bcmp[:, i:i + 1]).then_inc(s_ce, 1)
            act.wait_ge(s_ce, 2)
            act.activation(m.ckp[:, :], ccp[:, 0, :], ACT.Copy)
            act.wait_ge(s_ct, 1)
            act.activation(m.cvp[:, :], m.bank[6][0:NC_P, 0:128], ACT.Copy)

        @block.tensor
        def _(pe):
            for i, off in enumerate((0, 128, 256, 512)):
                for t, n in enumerate(TILE_ROWS):
                    last = pe.transpose(m.bank[i][:, t * 128:t * 128 + n], m.kv[0:n, t, off:off + 128], m.ident[0:n, 0:n])
                last.then_inc(s_t, 1)
            pe.wait_ge(s_te, 4)
            pe.wait_ge(s_w, 64)
            for i in range(2):
                for r in range(CMP):
                    last = pe.matmul(m.bank[4 + i][:, 0:NC_P], m.wc[:, i * CMP + r, :],
                                     m.kT[:, i, r:r + CST * (NC_P - 1) + 1:CST], start=(r == 0), stop=(r == CMP - 1))
                last.then_inc(s_c, 1)
            pe.wait_ge(s_ce, 2)
            pe.transpose(m.bank[6][0:NC_P, 0:128], ccp[:, 1, :], m.ident[:, :]).then_inc(s_ct, 1)

        @block.vector
        def _(dve):
            for i in range(4):
                dve.wait_ge(s_t, i + 1)
                dve.tensor_copy(m.kT[:, i, :], m.bank[i][:, 0:NTOK]).then_inc(s_te, 1)

        @block.gpsimd
        def _(pool):
            pool.memset(m.wc[:, :, :], 0.0).then_inc(s_z, 1)
            pool.memset(m.qbd[:, :], 0.0)
            pool.memset(m.key_mask[:, 0:128], 0.0)
            pool.tensor_copy(m.key_mask[:, 128:256], m.causal_tk[:, :])


def nsa_prompt(nc, m, a):
    s_q, s_qf, s_sc, s_msk = m.sem("np_q"), m.sem("np_qfree"), m.sem("np_scores"), m.sem("np_masked")
    s_nm, s_ex, s_dg, s_tp = m.sem("np_negmax"), m.sem("np_exp"), m.sem("np_diag"), m.sem("np_T")
    s_ea, s_ed, s_pv, s_oe = m.sem("np_ev_act"), m.sem("np_ev_dve"), m.sem("np_pv"), m.sem("np_out")
    s_chain = m.sem("np_dve")
    PER = 18
    with ExitStack() as c:
        def sb(name, shape):
            return c.enter_context(nc.sbuf_tensor(name, shape, FP))

        qs = sb("np_qs", [128, 128])
        s = [sb(f"np_s{p}", [128, 2, 2, SEQ]) for p in range(2)]
        sc = [sb(f"np_sc{p}", [128, 2, NC_P]) for p in range(2)]
        mx = [sb(f"np_mx{p}", [128, 6]) for p in range(2)]
        sm = [sb(f"np_sm{p}", [128, 6]) for p in range(2)]
        dg = sb("np_dg", [128, 6, 128])
        pt = sb("np_pt", [128, 2, 512])
        ptc = sb("np_ptc", [NC_P, 2, 128])
        block = c.enter_context(nc.Block())

        def turns(eng, turn):
            for T in range(2):
                with eng.Fori(0, 4) as i:
                    for p in range(2):
                        turn(T, 2 * i + p, p, 2 * i + (8 * T + p))

        @block.gpsimd
        def _(pool):
            def turn(T, u, p, U):
                pool.wait_ge(s_qf, U + 1)
                pool.tensor_copy(qs[:, :], m.zf[:, bass.ds(u + 32, 1), T * 128:(T + 1) * 128]).then_inc(s_q, 1)
            turns(pool, turn)

        @block.tensor
        def _(pe):
            pe.sem_inc(s_qf, 1)

            def turn(T, u, p, U):
                nk = 128 * (T + 1)
                pe.wait_ge(s_q, U + 1)
                pe.wait_ge(s_msk, U + 1)
                for g in range(2):
                    q = qs[g * HD:(g + 1) * HD, :]
                    for i, kind in enumerate((2, 3)):
                        pe.matmul(m.bank[g][:, i * nk:(i + 1) * nk], q, m.kT[g * HD:(g + 1) * HD, kind, 0:nk],
                                  start=True, stop=True)
                    last = pe.matmul(m.bank[(2, 7)[g]][:, 0:NC_P], q, m.ckp[g * HD:(g + 1) * HD, :],
                                     start=True, stop=True)
                last.then_inc(s_sc, 1)
                pe.wait_ge(s_sc, U + 1)
                pe.sem_inc(s_qf, 1)
                pe.wait_ge(s_dg, U + 1)
                pe.wait_ge(s_ea, U + 1)
                pe.wait_ge(s_ed, U + 1)
                for g in range(2):
                    for br in range(2):
                        for ch in range(T + 1):
                            o = (br * (T + 1) + ch) * 128
                            pe.matmul(m.bank[3 + g][:, o:o + 128], s[p][:, g, br, ch * 128:(ch + 1) * 128],
                                      dg[:, 2 * g + br, :], start=True, stop=True)
                    last = pe.matmul(m.bank[5][0:NC_P, g * 128:(g + 1) * 128], sc[p][:, g, :], dg[:, 4 + g, :],
                                     start=True, stop=True)
                last.then_inc(s_tp, 1)
                pe.wait_ge(s_ea, U + 2)
                pe.wait_ge(s_ed, U + 2)
                pe.wait_ge(s_oe, U + 1)
                for g in range(2):
                    out = m.bank[6][g * HD:(g + 1) * HD, 0:128]
                    for br, off in enumerate((384, 640)):
                        for ch in range(T + 1):
                            o = (br * (T + 1) + ch) * 128
                            pe.matmul(out, m.kv[:, ch, off + g * HD:off + (g + 1) * HD], pt[:, g, o:o + 128],
                                      start=(br + ch == 0), stop=False)
                    last = pe.matmul(out, m.cvp[:, g * HD:(g + 1) * HD], ptc[:, g, :], start=False, stop=True)
                last.then_inc(s_pv, 1)
            turns(pe, turn)

        @block.scalar
        def _(act):
            act.sem_inc(s_ea, 1)
            act.sem_inc(s_oe, 1)

            def turn(T, u, p, U):
                nk = 128 * (T + 1)
                act.wait_ge(s_nm, U + 1)
                for g in range(2):
                    for br in range(2):
                        act.activation(s[p][:, g, br, 0:nk], s[p][:, g, br, 0:nk], ACT.Exp,
                                       bias=mx[p][:, 2 * g + br:2 * g + br + 1], accum_out=sm[p][:, 2 * g + br:2 * g + br + 1])
                for g in range(2):
                    last = act.activation(sc[p][:, g, :], sc[p][:, g, :], ACT.Exp, bias=mx[p][:, 4 + g:5 + g],
                                          accum_out=sm[p][:, 4 + g:5 + g])
                last.then_inc(s_ex, 1)
                act.wait_ge(s_tp, U + 1)
                act.activation(ptc[:, :, :], m.bank[5][0:NC_P, 0:256].rearrange("p (g t) -> p g t", g=2), ACT.Copy)
                act.activation(pt[:, 0, 0:2 * nk], m.bank[3][:, 0:2 * nk], ACT.Copy).then_inc(s_ea, 1)
                act.wait_ge(s_pv, U + 1)
                act.activation(m.hnT[:, bass.ds(u, 1), T * 128:(T + 1) * 128], m.bank[6][:, 0:128], ACT.Copy).then_inc(s_oe, 1)
            turns(act, turn)

        @block.vector
        def _(dve):
            link = Link(dve, s_chain)
            dve.sem_inc(s_msk, 1)
            dve.sem_inc(s_ed, 1)

            def turn(T, u, p, U):
                nk = 128 * (T + 1)
                link.base, link.n = U * PER, 0
                dve.wait_ge(s_sc, U + 1)
                for g in range(2):
                    link.go(dve.tensor_tensor(s[p][:, g, :, 0:nk], m.bank[g][:, 0:2 * nk].rearrange("p (r k) -> p r k", r=2),
                                              m.key_mask[:, SEQ - nk:SEQ].unsqueeze(1).to_broadcast((128, 2, nk)), ALU.add))
                    link.go(dve.tensor_tensor(sc[p][:, g, :], m.bank[(2, 7)[g]][:, 0:NC_P], m.cmp_mask[:, T, :], ALU.add))
                link.wait()
                dve.sem_inc(s_msk, 1)
                link.go(dve.tensor_reduce(mx[p][:, 0:4], s[p][:, :, :, 0:nk], AX.X, ALU.max))
                link(dve.tensor_reduce(mx[p][:, 4:6], sc[p][:, :, :], AX.X, ALU.max))
                link(dve.tensor_scalar(mx[p][:, :], mx[p][:, :], NEG_CLAMP, -1.0, ALU.max, ALU.mult))
                dve.sem_inc(s_nm, 1)
                dve.wait_ge(s_ex, U + 1)
                link(dve.tensor_scalar(sm[p][:, :], sm[p][:, :], TINY, None, ALU.max))
                link(dve.reciprocal(sm[p][:, :], sm[p][:, :]))
                gate = m.ngate[:, T, :].rearrange("p (g j r) -> p g j r", g=2, r=3)
                link.go(dve.tensor_tensor(sm[p][:, 0:4].rearrange("p (g r) -> p g r", g=2), sm[p][:, 0:4].rearrange("p (g r) -> p g r", g=2),
                                          gate[:, :, bass.ds(u, 1), 1:3].rearrange("p g j r -> p g (j r)"), ALU.mult))
                link(dve.tensor_tensor(sm[p][:, 4:6], sm[p][:, 4:6],
                                       gate[:, :, bass.ds(u, 1), 0:1].rearrange("p g j r -> p g (j r)").rearrange("p g r -> p (g r)"), ALU.mult))
                for i in range(6):
                    link.go(dve.tensor_scalar(dg[:, i, :], m.ident[:, :], sm[p][:, i:i + 1], None, ALU.mult))
                link.wait()
                dve.sem_inc(s_dg, 1)
                dve.wait_ge(s_tp, U + 1)
                link(dve.tensor_copy(pt[:, 1, 0:2 * nk], m.bank[4][:, 0:2 * nk]))
                dve.sem_inc(s_ed, 1)
                assert link.n == PER, link.n
            turns(dve, turn)


def nsa_sample(nc, m, a):
    s_pg = [m.sem(f"pages_slot{p}") for p in range(2)]
    s_wn = [m.sem(f"win_slot_s{p}") for p in range(2)]
    s_free, s_q, s_qf = m.sem("ns_free"), m.sem("ns_q"), m.sem("ns_qfree")
    s_t, s_te, s_c, s_ce, s_ct = m.sem("ns_T"), m.sem("ns_T_ev"), m.sem("ns_cmp"), m.sem("ns_cmp_ev"), m.sem("ns_cvT")
    s_cv, s_sc, s_pc, s_imp = m.sem("ns_cv_ev"), m.sem("ns_scores"), m.sem("ns_pcmp"), m.sem("ns_imp")
    s_cm, s_ec, s_nm, s_ex = m.sem("ns_cmax"), m.sem("ns_cexp"), m.sem("ns_negmax"), m.sem("ns_exp")
    s_dg, s_p, s_pe_, s_pv, s_o = m.sem("ns_diag"), m.sem("ns_pT"), m.sem("ns_pT_ev"), m.sem("ns_pv"), m.sem("ns_out")
    s_chain, s_pd = m.sem("ns_dve"), m.sem("ns_pT_ev_dve")
    NS1, NS2, NS3, NS4 = PAST, PAST + 64, PAST + 64 + WIN, PAST + 64 + WIN + 64
    PER = 25
    with ExitStack() as c:
        def sb(name, shape):
            return c.enter_context(nc.sbuf_tensor(name, shape, FP))

        pg = [sb(f"ns_pg{p}", [128, NPG, 512]) for p in range(2)]
        wn = [sb(f"ns_wn{p}", [128, WIN // 128, 256]) for p in range(2)]
        kT = sb("ns_kT", [128, 3 * PAST + WIN])
        ck = sb("ns_ck", [128, NC_S])
        cvT = sb("ns_cvT", [128, NC_S])
        cv = sb("ns_cv", [NC_S, 128])
        s = sb("ns_s", [128, NS4])
        pc = sb("ns_pc", [128, NC_S])
        pen = sb("ns_pen", [128, 16])
        imp = sb("ns_imp", [128, 14])
        st = sb("ns_st", [128, 8])
        dg = sb("ns_dg", [128, 3, 128])
        pt = sb("ns_pt", [128, 15, 128])
        block = c.enter_context(nc.Block())

        def turns(eng, turn):
            with eng.Fori(0, NB // 2) as i:
                for p in range(2):
                    turn(2 * i + p, p)

        @block.sync
        def _(sp):
            def turn(b, p):
                sp.wait_ge(s_free, b + 1)
                for j in range(NPG):
                    page = sp.value_load(m.pages[0:1, bass.ds(b * NPG + j, 1)], min_val=0, max_val=a.cache_kv.shape[0] - 1)
                    sp.dma_start(pg[p][:, j, :], a.cache_kv[bass.ds(page, 1)].rearrange("n r l c g d -> r (n l c g d)")).then_inc(s_pg[p], 16)
                sp.dma_start(wn[p][:, :, :], a.cache_win_kv[0, bass.ds(b, 1)].rearrange("b (w r) c g d -> r (b w) (c g d)", r=128)).then_inc(s_wn[p], 16)
            turns(sp, turn)

        @block.gpsimd
        def _(pool):
            def turn(b, p):
                pool.wait_ge(s_qf, b + 1)
                for g in range(2):
                    pool.tensor_copy(m.qbd[g * HD:(g + 1) * HD, g * 64:(g + 1) * 64].rearrange("p (h t) -> p h t", t=TS),
                                     m.zf[g * HD:(g + 1) * HD, 32:40, bass.ds(b * TS + SEQ, TS)]).then_inc(s_q, 1)
            turns(pool, turn)

        @block.tensor
        def _(pe):
            pe.sem_inc(s_free, 2)
            pe.sem_inc(s_qf, 1)

            def turn(b, p):
                pe.wait_ge(s_pg[p], (b - p) * (8 * NPG) + 16 * NPG)
                pe.wait_ge(s_wn[p], (b - p) * 8 + 16)
                for f in range(7):
                    pe.wait_ge(s_te, 7 * b + f + 1)
                    for j in range(4):
                        src = (pg[p][:, (f % 2) * 4 + j, (f // 2) * 128:(f // 2 + 1) * 128] if f < 6 else wn[p][:, j, 0:128])
                        last = pe.transpose(m.bank[(7 * p + f) % 2][:, j * 128:(j + 1) * 128], src, m.ident[:, :])
                    last.then_inc(s_t, 1)
                pe.wait_ge(s_te, 7 * b + 9)
                pe.wait_ge(s_o, b + 1)
                for i in range(2):
                    for r in range(CMP):
                        last = pe.matmul(m.bank[2 + i][:, 0:NC_S], m.wc[:, i * CMP + r, :],
                                         kT[:, i * PAST + r:i * PAST + r + CST * (NC_S - 1) + 1:CST], start=(r == 0), stop=(r == CMP - 1))
                    last.then_inc(s_c, 1)
                pe.wait_ge(s_ce, 2 * b + 2)
                pe.matmul(m.bank[2][0:NC_S, 0:128], cvT[:, :], m.ident[:, :], start=True, stop=True).then_inc(s_ct, 1)
                pe.wait_ge(s_q, 2 * b + 2)
                pe.wait_ge(s_pe_, b + 1)
                pe.wait_ge(s_pd, b + 1)
                q = m.qbd[:, :]
                pe.matmul(m.bank[7][:, 0:NC_S], q, ck[:, :], start=True, stop=True)
                pe.matmul(m.bank[7][:, 64:128], q, m.kT[:, 2, SEQ:], start=True, stop=True)
                pe.matmul(m.bank[7][:, 128:192], q, m.kT[:, 3, SEQ:], start=True, stop=True).then_inc(s_sc, 1)
                pe.wait_ge(s_te, 7 * b + 9)
                pe.matmul(m.bank[4][:, :], q, kT[:, 2 * PAST:2 * PAST + 512], start=True, stop=True)
                pe.matmul(m.bank[5][:, :], q, kT[:, 2 * PAST + 512:3 * PAST], start=True, stop=True)
                pe.matmul(m.bank[6][:, :], q, kT[:, 3 * PAST:], start=True, stop=True).then_inc(s_sc, 1)
                pe.wait_ge(s_sc, 2 * b + 2)
                pe.sem_inc(s_qf, 1)
                pe.wait_ge(s_pc, b + 1)
                pe.matmul(m.bank[3][:, 0:NC_S], m.peer[:, :], pc[:, :], start=True, stop=True).then_inc(s_imp, 1)
                pe.wait_ge(s_dg, b + 1)
                for o in range(8):
                    pe.matmul(m.bank[4 + o // 4][:, (o % 4) * 128:(o % 4 + 1) * 128], s[:, o * 128:(o + 1) * 128], dg[:, 0, :],
                              start=True, stop=True)
                for o in range(4):
                    pe.matmul(m.bank[6][:, o * 128:(o + 1) * 128], s[:, NS2 + o * 128:NS2 + (o + 1) * 128], dg[:, 1, :],
                              start=True, stop=True)
                pe.matmul(m.bank[7][0:64, 0:128], s[:, NS1:NS2], dg[:, 0, :], start=True, stop=True)
                pe.matmul(m.bank[7][0:64, 128:256], s[:, NS3:NS4], dg[:, 1, :], start=True, stop=True)
                pe.matmul(m.bank[7][0:NC_S, 256:384], pc[:, :], dg[:, 2, :], start=True, stop=True).then_inc(s_p, 1)
                pe.wait_ge(s_cv, b + 1)
                pe.wait_ge(s_pe_, b + 2)
                pe.wait_ge(s_pd, b + 2)
                for o in range(8):
                    pe.matmul(m.bank[2][:, 0:128], pg[p][:, o, 384:512], pt[:, o, :], start=(o == 0), stop=False)
                for o in range(4):
                    pe.matmul(m.bank[2][:, 0:128], wn[p][:, o, 128:256], pt[:, 8 + o, :], start=False, stop=False)
                pe.matmul(m.bank[2][:, 0:128], m.kv[0:64, 2, 384:512], pt[0:64, 12, :], start=False, stop=False)
                pe.matmul(m.bank[2][:, 0:128], m.kv[0:64, 2, 640:768], pt[0:64, 13, :], start=False, stop=False)
                pe.matmul(m.bank[2][:, 0:128], cv[:, :], pt[0:NC_S, 14, :], start=False, stop=True).then_inc(s_pv, 1)
                pe.wait_ge(s_pv, b + 1)
                pe.sem_inc(s_free, 1)
            turns(pe, turn)

        @block.scalar
        def _(act):
            act.sem_inc(s_te, 2)
            act.sem_inc(s_o, 1)
            act.sem_inc(s_pe_, 1)

            def turn(b, p):
                for f in range(7):
                    act.wait_ge(s_t, 7 * b + f + 1)
                    act.activation(kT[:, f * 512:(f + 1) * 512], m.bank[(7 * p + f) % 2][:, :], ACT.Copy).then_inc(s_te, 1)
                act.wait_ge(s_c, 2 * b + 1)
                act.activation(ck[:, :], m.bank[2][:, 0:NC_S], ACT.Identity, bias=m.bcmp[:, 0:1]).then_inc(s_ce, 1)
                act.wait_ge(s_c, 2 * b + 2)
                act.activation(cvT[:, :], m.bank[3][:, 0:NC_S], ACT.Identity, bias=m.bcmp[:, 1:2]).then_inc(s_ce, 1)
                act.wait_ge(s_ct, b + 1)
                act.activation(cv[:, :], m.bank[2][0:NC_S, 0:128], ACT.Copy).then_inc(s_cv, 1)
                act.wait_ge(s_cm, b + 1)
                act.activation(pc[:, :], m.bank[7][:, 0:NC_S], ACT.Exp, bias=st[:, 0:1], accum_out=st[:, 1:2]).then_inc(s_ec, 1)
                act.wait_ge(s_nm, b + 1)
                act.activation(s[:, 0:NS2], s[:, 0:NS2], ACT.Exp, bias=st[:, 2:3], accum_out=st[:, 4:5])
                act.activation(s[:, NS2:NS4], s[:, NS2:NS4], ACT.Exp, bias=st[:, 3:4], accum_out=st[:, 5:6]).then_inc(s_ex, 1)
                act.wait_ge(s_p, b + 1)
                act.activation(pt[:, 0:4, :].rearrange("p o c -> p (o c)"), m.bank[4][:, :], ACT.Copy)
                act.activation(pt[:, 4:8, :].rearrange("p o c -> p (o c)"), m.bank[5][:, :], ACT.Copy).then_inc(s_pe_, 1)
                act.wait_ge(s_pv, b + 1)
                for g in range(2):
                    last = act.activation(m.hnT[g * HD:(g + 1) * HD, :, bass.ds(b * TS + SEQ, TS)],
                                          m.bank[2][g * HD:(g + 1) * HD, g * 64:(g + 1) * 64].rearrange("p (h t) -> p h t", t=TS), ACT.Copy)
                last.then_inc(s_o, 1)
            turns(act, turn)

        @block.vector
        def _(dve):
            link = Link(dve, s_chain)
            dve.sem_inc(s_pd, 1)

            def turn(b, p):
                link.base, link.n = b * PER, 0
                dve.wait_ge(s_sc, 2 * b + 1)
                link(dve.tensor_reduce(st[:, 0:1], m.bank[7][:, 0:NC_S], AX.X, ALU.max))
                link(dve.tensor_scalar(st[:, 0:1], st[:, 0:1], -1.0, None, ALU.mult))
                dve.sem_inc(s_cm, 1)
                dve.wait_ge(s_ec, b + 1)
                link(dve.reciprocal(st[:, 1:2], st[:, 1:2]))
                link(dve.tensor_scalar(pc[:, :], pc[:, :], st[:, 1:2], None, ALU.mult))
                dve.sem_inc(s_pc, 1)
                new = m.new_mask[:, bass.ds(b * 64, 64)]
                link.go(dve.tensor_tensor(s[:, NS1:NS2], m.bank[7][:, 64:128], new, ALU.add))
                link.go(dve.tensor_tensor(s[:, NS3:NS4], m.bank[7][:, 128:192], new, ALU.add))
                dve.wait_ge(s_sc, 2 * b + 2)
                link.go(dve.tensor_tensor(s[:, NS2:NS3], m.bank[6][:, :], m.win_mask[:, :], ALU.add))
                dve.wait_ge(s_imp, b + 1)
                ib = m.bank[3][:, 4:60].rearrange("p (n c) -> p n c", c=4)
                before = m.bank[3][:, 3:59].rearrange("p (n c) -> p n c", c=4)
                link(dve.tensor_reduce(imp[:, :], ib[:, :, 0:3], AX.X, ALU.add))
                for half in (before[:, :, 0:1], ib[:, :, 3:4]):
                    link(dve.scalar_tensor_tensor(imp[:, :], half.rearrange("p n c -> p (n c)"), 0.5, imp[:, :], ALU.mult, ALU.add))
                link(dve.tensor_reduce(st[:, 6:7], imp[:, :], AX.X, ALU.min))
                link(dve.tensor_scalar(imp[:, :], imp[:, :], st[:, 6:7], None, ALU.is_equal))
                link(dve.tensor_tensor(imp[:, :], imp[:, :], m.blk_idx[:, 1:15], ALU.mult))
                link(dve.tensor_reduce(st[:, 7:8], imp[:, :], AX.X, ALU.max))
                link(dve.tensor_scalar(pen[:, :], m.blk_idx[:, :], st[:, 7:8], NEG, ALU.is_equal, ALU.mult))
                for i in range(2):
                    link.go(dve.tensor_tensor(s[:, i * 512:(i + 1) * 512].rearrange("p (n k) -> p n k", k=64),
                                              m.bank[4 + i][:, :].rearrange("p (n k) -> p n k", k=64),
                                              pen[:, i * 8:(i + 1) * 8].unsqueeze(2).to_broadcast((128, 8, 64)), ALU.add))
                link.wait()
                link.go(dve.tensor_reduce(st[:, 2:3], s[:, 0:NS2], AX.X, ALU.max))
                link(dve.tensor_reduce(st[:, 3:4], s[:, NS2:NS4], AX.X, ALU.max))
                link(dve.tensor_scalar(st[:, 2:4], st[:, 2:4], -1.0, None, ALU.mult))
                dve.sem_inc(s_nm, 1)
                dve.wait_ge(s_ex, b + 1)
                link(dve.reciprocal(st[:, 4:6], st[:, 4:6]))
                gate = m.gate_s[:, bass.ds(b, 1), 1:3].rearrange("p b r -> p (b r)")
                link(dve.tensor_tensor(st[:, 4:6], st[:, 4:6], gate, ALU.mult))
                for i in range(2):
                    link.go(dve.tensor_scalar(dg[:, i, :], m.ident[:, :], st[:, 4 + i:5 + i], None, ALU.mult))
                link(dve.tensor_scalar(dg[:, 2, :], m.ident[:, :], m.gate_s[:, bass.ds(b, 1), 0:1].rearrange("p b r -> p (b r)"), None, ALU.mult))
                dve.sem_inc(s_dg, 1)
                dve.wait_ge(s_p, b + 1)
                dve.tensor_copy(pt[:, 8:12, :].rearrange("p o c -> p (o c)"), m.bank[6][:, :])
                dve.tensor_copy(pt[0:64, 12:14, :].rearrange("p o c -> p (o c)"), m.bank[7][0:64, 0:256])
                dve.tensor_copy(pt[0:NC_S, 14, :], m.bank[7][0:NC_S, 256:384]).then_inc(s_pd, 1)
                assert link.n == PER, link.n
            turns(dve, turn)


def merge(nc, m, a):
    s_wm, s_wn, s_wo = m.sem("wbm_in"), m.sem("wbn_in"), m.sem("wout_in")
    s_pe, s_ev, s_chain, s_po, s_x = m.sem("mg_branch"), m.sem("mg_gated"), m.sem("mg_dve"), m.sem("mg_out"), m.sem("mg_added")
    with ExitStack() as c:
        wm = c.enter_context(nc.sbuf_tensor("w_bm", [128, KD, D], FP))
        wn = c.enter_context(nc.sbuf_tensor("w_bn", [128, KD, D], FP))
        wo = c.enter_context(nc.sbuf_tensor("w_o", [128, KD, D], FP))
        t1 = c.enter_context(nc.sbuf_tensor("mg_t1", [128, NTOK], FP))
        mT = m.zf[:, 32:40, :]
        block = c.enter_context(nc.Block())

        @block.sync
        def _(sp):
            sp.dma_start(wm[:, :, :], a.w_branch_m[0].rearrange("(k p) n -> p k n", p=128)).then_inc(s_wm, 16)
            wn_v = a.w_branch_n[0].rearrange("(g j d) n -> g d j n", g=2, d=HD)
            for g in range(2):
                sp.dma_start(wn[g * HD:(g + 1) * HD, :, :], wn_v[g]).then_inc(s_wn, 16)
            sp.dma_start(wo[:, :, :], a.w_out[0].rearrange("(k p) n -> p k n", p=128)).then_inc(s_wo, 16)

        @block.tensor
        def _(pe):
            for f in range(KD):
                for i, (w, h, s_w, n) in enumerate(((wm, m.hmT, s_wm, 16), (wn, m.hnT, s_wn, 32))):
                    if f == 0:
                        pe.wait_ge(s_w, n)
                    if f >= 2:
                        pe.wait_ge(s_ev, f - 1)
                    for k in range(KD):
                        last = pe.matmul(m.bank[2 * i + f % 2][:, 0:NTOK], w[:, k, f * 128:(f + 1) * 128], h[:, k, :],
                                         start=(k == 0), stop=(k == KD - 1))
                last.then_inc(s_pe, 1)
            pe.wait_ge(s_wo, 16)
            pe.wait_ge(s_ev, KD)
            n = 0
            for t, rows in enumerate(TILE_ROWS):
                for h in range(2):
                    if n >= 4:
                        pe.wait_ge(s_x, n - 3)
                    for k in range(KD):
                        last = pe.matmul(m.bank[4 + n % 4][0:rows, :], mT[:, k, t * 128:t * 128 + rows],
                                         wo[:, k, h * 512:(h + 1) * 512], start=(k == 0), stop=(k == KD - 1))
                    last.then_inc(s_po, 1)
                    n += 1

        @block.vector
        def _(dve):
            link = Link(dve, s_chain)
            for f in range(KD):
                dve.wait_ge(s_pe, f + 1)
                link.go(dve.tensor_tensor(mT[:, f, :], m.bank[f % 2][:, 0:NTOK], m.zf[:, 16 + f, :], ALU.mult))
                link(dve.tensor_tensor(t1[:, :], m.bank[2 + f % 2][:, 0:NTOK], m.zf[:, 24 + f, :], ALU.mult))
                dve.tensor_tensor(mT[:, f, :], mT[:, f, :], t1[:, :], ALU.add).then_inc(s_ev, 1)
                dve.wait_ge(s_ev, f + 1)
            n = 0
            for t, rows in enumerate(TILE_ROWS):
                for h in range(2):
                    dve.wait_ge(s_po, n + 1)
                    xs = m.x[0:rows, t, h * 512:(h + 1) * 512]
                    dve.tensor_tensor(xs, xs, m.bank[4 + n % 4][0:rows, :], ALU.add).then_inc(s_x, 1)
                    n += 1


def weight_loads(sp, m, a, e, wait=None):
    for c in range(12):
        if wait is not None:
            wait(c)
        if c < 8:
            src = a.w_gu[0, bass.ds(e, 1), c * 128:(c + 1) * 128, :].rearrange("e p n -> p (e n)")
            sp.dma_start(m.wring[:, c, :], src).then_inc(m.s_slot[c], 16)
        else:
            q = c - 8
            src = a.w_dn[0, bass.ds(e, 1), q * 256:(q + 1) * 256, :].rearrange("e (j p) n -> p (e j) n", p=128)
            sp.dma_start(m.wring[:, c, :].rearrange("p (j n) -> p j n", j=2), src).then_inc(m.s_slot[c], 16)


def route(nc, m, a):
    s_g, s_bg, s_w, s_br = m.sem("g2_in"), m.sem("bgu_in"), m.sem("wr_in"), m.sem("br_in")
    s_ms, s_sq, s_xn, s_xT, s_xTe = m.sem("n2_ms"), m.sem("n2_sqrt"), m.sem("xn2_ready"), m.sem("xn2_T"), m.sem("xn2_T_ev")
    s_lg, s_bT, s_mx, s_ex, s_sel = m.sem("logits"), m.sem("bgu_T"), m.sem("top_max"), m.sem("top_exp"), m.sem("sel_ready")
    s_pos, s_wT, s_c2, s_chain = m.sem("pos_done"), m.sem("wt_T"), m.sem("bdn_in"), m.sem("route_dve")
    with ExitStack() as c:
        def sb(name, shape, dt=FP):
            return c.enter_context(nc.sbuf_tensor(name, shape, dt))

        g2 = sb("g2b", [128, D])
        br = sb("brb", [128, NE])
        bgr = sb("bgu_rows", [NE, 2 * FE])
        wr = sb("w_r", [128, KD, NE])
        xT = sb("xn2T", [128, KD, NTOK])
        junk = sb("junk2", [128, D])
        ss = sb("ss2", [128, NT])
        lg = sb("lg", [128, NT, NE])
        mx = sb("mx8", [128, NT, 8])
        ix = sb("ix8", [128, NT, 8], U32)
        ixf = sb("ixf", [128, NT, 8])
        nm = sb("nmx", [128, NT])
        sm = sb("sm4", [128, NT])
        w4 = sb("w4", [128, NT, 4])
        sel = sb("sel", [128, NT, NE])
        oh = sb("oh", [128, NE])
        cnt = sb("cnt", [128, NE])
        ext = sb("ext", [128, NE])
        cs = sb("cs", [128, NE])
        cse = sb("cse", [128, NE])
        o1 = sb("o1", [128, N_OVER, NE])
        o2 = sb("o2", [128, N_OVER, NE])
        ej = sb("ej", [128, N_OVER])
        bj = sb("bj", [128, N_OVER])
        ef = sb("ef", [1, NITEM + 1])
        block = c.enter_context(nc.Block())

        @block.sync
        def _(sp):
            sp.dma_start(g2[:, :], a.norm2_g.to_broadcast((128, D))).then_inc(s_g, 16)
            sp.dma_start(br[:, :], a.b_router.to_broadcast((128, NE))).then_inc(s_br, 16)
            sp.dma_start(wr[:, :, :], a.w_router[0].rearrange("(k p) e -> p k e", p=128)).then_inc(s_w, 16)
            sp.dma_start(bgr[:, :], a.b_gu[0]).then_inc(s_bg, 16)
            sp.dma_start(m.bdn[:, :], a.b_dn[0]).then_inc(s_c2, 16)
            sp.wait_ge(s_c2, 16)
            weight_loads(sp, m, a, 0)

        @block.tensor
        def _(pe):
            pe.wait_ge(s_bg, 16)
            for j in range(16):
                last = pe.transpose(m.bank[0][:, j * NE:(j + 1) * NE], bgr[:, j * 128:(j + 1) * 128], m.ident[0:NE, 0:NE])
            last.then_inc(s_bT, 1)
            pe.wait_ge(s_xn, NT)
            for k in range(KD):
                if k >= 2:
                    pe.wait_ge(s_xTe, k - 1)
                for t, n in enumerate(TILE_ROWS):
                    last = pe.transpose(m.bank[1 + k % 2][:, t * 128:t * 128 + n], m.xn[0:n, t, k * 128:(k + 1) * 128],
                                        m.ident[0:n, 0:n])
                last.then_inc(s_xT, 1)
            pe.wait_ge(s_xTe, KD)
            pe.wait_ge(s_w, 16)
            for t, n in enumerate(TILE_ROWS):
                for k in range(KD):
                    last = pe.matmul(m.bank[3][0:n, t * NE:(t + 1) * NE], xT[:, k, t * 128:t * 128 + n], wr[:, k, :],
                                     start=(k == 0), stop=(k == KD - 1))
            last.then_inc(s_lg, 1)
            pe.wait_ge(s_sel, 1)
            for t, n in enumerate(TILE_ROWS):
                for u in range(t + 1):
                    nu = TILE_ROWS[u]
                    lhs = m.tri if u == t else m.ones
                    pe.matmul(m.bank[4][0:n, t * NE:(t + 1) * NE], lhs[0:nu, 0:n], sel[0:nu, u, :], start=(u == 0), stop=(u == t))
            for u, nu in enumerate(TILE_ROWS):
                last = pe.matmul(m.bank[4][:, NT * NE:(NT + 1) * NE], m.ones[0:nu, :], sel[0:nu, u, :], start=(u == 0), stop=(u == NT - 1))
            last.then_inc(s_pos, 1)
            for t, n in enumerate(TILE_ROWS):
                last = pe.transpose(m.bank[5][0:NE, t * 128:t * 128 + n], m.wt[0:n, t, 0:NE], m.ident[0:n, 0:n])
            last.then_inc(s_wT, 1)

        @block.scalar
        def _(act):
            act.wait_ge(s_ms, 1)
            act.activation(ss[:, :], ss[:, :], ACT.Sqrt).then_inc(s_sq, 1)
            for t, n in enumerate(TILE_ROWS):
                act.wait_ge(s_mx, t + 1)
                act.activation(w4[0:n, t, :], mx[0:n, t, 0:4], ACT.Exp, bias=nm[0:n, t:t + 1],
                               accum_out=sm[0:n, t:t + 1]).then_inc(s_ex, 1)

        @block.vector
        def _(dve):
            link = Link(dve, s_chain)
            link.go(dve.memset(m.acc[:, :, :], 0.0))
            link.go(dve.memset(m.pos[:, :, :], -1.0))
            link.go(dve.memset(m.wt[:, :, :], 0.0))
            link.go(dve.memset(ef[:, :], 0.0))
            link(dve.memset(ss[:, :], 1.0))
            for t, n in enumerate(TILE_ROWS):
                link(dve.tensor_tensor_reduce(out=junk[0:n, :], in0=m.x[0:n, t, :], in1=m.x[0:n, t, :], scale=1.0,
                                              scalar=0.0, op0=ALU.mult, op1=ALU.add, accum_out=ss[0:n, t:t + 1]))
            link(dve.tensor_scalar(ss[:, :], ss[:, :], 1.0 / D, EPS, ALU.mult, ALU.add))
            dve.sem_inc(s_ms, 1)
            dve.wait_ge(s_sq, 1)
            link(dve.reciprocal(ss[:, :], ss[:, :]))
            dve.wait_ge(s_g, 16)
            for t, n in enumerate(TILE_ROWS):
                dve.scalar_tensor_tensor(m.xn[0:n, t, :], m.x[0:n, t, :], ss[0:n, t:t + 1], g2[0:n, :], ALU.mult,
                                         ALU.mult).then_inc(s_xn, 1)
            dve.wait_ge(s_bT, 1)
            dve.tensor_copy(m.bgu[:, :, :], m.bank[0][:, :].rearrange("p (j e) -> p j e", e=NE))
            for k in range(KD):
                dve.wait_ge(s_xT, k + 1)
                dve.tensor_copy(xT[:, k, :], m.bank[1 + k % 2][:, 0:NTOK]).then_inc(s_xTe, 1)
            dve.wait_ge(s_lg, 1)
            dve.wait_ge(s_br, 16)
            for t, n in enumerate(TILE_ROWS):
                link(dve.tensor_tensor(lg[0:n, t, :], m.bank[3][0:n, t * NE:(t + 1) * NE], br[0:n, :], ALU.add))
                link(dve.max(mx[0:n, t, :], lg[0:n, t, :]))
                link.go(dve.max_index(ix[0:n, t, :], mx[0:n, t, :], lg[0:n, t, :]))
                link(dve.tensor_scalar(nm[0:n, t:t + 1], mx[0:n, t, 0:1], -1.0, None, ALU.mult))
                dve.sem_inc(s_mx, 1)
                link(dve.tensor_copy(ixf[0:n, t, :], ix[0:n, t, :]))
                dve.wait_ge(s_ex, t + 1)
                link(dve.reciprocal(sm[0:n, t:t + 1], sm[0:n, t:t + 1]))
                link(dve.tensor_scalar(w4[0:n, t, :], w4[0:n, t, :], sm[0:n, t:t + 1], None, ALU.mult))
                for k in range(4):
                    if k == 0:
                        link.go(dve.tensor_scalar(sel[0:n, t, :], m.exp_idx[0:n, :], ixf[0:n, t, 0:1], None, ALU.is_equal))
                        link(dve.tensor_scalar(m.wt[0:n, t, 0:NE], m.exp_idx[0:n, :], ixf[0:n, t, 0:1], w4[0:n, t, 0:1],
                                               ALU.is_equal, ALU.mult))
                    else:
                        link.go(dve.scalar_tensor_tensor(sel[0:n, t, :], m.exp_idx[0:n, :], ixf[0:n, t, k:k + 1], sel[0:n, t, :],
                                                         ALU.is_equal, ALU.add))
                        link(dve.tensor_scalar(oh[0:n, :], m.exp_idx[0:n, :], ixf[0:n, t, k:k + 1], w4[0:n, t, k:k + 1],
                                               ALU.is_equal, ALU.mult))
                        link(dve.tensor_tensor(m.wt[0:n, t, 0:NE], m.wt[0:n, t, 0:NE], oh[0:n, :], ALU.add))
            dve.sem_inc(s_sel, 1)
            dve.wait_ge(s_pos, 1)
            for t, n in enumerate(TILE_ROWS):
                link(dve.tensor_tensor(m.pos[0:n, t, 0:NE], m.bank[4][0:n, t * NE:(t + 1) * NE], sel[0:n, t, :], ALU.mult))
                link(dve.tensor_scalar(sel[0:n, t, :], sel[0:n, t, :], 1e6, -1e6, ALU.mult, ALU.add))
                link(dve.tensor_tensor(m.pos[0:n, t, 0:NE], m.pos[0:n, t, 0:NE], sel[0:n, t, :], ALU.add))
            link(dve.tensor_copy(cnt[:, :], m.bank[4][:, NT * NE:(NT + 1) * NE]))
            link(dve.tensor_scalar(ext[:, :], cnt[:, :], float(SLOT), None, ALU.is_gt))
            for k in range(2, NTOK // SLOT):
                link(dve.scalar_tensor_tensor(ext[:, :], cnt[:, :], float(k * SLOT), ext[:, :], ALU.is_gt, ALU.add))
            link(dve.tensor_tensor_scan(cs[:, :], m.ones[:, 0:NE], ext[:, :], 0.0, ALU.mult, ALU.add))
            link(dve.tensor_tensor(cse[:, :], cs[:, :], ext[:, :], ALU.subtract))
            ov = (128, N_OVER, NE)
            wide = lambda t: t.unsqueeze(1).to_broadcast(ov)
            link.go(dve.tensor_tensor(o1[:, :, :], m.over_idx[:, :, :], wide(cse[:, :]), ALU.is_ge))
            link(dve.tensor_tensor(o2[:, :, :], m.over_idx[:, :, :], wide(cs[:, :]), ALU.is_ge))
            link(dve.tensor_tensor(o1[:, :, :], o1[:, :, :], o2[:, :, :], ALU.subtract))
            link(dve.tensor_tensor(o2[:, :, :], o1[:, :, :], wide(m.exp_idx[:, :]), ALU.mult))
            link(dve.tensor_reduce(ej[:, :], o2[:, :, :], AX.X, ALU.add))
            link(dve.tensor_tensor(o2[:, :, :], m.over_idx[:, :, :], wide(cse[:, :]), ALU.subtract))
            link(dve.tensor_scalar(o2[:, :, :], o2[:, :, :], 1.0, None, ALU.add))
            link(dve.tensor_tensor(o2[:, :, :], o2[:, :, :], o1[:, :, :], ALU.mult))
            link(dve.tensor_reduce(bj[:, :], o2[:, :, :], AX.X, ALU.add))
            for t, n in enumerate(TILE_ROWS):
                for dst in (m.pos, m.wt):
                    link(dve.tensor_tensor(o2[0:n, :, :], o1[0:n, :, :], dst[0:n, t, 0:NE].unsqueeze(1).to_broadcast((n, N_OVER, NE)), ALU.mult))
                    link(dve.tensor_reduce(dst[0:n, t, NE:NITEM], o2[0:n, :, :], AX.X, ALU.add))
                link(dve.scalar_tensor_tensor(m.pos[0:n, t, NE:NITEM], bj[0:n, :], -float(SLOT), m.pos[0:n, t, NE:NITEM], ALU.mult, ALU.add))
            link.go(dve.tensor_copy(ef[:, 0:NE], m.exp_idx[0:1, :]))
            link(dve.tensor_copy(ef[:, NE:NITEM], ej[0:1, :]))
            link(dve.tensor_copy(m.etab[:, 0:NITEM + 1], ef[:, :]))
            link(dve.tensor_scalar(ef[:, 0:1], cs[0:1, NE - 1:NE], float(NE), None, ALU.add))
            link(dve.tensor_copy(m.etab[:, NITEM + 1:NITEM + 2], ef[:, 0:1]))
            dve.wait_ge(s_wT, 1)
            dve.tensor_copy(m.wtT[:, :], m.bank[5][0:NE, 0:NTOK])


def experts(nc, m, a):
    s_oh, s_ohw, s_g, s_xe = m.sem("ex_onehot"), m.sem("ex_onehot_w"), m.sem("ex_gathered"), m.sem("ex_xT")
    s_used, s_gf, s_tr, s_oht = m.sem("ex_chunk_used"), m.sem("ex_gu_read"), m.sem("ex_scatter_T"), m.sem("ex_scatter_m")
    s_sc, s_acc, s_gm, s_sg = m.sem("ex_scattered"), m.sem("ex_added"), m.sem("ex_gate"), m.sem("ex_sigmoid")
    s_at, s_ys, s_chain = m.sem("ex_act"), m.sem("ex_y"), m.sem("ex_dve")
    PER = 6
    with ExitStack() as c:
        def sb(name, shape):
            return c.enter_context(nc.sbuf_tensor(name, shape, FP))

        oh = sb("ex_oh", [128, NT, SLOT])
        ohw = sb("ex_ohw", [128, NT, SLOT])
        oht = sb("ex_oht", [SLOT, NT * 128])
        xe = sb("ex_xe", [128, KD, SLOT])
        gt = sb("ex_gt", [128, 8, SLOT])
        up = sb("ex_up", [128, 8, SLOT])
        sg = sb("ex_sg", [128, 8, SLOT])
        at = sb("ex_at", [128, 8, SLOT])
        ys = sb("ex_ys", [SLOT, D])
        block = c.enter_context(nc.Block())

        def n_items(eng):
            return eng.value_load(m.etab[0:1, NITEM + 1:NITEM + 2], min_val=NE, max_val=NITEM)

        @block.sync
        def _(sp):
            nw = n_items(sp)
            with sp.Fori(1, nw) as i:
                e = sp.value_load(m.etab[0:1, bass.ds(i, 1)], min_val=0, max_val=NE - 1)
                weight_loads(sp, m, a, e, wait=lambda ch: sp.wait_ge(s_used, 12 * i + (ch + 1 - 12)))

        @block.tensor
        def _(pe):
            def gather():
                for k in range(KD):
                    for t, n in enumerate(TILE_ROWS):
                        last = pe.matmul(m.bank[0][:, k * SLOT:(k + 1) * SLOT], m.xn[0:n, t, k * 128:(k + 1) * 128],
                                         oh[0:n, t, :], start=(t == 0), stop=(t == NT - 1))
                last.then_inc(s_g, 1)

            def scatter(i):
                pe.wait_ge(s_ys, i + 1)
                pe.wait_ge(s_oht, i + 1)
                for r in range(2 * NT):
                    pe.wait_ge(s_acc, 6 * i + r + 1)
                    pe.matmul(m.bank[6 + r % 2][:, :], oht[:, (r // 2) * 128:(r // 2 + 1) * 128],
                              ys[:, (r % 2) * 512:(r % 2 + 1) * 512], start=True, stop=True).then_inc(s_sc, 1)

            nw = n_items(pe)
            pe.wait_ge(s_oh, 1)
            gather()
            with pe.Fori(0, nw) as i:
                pe.wait_ge(s_xe, i + 1)
                pe.wait_ge(s_gf, i + 1)
                for k in range(KD):
                    pe.wait_ge(m.s_slot[k], 16 * i + 16)
                    for half in range(2):
                        for f in range(8):
                            o = half * FE + f * 128
                            last = pe.matmul(m.bank[2 + half][:, f * SLOT:(f + 1) * SLOT], m.wring[:, k, o:o + 128],
                                             xe[:, k, :], start=(k == 0 and f == 0), stop=(k == KD - 1), skip_group_check=True)
                    last.then_inc(s_used, 1)
                pe.wait_ge(s_oh, i + 2)
                gather()
                pe.wait_ge(s_ohw, i + 1)
                pe.wait_ge(s_oht, i + 1)
                for t, n in enumerate(TILE_ROWS):
                    last = pe.matmul(m.bank[1][0:SLOT, t * 128:t * 128 + n], ohw[0:n, t, :], m.ident[0:n, 0:n], start=True, stop=True)
                last.then_inc(s_tr, 1)
                scatter(i)
                pe.wait_ge(s_at, i + 1)
                for q in range(4):
                    pe.wait_ge(m.s_slot[8 + q], 16 * i + 16)
                    for j in range(2):
                        for h in range(2):
                            o = j * D + h * 512
                            last = pe.matmul(m.bank[4 + h][0:SLOT, :], at[:, 2 * q + j, :], m.wring[:, 8 + q, o:o + 512],
                                             start=(q + j == 0), stop=(q + j == 4), skip_group_check=True)
                    last.then_inc(s_used, 1)
            scatter(nw)

        @block.scalar
        def _(act):
            act.sem_inc(s_ys, 1)
            act.sem_inc(s_oht, 1)

            def take_x():
                act.activation(xe[:, :, :], m.bank[0][:, :].rearrange("p (k s) -> p k s", s=SLOT), ACT.Copy).then_inc(s_xe, 1)

            nw = n_items(act)
            act.wait_ge(s_g, 1)
            take_x()
            with act.Fori(0, nw) as i:
                act.wait_ge(s_gm, i + 1)
                act.activation(sg[:, :, :], gt[:, :, :], ACT.Sigmoid, scale=1.702).then_inc(s_sg, 1)
                act.wait_ge(s_g, i + 2)
                take_x()
                act.wait_ge(s_tr, i + 1)
                act.wait_ge(s_sc, 6 * i + 6)
                act.activation(oht[:, 0:NTOK], m.bank[1][0:SLOT, 0:NTOK], ACT.Copy).then_inc(s_oht, 1)
                act.wait_ge(s_used, 12 * i + 12)
                act.activation(ys[:, 0:512], m.bank[4][0:SLOT, :], ACT.Copy)
                act.activation(ys[:, 512:1024], m.bank[5][0:SLOT, :], ACT.Copy).then_inc(s_ys, 1)

        @block.vector
        def _(dve):
            link = Link(dve, s_chain)

            def one_hot(i, dst, weighted, sem):
                for t, n in enumerate(TILE_ROWS):
                    w = m.wt[0:n, t, bass.ds(i, 1)] if weighted else None
                    last = dve.tensor_scalar(dst[0:n, t, :], m.slot_idx[0:n, :], m.pos[0:n, t, bass.ds(i, 1)], w,
                                             ALU.is_equal, *((ALU.mult,) if weighted else ()))
                last.then_inc(sem, 1)

            def add_scattered(i):
                for r in range(2 * NT):
                    n = TILE_ROWS[r // 2]
                    part = m.acc[0:n, r // 2, (r % 2) * 512:(r % 2 + 1) * 512]
                    dve.wait_ge(s_sc, 6 * i + r + 1)
                    dve.tensor_tensor(part, part, m.bank[6 + r % 2][0:n, :], ALU.add).then_inc(s_acc, 1)

            nw = n_items(dve)
            dve.memset(ys[:, :], 0.0).then_inc(s_acc, 1)
            dve.memset(oht[:, :], 0.0).then_inc(s_acc, 1)
            dve.sem_inc(s_gf, 1)
            one_hot(0, oh, False, s_oh)
            one_hot(0, ohw, True, s_ohw)
            with dve.Fori(0, nw) as i:
                link.base, link.n = i * PER, 0
                e = dve.value_load(m.etab[0:1, bass.ds(i, 1)], min_val=0, max_val=NE - 1)
                dve.wait_ge(s_g, i + 1)
                one_hot(i + 1, oh, False, s_oh)
                dve.wait_ge(s_used, 12 * i + 8)
                bias = lambda h: m.bgu[:, 8 * h:8 * h + 8, bass.ds(e, 1)].to_broadcast((128, 8, SLOT))
                ps = lambda h: m.bank[2 + h][:, :].rearrange("p (f s) -> p f s", s=SLOT)
                link(dve.tensor_tensor(gt[:, :, :], ps(0), bias(0), ALU.add))
                link(dve.tensor_scalar(gt[:, :, :], gt[:, :, :], 7.0, None, ALU.min))
                dve.sem_inc(s_gm, 1)
                link(dve.tensor_tensor(up[:, :, :], ps(1), bias(1), ALU.add))
                dve.sem_inc(s_gf, 1)
                link(dve.tensor_scalar(up[:, :, :], up[:, :, :], 7.0, -7.0, ALU.min, ALU.max))
                link(dve.scalar_tensor_tensor(up[:, :, :].rearrange("p f s -> p (f s)"), up[:, :, :].rearrange("p f s -> p (f s)"), 1.0,
                                              gt[:, :, :].rearrange("p f s -> p (f s)"), ALU.add, ALU.mult))
                dve.wait_ge(s_sg, i + 1)
                link(dve.tensor_tensor(at[:, :, :], up[:, :, :], sg[:, :, :], ALU.mult))
                dve.sem_inc(s_at, 1)
                assert link.n == PER, link.n
                dve.wait_ge(s_tr, i + 1)
                one_hot(i + 1, ohw, True, s_ohw)
                dve.wait_ge(s_acc, 6 * i + 2)
                add_scattered(i)
            dve.wait_ge(s_acc, 6 * nw + 2)
            add_scattered(nw)


def finish(nc, m, a):
    s_g, s_b, s_ms, s_sq, s_chain, s_y, s_out = (m.sem("gf_in"), m.sem("bdn_sum"), m.sem("fin_ms"), m.sem("fin_sqrt"),
                                                 m.sem("fin_dve"), m.sem("y_ready"), m.sem("y_out"))
    with ExitStack() as c:
        gf = c.enter_context(nc.sbuf_tensor("gf", [128, D], FP))
        junk = c.enter_context(nc.sbuf_tensor("junk3", [128, D], FP))
        ss = c.enter_context(nc.sbuf_tensor("ss3", [128, NT], FP))
        block = c.enter_context(nc.Block())

        @block.sync
        def _(sp):
            sp.dma_start(gf[:, :], a.normf_g.rearrange("(o n) -> o n", o=1).to_broadcast((128, D))).then_inc(s_g, 16)
            sp.wait_ge(s_y, 1)
            sp.dma_start(a.y_prompt[0, 0:128], m.x[:, 0, :]).then_inc(s_out, 16)
            sp.wait_ge(s_y, 2)
            sp.dma_start(a.y_prompt[0, 128:256], m.x[:, 1, :]).then_inc(s_out, 16)
            sp.wait_ge(s_y, 3)
            sp.dma_start(a.y_sample.rearrange("b t d -> (b t) d"), m.x[0:64, 2, :]).then_inc(s_out, 16)
            sp.wait_ge(s_out, 48)

        @block.tensor
        def _(pe):
            for r in range(2 * NT):
                n = TILE_ROWS[r // 2]
                last = pe.matmul(m.bank[r][0:n, :], m.wtT[:, (r // 2) * 128:(r // 2) * 128 + n],
                                 m.bdn[:, (r % 2) * 512:(r % 2 + 1) * 512], start=True, stop=True)
            last.then_inc(s_b, 1)

        @block.scalar
        def _(act):
            act.wait_ge(s_ms, 1)
            act.activation(ss[:, :], ss[:, :], ACT.Sqrt).then_inc(s_sq, 1)

        @block.vector
        def _(dve):
            link = Link(dve, s_chain)
            link(dve.memset(ss[:, :], 1.0))
            for t, n in enumerate(TILE_ROWS):
                link.go(dve.tensor_tensor(m.x[0:n, t, :], m.x[0:n, t, :], m.acc[0:n, t, :], ALU.add))
            link.wait()
            dve.wait_ge(s_b, 1)
            for r in range(2 * NT):
                n = TILE_ROWS[r // 2]
                part = m.x[0:n, r // 2, (r % 2) * 512:(r % 2 + 1) * 512]
                link.go(dve.tensor_tensor(part, part, m.bank[r][0:n, :], ALU.add))
            link.wait()
            for t, n in enumerate(TILE_ROWS):
                link(dve.tensor_tensor_reduce(out=junk[0:n, :], in0=m.x[0:n, t, :], in1=m.x[0:n, t, :], scale=1.0,
                                              scalar=0.0, op0=ALU.mult, op1=ALU.add, accum_out=ss[0:n, t:t + 1]))
            link(dve.tensor_scalar(ss[:, :], ss[:, :], 1.0 / D, EPS, ALU.mult, ALU.add))
            dve.sem_inc(s_ms, 1)
            dve.wait_ge(s_sq, 1)
            link(dve.reciprocal(ss[:, :], ss[:, :]))
            dve.wait_ge(s_g, 16)
            for t, n in enumerate(TILE_ROWS):
                dve.scalar_tensor_tensor(m.x[0:n, t, :], m.x[0:n, t, :], ss[0:n, t:t + 1], gf[0:n, :], ALU.mult,
                                         ALU.mult).then_inc(s_y, 1)


def allocate(nc, m, c):
    def sb(name, shape, dt=FP):
        return c.enter_context(nc.sbuf_tensor(name, shape, dt))

    m.bank = [c.enter_context(nc.psum_tensor(f"bank{i}", [128, 512], FP)) for i in range(8)]
    m.ident = sb("ident", [128, 128])
    m.ones = sb("ones", [128, 128])
    m.tri = sb("tri", [128, 128])
    m.causal_st = sb("causal_st", [128, 128])
    m.causal_tk = sb("causal_tk", [128, 128])
    m.same_seq = sb("same_seq", [64, 64])
    m.seg_mul = sb("seg_mul", [MH, NTOK])
    m.seg_add = sb("seg_add", [MH, NTOK])
    m.seq_onehot = sb("seq_onehot", [64, NB])
    m.cmp_mask = sb("cmp_mask", [128, 2, NC_P])
    m.period = sb("period", [TS, 128])
    m.new8 = sb("new8", [TS, 512])
    m.win8 = sb("win8", [TS, WIN])
    m.new_mask = sb("new_mask", [128, NB * 64])
    m.win_mask = sb("win_mask", [128, WIN])
    m.peer = sb("peer", [128, 128])
    m.blk_idx = sb("blk_idx", [128, 16])
    m.slot_idx = sb("slot_idx", [128, SLOT])
    m.exp_idx = sb("exp_idx", [128, NE])
    m.over_idx = sb("over_idx", [128, N_OVER, NE])
    m.x = sb("x", [128, NT, D])


def allocate_mixers(nc, m, c):
    def sb(name, shape, dt=FP):
        return c.enter_context(nc.sbuf_tensor(name, shape, dt))

    m.par = sb("par", [128, 7, KD])
    m.bias_feat = sb("bias_feat", [128, 40])
    m.zf = sb("zf", [128, 40, NTOK])
    m.kv = sb("kv", [128, NT, KVC])
    m.ngate = sb("ngate", [128, NT, 48])
    m.gate_bias = sb("gate_bias", [MH, 2])
    m.hmT = m.zf[:, 0:KD, :]
    m.hnT = m.zf[:, KD:2 * KD, :]


def allocate_mlstm(nc, m, c):
    def sb(name, shape, dt=FP):
        return c.enter_context(nc.sbuf_tensor(name, shape, dt))

    m.xc = sb("xc", [128, KD, NTOK])
    m.mqT = sb("mqT", [128, MH, NTOK])
    m.mkT = sb("mkT", [128, MH, NTOK])
    m.mk = sb("mk", [128, MH, 3 * DQK])
    m.grow = sb("grow", [MH, NTOK + 64 + NB])
    m.gcol = sb("gcol", [128, NT, 3, MH])


def allocate_nsa(nc, m, c):
    def sb(name, shape, dt=FP):
        return c.enter_context(nc.sbuf_tensor(name, shape, dt))

    m.wc = sb("wc", [128, 2 * CMP, 128])
    m.bcmp = sb("bcmp", [128, 2])
    m.kT = sb("kT", [128, 4, NTOK])
    m.ckp = sb("ckp", [128, NC_P])
    m.cvp = sb("cvp", [NC_P, 128])
    m.gate_s = sb("gate_s", [128, NB, 3])
    m.pages = sb("pages", [1, NB * NPG], I32)
    m.qbd = sb("qbd", [128, 128])
    m.key_mask = sb("key_mask", [128, SEQ])


def allocate_moe(nc, m, c):
    def sb(name, shape, dt=FP):
        return c.enter_context(nc.sbuf_tensor(name, shape, dt))

    m.wring = sb("wring", [128, 12, 2048])
    m.s_slot = [m.sem(f"chunk{i}_in") for i in range(12)]
    m.xn = sb("xn2", [128, NT, D])
    m.acc = sb("acc", [128, NT, D])
    m.pos = sb("pos", [128, NT, NITEM + 1])
    m.wt = sb("wt", [128, NT, NITEM + 1])
    m.wtT = sb("wtT", [NE, NTOK])
    m.bgu = sb("bgu", [128, 16, NE])
    m.bdn = sb("bdn", [NE, D])
    m.etab = sb("etab", [1, NITEM + 2], I32)


def hybrid_step(nc, a, stages=31):
    with ExitStack() as c:
        m = Mem()
        done_with = []

        def sem(name):
            done_with.append(nc.alloc_semaphore(name))
            return done_with[-1]

        m.sem = sem
        allocate(nc, m, c)
        with ExitStack() as mix:
            allocate_mixers(nc, m, mix)
            make_consts(nc, m)
            with ExitStack() as cell:
                m.v = cell.enter_context(nc.sbuf_tensor("v", [128, NT, MH, VX], FP))
                m.gate_rows = cell.enter_context(nc.sbuf_tensor("gate_rows", [MH, 2, NTOK], FP))
                with ExitStack() as proj:
                    m.uT = proj.enter_context(nc.sbuf_tensor("uT", [128, KD, NTOK], FP))
                    m.bias_tok = proj.enter_context(nc.sbuf_tensor("bias_tok", [128, D + OFF_BG - OFF_NKV], FP))
                    norm_in(nc, m, a)
                    project(nc, m, a)
                allocate_mlstm(nc, m, cell)
                if stages & 1:
                    conv_silu(nc, m, a)
                    mlstm_gates(nc, m, a)
                    mlstm_heads(nc, m, a)
            nc.clear_and_free_semaphores(done_with)
            with nc.Block():
                pass
            with ExitStack() as attn:
                allocate_nsa(nc, m, attn)
                if stages & 2:
                    nsa_prepare(nc, m, a)
                    nsa_prompt(nc, m, a)
                if stages & 4:
                    nsa_sample(nc, m, a)
            if stages & 8:
                merge(nc, m, a)
        if stages & 8:
            allocate_moe(nc, m, c)
            route(nc, m, a)
        if stages & 16:
            experts(nc, m, a)
            finish(nc, m, a)


_INS = ['x_prompt', 'x_sample', 'cache_kv', 'cache_win_kv', 'state_conv', 'state_C', 'state_n', 'state_m',
        'page_table', 'norm1_g', 'w_in', 'b_in', 'w_conv', 'b_conv', 'w_mq', 'w_mk', 'g_mnorm', 'w_cmp', 'b_cmp',
        'w_branch_m', 'w_branch_n', 'w_out', 'norm2_g', 'w_router', 'b_router', 'w_gu', 'b_gu', 'w_dn', 'b_dn',
        'normf_g']
_OUTS = [('y_prompt', (1, 256, 1024)), ('y_sample', (8, 8, 1024)), ('new_kv_p', (1, 256, 1, 4, 2, 64)),
         ('new_win_p', (1, 1, 256, 2, 2, 64)), ('new_conv_p', (1, 1, 3, 1024)), ('new_C_p', (1, 1, 4, 128, 256)),
         ('new_n_p', (1, 1, 4, 128)), ('new_m_p', (1, 1, 4)), ('new_kv_s', (8, 8, 1, 4, 2, 64)),
         ('new_win_s', (1, 8, 512, 2, 2, 64)), ('new_conv_s', (1, 8, 3, 1024)), ('new_C_s', (1, 8, 4, 128, 256)),
         ('new_n_s', (1, 8, 4, 128)), ('new_m_s', (1, 8, 4))]


class Args:
    pass


def kernel(**inputs):
    import numpy as np
    import concourse.bacc as bacc
    from concourse.bass_utils import run_bass_kernel_spmd

    nc = bacc.Bacc("TRN2", target_bir_lowering=False, num_devices=1)
    arrays, a = {}, Args()
    for name in _INS:
        arr = np.ascontiguousarray(inputs[name])
        arrays[name] = arr
        a.__dict__[name] = nc.dram_tensor(name, arr.shape, mybir.dt.from_np(arr.dtype), kind="ExternalInput").ap()
    for name, shape in _OUTS:
        a.__dict__[name] = nc.dram_tensor(name, shape, FP, kind="ExternalOutput").ap()
    hybrid_step(nc, a)
    r = run_bass_kernel_spmd(nc, [arrays], core_ids=[0])
    return tuple(r.results[0][name] for name, _ in _OUTS)
```

```python
import concourse.bass as bass
from concourse import mybir
from contextlib import ExitStack

FP = mybir.dt.float32
I32 = mybir.dt.int32
U32 = mybir.dt.uint32
ALU = mybir.AluOpType
ACT = mybir.ActivationFunctionType
AX = mybir.AxisListType

D = 1024
SEQ = 256
NB = 8
TS = 8
NTOK = SEQ + NB * TS
KD = D // 128
TILE_ROWS = [128, 128, 64]
NT = len(TILE_ROWS)
EPS = 1e-6
TINY = 1e-30
NEG = -1e30
NEG_CLAMP = -1e29

MH = 4
DV = 256
DQK = 128
VX = DV + 1
HD = 64
KVC = 768
PAST = 1024
PAGE = 128
NPG = PAST // PAGE
WIN = 512
CMP = 32
CST = 16
NC_P = SEQ // CST - 1
NC_S = PAST // CST - 1
NE = 32
FE = 1024
SLOT = 64
N_OVER = 20
NITEM = NE + N_OVER
NCHUNK = 6

OFF_MX, OFF_MV, OFF_MO, OFF_MI, OFF_MF, OFF_NQ = 0, 1024, 2048, 3072, 3076, 3080
OFF_NKV, OFF_NG, OFF_BG = 4104, 4872, 4920


class Link:

    def __init__(self, eng, sem):
        self.eng, self.sem, self.base, self.n = eng, sem, 0, 0

    def go(self, ins):
        ins.then_inc(self.sem, 1)
        self.n += 1

    def wait(self):
        self.eng.wait_ge(self.sem, self.base + self.n)

    def __call__(self, ins):
        self.go(ins)
        self.wait()

    def loop(self, i, per):
        if isinstance(i, int) and i > 0:
            assert self.n == per, (self.n, per)
            self.base, self.n = i * per + self.before, 0
        else:
            self.before, self.per, self.base, self.n = self.n, per, i * per + self.n, 0

    def done(self, turns):
        assert self.n == self.per, (self.n, self.per)
        self.base, self.n = 0, self.before + turns * self.per


class Mem:
    pass


def make_consts(nc, m):
    s0, s1, s2 = m.sem("const_fill"), m.sem("const_sel"), m.sem("const_sel2")
    s_pe, s_ev = m.sem("const_pe"), m.sem("const_ev")
    with nc.Block() as block:
        @block.gpsimd
        def _(pool):
            fills = [(m.ident, 0.0), (m.ones, 1.0), (m.tri, 1.0), (m.causal_st, 0.0), (m.causal_tk, 0.0),
                     (m.same_seq, 0.0), (m.seg_mul, 1.0), (m.seg_add, 0.0), (m.seq_onehot, 1.0),
                     (m.cmp_mask, 0.0), (m.period, 1.0), (m.new8, 0.0), (m.win8, 0.0)]
            for t, v in fills:
                pool.memset(t[:], v).then_inc(s0, 1)
            pool.iota(m.blk_idx[:], [[1, 16]], base=0, channel_multiplier=0,
                      allow_small_or_imprecise_dtypes=True).then_inc(s0, 1)
            pool.iota(m.slot_idx[:], [[0, 2], [1, SLOT]], base=0, channel_multiplier=0,
                      allow_small_or_imprecise_dtypes=True).then_inc(s0, 1)
            pool.iota(m.exp_idx[:], [[1, NE]], base=0, channel_multiplier=0,
                      allow_small_or_imprecise_dtypes=True).then_inc(s0, 1)
            pool.iota(m.over_idx[:], [[1, N_OVER], [0, NE]], base=0, channel_multiplier=0,
                      allow_small_or_imprecise_dtypes=True).then_inc(s0, 1)
            pool.iota(m.part_idx[:], [[0, 1]], base=0, channel_multiplier=1,
                      allow_small_or_imprecise_dtypes=True).then_inc(s0, 1)
            pool.wait_ge(s0, len(fills) + 5)

            def sel(t, pattern, base, cm, op, fill, sem=s1):
                pool.affine_select(out=t, in_=t, pattern=pattern, compare_op=op, fill=fill,
                                   base=base, channel_multiplier=cm).then_inc(sem, 1)

            sel(m.ident[:], [[-1, 128]], 0, 1, ALU.not_equal, 1.0)
            sel(m.tri[:], [[1, 128]], 0, -1, ALU.is_gt, 0.0)
            sel(m.causal_st[:], [[1, 128]], 0, -1, ALU.is_ge, NEG)
            sel(m.causal_tk[:], [[-1, 128]], 0, 1, ALU.is_ge, NEG)
            sel(m.same_seq[:], [[1, 64]], 0, -1, ALU.is_ge, NEG)
            sel(m.seg_mul[:, SEQ:], [[0, NB], [1, TS]], 0, 0, ALU.is_gt, 0.0)
            sel(m.seg_add[:, SEQ:], [[0, NB], [1, TS]], 0, 0, ALU.is_gt, NEG)
            sel(m.seq_onehot[:], [[-TS, NB]], 0, 1, ALU.is_ge, 0.0)
            for t in range(2):
                sel(m.cmp_mask[:, t, :], [[-CST, NC_P]], 128 * t - (CMP - 1), 1, ALU.is_ge, NEG)
            sel(m.period[:], [[0, 16], [-1, TS]], 0, 1, ALU.is_equal, 0.0)
            sel(m.new8[:], [[0, NB], [0, NB], [-1, TS]], 0, 1, ALU.is_ge, NEG)
            sel(m.win8[:], [[1, WIN]], 0, -1, ALU.is_gt, NEG)
            pool.wait_ge(s1, 13)
            sel(m.same_seq[:], [[-TS, NB], [0, TS]], 0, 1, ALU.is_ge, NEG, s2)
            sel(m.seq_onehot[:], [[TS, NB]], TS - 1, -1, ALU.is_ge, 0.0, s2)
            sel(m.new8[:], [[1, NB], [-1, NB], [0, TS]], 0, 0, ALU.is_equal, NEG, s2)

        @block.tensor
        def _(pe):
            pe.wait_ge(s2, 3)
            pe.matmul(m.bank[0][:, :], m.period[:], m.new8[:], start=True, stop=True).then_inc(s_pe, 1)
            pe.matmul(m.bank[1][:, :], m.period[:], m.win8[:], start=True, stop=True).then_inc(s_pe, 1)
            pe.matmul(m.bank[2][:, 0:128], m.period[:], m.period[:], start=True, stop=True).then_inc(s_pe, 1)

        @block.vector
        def _(dve):
            dve.wait_ge(s_pe, 3)
            dve.tensor_copy(m.new_mask[:], m.bank[0][:, :])
            dve.tensor_copy(m.win_mask[:], m.bank[1][:, :])
            dve.tensor_copy(m.peer[:], m.bank[2][:, 0:128]).then_inc(s_ev, 1)
            dve.wait_ge(s_ev, 1)
            dve.memset(m.peer[0:64, 64:128], 0.0)
            dve.memset(m.peer[64:128, 0:64], 0.0)


def norm_in(nc, m, a):
    s_x, s_p, s_v = m.sem("x_in"), m.sem("params_in"), m.sem("vec_in")
    s_tp, s_ev, s_chain = m.sem("tp_done"), m.sem("tp_evicted"), m.sem("norm1_dve")
    s_ms, s_sq, s_r = m.sem("norm1_ms"), m.sem("norm1_sqrt"), m.sem("norm1_rstd")
    s_xn = m.sem("norm1_scaled")
    xp = a.x_prompt.rearrange("b (t p) d -> p (b t) d", p=128)
    xs = a.x_sample.rearrange("b t d -> (b t) d")
    with ExitStack() as c:
        xn = c.enter_context(nc.sbuf_tensor("xn1", [128, NT, D], FP))
        junk = c.enter_context(nc.sbuf_tensor("junk1", [128, D], FP))
        ss = c.enter_context(nc.sbuf_tensor("ss1", [128, NT], FP))
        prow = c.enter_context(nc.sbuf_tensor("prow", [12, D], FP))
        pcol = c.enter_context(nc.sbuf_tensor("pcol", [128, KD, 12], FP))
        block = c.enter_context(nc.Block())

        @block.sync
        def _(sp):
            sp.dma_start(m.x[:, 0:2, :], xp).then_inc(s_x, 16)
            sp.dma_start(m.x[0:64, 2, :], xs).then_inc(s_x, 16)

        @block.scalar
        def _(act):
            b_in = a.b_in
            act.dma_start(prow[0:4, :], a.w_conv[0]).then_inc(s_p, 16)
            act.dma_start(prow[4:5, :], a.b_conv).then_inc(s_p, 16)
            act.dma_start(prow[5:6, :], a.g_mnorm.rearrange("l h v -> l (h v)")).then_inc(s_p, 16)
            act.dma_start(prow[6:7, :], a.norm1_g).then_inc(s_p, 16)
            act.dma_start(prow[7:8, :], b_in[:, OFF_MX:OFF_MX + D]).then_inc(s_p, 16)
            act.dma_start(prow[8:9, :], b_in[:, OFF_MO:OFF_MO + D]).then_inc(s_p, 16)
            act.dma_start(prow[9:10, :], b_in[:, OFF_BG:OFF_BG + D]).then_inc(s_p, 16)
            act.dma_start(prow[10:11, :], b_in[:, OFF_BG + D:OFF_BG + 2 * D]).then_inc(s_p, 16)
            for g in range(2):
                act.dma_start(prow[11:12, :].rearrange("p (j g d) -> p g j d", g=2, d=HD)[:, g],
                              b_in[:, OFF_NQ + g * 512:OFF_NQ + (g + 1) * 512].rearrange("l (j d) -> l j d", d=HD)).then_inc(s_p, 16)
            act.dma_start(m.bias_tok[:, 0:D], b_in[:, OFF_MV:OFF_MV + D].to_broadcast((128, D))).then_inc(s_v, 16)
            act.dma_start(m.bias_tok[:, D:], b_in[:, OFF_NKV:OFF_BG].to_broadcast((128, OFF_BG - OFF_NKV))).then_inc(s_v, 16)
            act.dma_start(m.gate_bias[:, 0:1], b_in[:, OFF_MI:OFF_MF].rearrange("l h -> h l")).then_inc(s_v, 16)
            act.dma_start(m.gate_bias[:, 1:2], b_in[:, OFF_MF:OFF_NQ].rearrange("l h -> h l")).then_inc(s_v, 16)
            act.wait_ge(s_ms, 1)
            act.activation(ss[:, :], ss[:, :], ACT.Sqrt).then_inc(s_sq, 1)
            act.wait_ge(s_v, 64)

        @block.vector
        def _(dve):
            link = Link(dve, s_chain)
            link(dve.memset(ss[:, :], 1.0))
            dve.wait_ge(s_x, 32)
            for t, n in enumerate(TILE_ROWS):
                link(dve.tensor_tensor_reduce(out=junk[0:n, :], in0=m.x[0:n, t, :], in1=m.x[0:n, t, :], scale=1.0,
                                              scalar=0.0, op0=ALU.mult, op1=ALU.add, accum_out=ss[0:n, t:t + 1]))
            dve.tensor_scalar(ss[:, :], ss[:, :], 1.0 / D, EPS, ALU.mult, ALU.add).then_inc(s_ms, 1)
            dve.wait_ge(s_sq, 1)
            link(dve.reciprocal(ss[:, :], ss[:, :]))
            for t, n in enumerate(TILE_ROWS):
                dve.tensor_scalar(xn[0:n, t, :], m.x[0:n, t, :], ss[0:n, t:t + 1], None, ALU.mult).then_inc(s_xn, 1)
            dve.wait_ge(s_tp, 1)
            link(dve.tensor_copy(pcol[:, :, :], m.bank[0][:, 0:KD * 12].rearrange("p (k r) -> p k r", r=12)))
            dve.tensor_copy(m.par[:, :, :], pcol[:, :, 0:7].rearrange("p k r -> p r k"))
            dve.tensor_copy(m.bias_feat[:, :].rearrange("p (r k) -> p r k", k=KD), pcol[:, :, 7:12].rearrange("p k r -> p r k"))
            for k in range(KD):
                dve.wait_ge(s_tp, 2 + k)
                dve.tensor_scalar(m.uT[:, k, :], m.bank[1 + k % 2][:, 0:NTOK], pcol[:, k, 6:7], None,
                                  ALU.mult).then_inc(s_ev, 1)

        @block.tensor
        def _(pe):
            pe.wait_ge(s_p, 160)
            for k in range(KD):
                last = pe.transpose(m.bank[0][:, k * 12:(k + 1) * 12], prow[:, k * 128:(k + 1) * 128], m.ident[0:12, 0:12])
            last.then_inc(s_tp, 1)
            pe.wait_ge(s_xn, NT)
            for k in range(KD):
                if k >= 2:
                    pe.wait_ge(s_ev, k - 1)
                for t, n in enumerate(TILE_ROWS):
                    last = pe.transpose(m.bank[1 + k % 2][:, t * 128:t * 128 + n], xn[0:n, t, k * 128:(k + 1) * 128],
                                        m.ident[0:n, 0:n])
                last.then_inc(s_tp, 1)


def project(nc, m, a):
    NCH = 8
    NSL = 4
    s_w = [m.sem(f"win_slot{i}") for i in range(NSL)]
    s_wg, s_pe = m.sem("wgate_in"), m.sem("proj_done")
    s_ev, s_pt, s_et = m.sem("proj_evicted"), m.sem("ptok_done"), m.sem("ptok_evicted")
    s_pg, s_sg, s_pq, s_eq = m.sem("pgate_done"), m.sem("sigmoid_gates"), m.sem("pq_done"), m.sem("pq_evicted")
    w_v = a.w_in[0].rearrange("(k p) n -> p k n", p=128)
    feat_off = [OFF_MX, OFF_MX + 512, OFF_MO, OFF_MO + 512] + [OFF_BG + 512 * i for i in range(4)]
    tok_cols = [(OFF_MV, 512, 0), (OFF_MV + 512, 512, 512), (OFF_NKV, 512, 1024), (OFF_NKV + 512, 304, 1536)]
    with ExitStack() as c:
        w = c.enter_context(nc.sbuf_tensor("w_slots", [128, NSL, KD, 512], FP))
        wg = c.enter_context(nc.sbuf_tensor("w_gates", [128, KD, 8], FP))
        block = c.enter_context(nc.Block())

        @block.sync
        def _(sp):
            sp.dma_start(wg[:, :, :], w_v[:, :, OFF_MI:OFF_NQ]).then_inc(s_wg, 16)
            loads = [(o, 512) for o in feat_off] + [(OFF_NQ, 512), (OFF_NQ + 512, 512)] + [(o, n) for o, n, _ in tok_cols]
            for i, (o, n) in enumerate(loads):
                before = i - NSL
                if before >= NCH:
                    sp.wait_ge(s_pq, KD)
                elif before >= 0:
                    sp.wait_ge(s_pe, 4 * (before + 1))
                sp.dma_start(w[:, i % NSL, :, 0:n], w_v[:, :, o:o + n]).then_inc(s_w[i % NSL], 16)

        @block.tensor
        def _(pe):
            pe.wait_ge(s_wg, 16)
            for r in range(2):
                for k in range(KD):
                    last = pe.matmul(m.bank[4 + r][0:MH, 0:NTOK], wg[:, k, MH * r:MH * (r + 1)], m.uT[:, k, :],
                                     start=(k == 0), stop=(k == KD - 1))
            last.then_inc(s_pg, 1)
            with pe.Fori(0, NCH // NSL) as i:
                for s in range(NSL):
                    pe.wait_ge(s_w[s], 16 * i + 16)
                    for j in range(4):
                        pe.wait_ge(s_ev, NSL * 4 * i + 4 * s + j + 1)
                        for k in range(KD):
                            last = pe.matmul(m.bank[j][:, 0:NTOK], w[:, s, k, j * 128:(j + 1) * 128], m.uT[:, k, :],
                                             start=(k == 0), stop=(k == KD - 1))
                        last.then_inc(s_pe, 1)
            for s in range(2):
                pe.wait_ge(s_w[s], 16 * 3)
            for j in range(KD):
                pe.wait_ge(s_ev, 4 + 32 - 3 + j) if j < 4 else pe.wait_ge(s_eq, j - 3)
                for g in range(2):
                    for k in range(KD):
                        last = pe.matmul(m.bank[j % 4][g * HD:(g + 1) * HD, 0:NTOK], w[:, g, k, j * HD:(j + 1) * HD],
                                         m.uT[:, k, :], start=(k == 0), stop=(k == KD - 1))
                last.then_inc(s_pq, 1)
            n = 0
            for i, (_, width, _) in enumerate(tok_cols):
                s = (10 + i) % NSL
                pe.wait_ge(s_w[s], 16 * (3 if i < 2 else 4))
                for t, rows in enumerate(TILE_ROWS):
                    pe.wait_ge(s_eq, n + 5) if n < 4 else pe.wait_ge(s_et, n - 3)
                    for k in range(KD):
                        last = pe.matmul(m.bank[n % 4][0:rows, 0:width], m.uT[:, k, t * 128:t * 128 + rows],
                                         w[:, s, k, 0:width], start=(k == 0), stop=(k == KD - 1))
                    last.then_inc(s_pt, 1)
                    n += 1

        @block.scalar
        def _(act):
            act.sem_inc(s_ev, 4)
            act.wait_ge(s_pg, 1)
            for r in range(2):
                act.activation(m.gate_rows[:, r, :], m.bank[4 + r][0:MH, 0:NTOK], ACT.Identity, bias=m.gate_bias[:, r:r + 1])
            with act.Fori(0, NCH) as i:
                for j in range(4):
                    act.wait_ge(s_pe, 4 * i + j + 1)
                    act.activation(m.zf[:, bass.ds(4 * i + j, 1), :], m.bank[j][:, 0:NTOK], ACT.Identity,
                                   bias=m.bias_feat[:, bass.ds(4 * i + j, 1)]).then_inc(s_ev, 1)
            for j in range(KD):
                act.wait_ge(s_pq, j + 1)
                act.activation(m.zf[:, 32 + j, :], m.bank[j % 4][:, 0:NTOK], ACT.Identity,
                               bias=m.bias_feat[:, 32 + j:33 + j]).then_inc(s_eq, 1)
            act.wait_ge(s_ev, 36)
            act.activation(m.zf[:, 8:32, :], m.zf[:, 8:32, :], ACT.Sigmoid)
            act.wait_ge(s_eq, 8)
            act.activation(m.zf[:, 32:40, :], m.zf[:, 32:40, :], ACT.Copy, scale=HD ** -0.5)
            act.wait_ge(s_et, 12)
            act.activation(m.ngate[:, 0:2, :], m.ngate[:, 0:2, :], ACT.Sigmoid)
            act.activation(m.ngate[0:64, 2, :], m.ngate[0:64, 2, :], ACT.Sigmoid)

        @block.vector
        def _(dve):
            dve.memset(m.v[:, :, :, DV:VX], 1.0)
            n = 0
            for i, (_, width, off) in enumerate(tok_cols):
                for t, rows in enumerate(TILE_ROWS):
                    dve.wait_ge(s_pt, n + 1)
                    ps = m.bank[n % 4]
                    bias = m.bias_tok[0:rows, off:off + width]
                    if i < 2:
                        dve.tensor_tensor(m.v[0:rows, t, 2 * i:2 * i + 2, 0:DV],
                                          ps[0:rows, 0:512].rearrange("p (h v) -> p h v", v=DV),
                                          bias.rearrange("p (h v) -> p h v", v=DV), ALU.add).then_inc(s_et, 1)
                    elif i == 2:
                        dve.tensor_tensor(m.kv[0:rows, t, 0:512], ps[0:rows, 0:512], bias, ALU.add).then_inc(s_et, 1)
                    else:
                        dve.tensor_tensor(m.kv[0:rows, t, 512:KVC], ps[0:rows, 0:256], bias[:, 0:256], ALU.add)
                        dve.tensor_tensor(m.ngate[0:rows, t, :], ps[0:rows, 256:304], bias[:, 256:304],
                                          ALU.add).then_inc(s_et, 1)
                    n += 1

def conv_silu(nc, m, a):
    s_in, s_tp, s_pad, s_last = m.sem("conv_state_in"), m.sem("conv_state_T"), m.sem("conv_padded"), m.sem("conv_last")
    s_lt, s_le, s_out = m.sem("conv_last_T"), m.sem("conv_last_ev"), m.sem("conv_out")
    s_chain, s_acc, s_sig, s_zero = m.sem("conv_dve"), m.sem("conv_acc"), m.sem("conv_sig"), m.sem("conv_zero")
    R = NB * 3
    with ExitStack() as c:
        state = c.enter_context(nc.sbuf_tensor("conv_state", [R, D], FP))
        xp = c.enter_context(nc.sbuf_tensor("conv_xp", [128, KD, SEQ + 3], FP))
        xs = c.enter_context(nc.sbuf_tensor("conv_xs", [128, KD, NB, TS + 3], FP))
        last3 = c.enter_context(nc.sbuf_tensor("conv_last3", [128, KD, R + 3], FP))
        rows = c.enter_context(nc.sbuf_tensor("conv_rows", [R + 3, D], FP))
        sig = c.enter_context(nc.sbuf_tensor("conv_sigm", [128, KD, NTOK], FP))
        block = c.enter_context(nc.Block())

        @block.sync
        def _(sp):
            sp.dma_start(state[:, :], a.state_conv[0].rearrange("b r d -> (b r) d")).then_inc(s_in, 16)
            sp.wait_ge(s_le, 2)
            sp.dma_start(a.new_conv_p[0, 0], rows[0:3, :]).then_inc(s_out, 16)
            sp.dma_start(a.new_conv_s[0].rearrange("b r d -> (b r) d"), rows[3:R + 3, :]).then_inc(s_out, 16)
            sp.wait_ge(s_out, 32)

        @block.tensor
        def _(pe):
            pe.wait_ge(s_in, 16)
            for k in range(KD):
                last = pe.transpose(m.bank[0][:, k * R:(k + 1) * R], state[:, k * 128:(k + 1) * 128], m.ident[0:R, 0:R])
            last.then_inc(s_tp, 1)
            pe.wait_ge(s_last, 1)
            for k in range(KD):
                last = pe.transpose(m.bank[1 + k // 4][0:R + 3, (k % 4) * 128:(k % 4 + 1) * 128], last3[:, k, :], m.ident[:, :])
                if k % 4 == 3:
                    last.then_inc(s_lt, 1)

        @block.gpsimd
        def _(pool):
            pool.memset(xp[:, :, 0:3], 0.0)
            pool.tensor_copy(xp[:, :, 3:], m.zf[:, 0:KD, 0:SEQ]).then_inc(s_zero, 1)

        @block.vector
        def _(dve):
            link = Link(dve, s_chain)
            link.go(dve.tensor_copy(xs[:, :, :, 3:], m.zf[:, 0:KD, SEQ:].rearrange("p k (b t) -> p k b t", t=TS)))
            dve.wait_ge(s_tp, 1)
            link(dve.tensor_copy(xs[:, :, :, 0:3], m.bank[0][:, 0:KD * R].rearrange("p (k b r) -> p k b r", b=NB, r=3)))
            dve.wait_ge(s_zero, 1)
            link.go(dve.tensor_copy(last3[:, :, 0:3], xp[:, :, SEQ:SEQ + 3]))
            link(dve.tensor_copy(last3[:, :, 3:].rearrange("p k (b r) -> p k b r", r=3), xs[:, :, :, TS:TS + 3]))
            dve.sem_inc(s_last, 1)
            with dve.Fori(0, KD) as k:
                link.loop(k, 8)
                w = [m.par[:, j, bass.ds(k, 1)] for j in range(5)]
                yp = m.xc[:, bass.ds(k, 1), 0:SEQ]
                ys = m.xc[:, bass.ds(k, 1), SEQ:].rearrange("p k (b t) -> p (k b) t", t=TS)
                for j in range(4):
                    inp = xp[:, bass.ds(k, 1), j:j + SEQ]
                    ins = xs[:, bass.ds(k, 1), :, j:j + TS].rearrange("p k b t -> p (k b) t")
                    if j == 0:
                        link.go(dve.tensor_scalar(yp, inp, w[0], w[4], ALU.mult, ALU.add))
                        link(dve.tensor_scalar(ys, ins, w[0], w[4], ALU.mult, ALU.add))
                    else:
                        link.go(dve.scalar_tensor_tensor(yp, inp, w[j], yp, ALU.mult, ALU.add))
                        link(dve.scalar_tensor_tensor(ys, ins, w[j], ys, ALU.mult, ALU.add))
            link.done(KD)
            dve.sem_inc(s_acc, 1)
            for i in range(2):
                dve.wait_ge(s_lt, i + 1)
                dve.tensor_copy(rows[:, i * 512:(i + 1) * 512], m.bank[1 + i][0:R + 3, :]).then_inc(s_le, 1)
            dve.wait_ge(s_sig, 1)
            dve.tensor_tensor(m.xc[:, :, :], m.xc[:, :, :], sig[:, :, :], ALU.mult)

        @block.scalar
        def _(act):
            act.wait_ge(s_acc, 1)
            act.activation(sig[:, :, :], m.xc[:, :, :], ACT.Sigmoid).then_inc(s_sig, 1)


def mlstm_gates(nc, m, a):
    s_w, s_m0, s_qk, s_ev = m.sem("wqk_in"), m.sem("m0_in"), m.sem("qk_done"), m.sem("qk_evicted")
    s_abs, s_e, s_ln, s_lf = m.sem("g_abs"), m.sem("g_exp"), m.sem("g_ln"), m.sem("g_dve")
    s_mt, s_wi, s_we, s_cols = m.sem("g_mt"), m.sem("g_winter"), m.sem("g_wend"), m.sem("g_cols_T")
    s_mo, s_out, s_dec = m.sem("g_mout"), m.sem("g_m_stored"), m.sem("g_decay")
    with ExitStack() as c:
        wq = c.enter_context(nc.sbuf_tensor("wq", [128, 2 * MH, DQK], FP))
        wk = c.enter_context(nc.sbuf_tensor("wk", [128, 2 * MH, DQK], FP))
        lf = c.enter_context(nc.sbuf_tensor("g_lf", [MH, NTOK], FP))
        t0 = c.enter_context(nc.sbuf_tensor("g_t0", [MH, NTOK], FP))
        t1 = c.enter_context(nc.sbuf_tensor("g_t1", [MH, NTOK], FP))
        bsum = c.enter_context(nc.sbuf_tensor("g_b", [MH, NTOK], FP))
        mrow = c.enter_context(nc.sbuf_tensor("g_m", [MH, NTOK], FP))
        m0 = c.enter_context(nc.sbuf_tensor("g_m0", [MH, NTOK], FP))
        m0s = c.enter_context(nc.sbuf_tensor("g_m0s", [MH, NB], FP))
        mt = c.enter_context(nc.sbuf_tensor("g_mtrow", [MH, NTOK], FP))
        wa = c.enter_context(nc.sbuf_tensor("g_wa", [MH, 64], FP))
        we = c.enter_context(nc.sbuf_tensor("g_we", [MH, 64], FP))
        crow = c.enter_context(nc.sbuf_tensor("g_crow", [MH, 3, NTOK], FP))
        mout = c.enter_context(nc.sbuf_tensor("g_mo", [MH, 1 + NB], FP))
        block = c.enter_context(nc.Block())
        r = crow[:, 0, :]

        @block.sync
        def _(sp):
            sp.dma_start(wq[:, :, :], a.w_mq[0].rearrange("h (c p) d -> p (h c) d", p=128)).then_inc(s_w, 16)
            sp.dma_start(wk[:, :, :], a.w_mk[0].rearrange("h (c p) d -> p (h c) d", p=128)).then_inc(s_w, 16)
            sp.dma_start(m0s[:, :], a.state_m[0].rearrange("b h -> h b"), allow_slow_non_contiguous=True).then_inc(s_m0, 16)
            sp.wait_ge(s_mo, 1)
            sp.dma_start(a.new_m_p[0].rearrange("b h -> h b"), mout[:, 0:1], allow_slow_non_contiguous=True).then_inc(s_out, 16)
            sp.dma_start(a.new_m_s[0].rearrange("b h -> h b"), mout[:, 1:], allow_slow_non_contiguous=True).then_inc(s_out, 16)
            sp.wait_ge(s_out, 32)

        @block.tensor
        def _(pe):
            pe.wait_ge(s_w, 32)
            for h in range(MH):
                pe.wait_ge(s_ev, 3 * h + 1)
                for i in range(2):
                    last = pe.matmul(m.bank[0][:, 0:NTOK], wq[:, bass.ds(2 * h + i, 1), :], m.xc[:, bass.ds(2 * h + i, 1), :],
                                     start=(i == 0), stop=(i == 1))
                last.then_inc(s_qk, 1)
                pe.wait_ge(s_ev, 3 * h + 2)
                for i in range(2):
                    last = pe.matmul(m.bank[1][:, 0:NTOK], wk[:, bass.ds(2 * h + i, 1), :], m.xc[:, bass.ds(2 * h + i, 1), :],
                                     start=(i == 0), stop=(i == 1))
                last.then_inc(s_qk, 1)
                pe.wait_ge(s_ev, 3 * h + 3)
                for t, n in enumerate(TILE_ROWS):
                    for i in range(2):
                        last = pe.matmul(m.bank[2][0:n, t * 128:(t + 1) * 128], m.xc[:, bass.ds(2 * h + i, 1), t * 128:t * 128 + n],
                                         wk[:, bass.ds(2 * h + i, 1), :], start=(i == 0), stop=(i == 1))
                last.then_inc(s_qk, 1)
            pe.wait_ge(s_we, 2)
            pe.wait_ge(s_e, 2)
            for t, n in enumerate(TILE_ROWS):
                for q in range(3):
                    last = pe.transpose(m.bank[3][0:n, (t * 3 + q) * MH:(t * 3 + q + 1) * MH],
                                        crow[:, q, t * 128:t * 128 + n], m.ident[0:MH, 0:MH])
            last.then_inc(s_cols, 1)

        @block.scalar
        def _(act):
            act.sem_inc(s_ev, 3)
            act.activation(t0[:, :], m.gate_rows[:, 1, :], ACT.Abs).then_inc(s_abs, 1)
            act.wait_ge(s_abs, 1)
            act.activation(t0[:, :], t0[:, :], ACT.Exp, scale=-1.0).then_inc(s_e, 1)
            act.wait_ge(s_e, 1)
            act.activation(t1[:, :], t0[:, :], ACT.Ln, bias=1.0).then_inc(s_ln, 1)
            act.wait_ge(s_mt, 1)
            act.activation(crow[:, 1, :], mt[:, :], ACT.Exp, scale=-1.0).then_inc(s_e, 1)
            act.activation(m.grow[:, NTOK:NTOK + 64], wa[:, :], ACT.Exp).then_inc(s_wi, 1)
            act.activation(crow[:, 2, 0:SEQ], r[:, 0:SEQ], ACT.Exp, bias=m.grow[:, SEQ - 1:SEQ]).then_inc(s_we, 1)
            act.activation(crow[:, 2, SEQ:], we[:, :], ACT.Exp).then_inc(s_we, 1)
            for h in range(MH):
                act.wait_ge(s_qk, 3 * h + 1)
                act.activation(m.mqT[:, bass.ds(h, 1), :], m.bank[0][:, 0:NTOK], ACT.Copy).then_inc(s_ev, 1)
                act.wait_ge(s_qk, 3 * h + 2)
                act.activation(m.mkT[:, bass.ds(h, 1), :], m.bank[1][:, 0:NTOK], ACT.Copy, scale=DQK ** -0.5).then_inc(s_ev, 1)
                act.wait_ge(s_qk, 3 * h + 3)
                act.activation(m.mk[:, bass.ds(h, 1), 0:2 * DQK], m.bank[2][:, 0:2 * DQK], ACT.Copy, scale=DQK ** -0.5)
                act.activation(m.mk[0:64, bass.ds(h, 1), 2 * DQK:], m.bank[2][0:64, 2 * DQK:3 * DQK], ACT.Copy,
                               scale=DQK ** -0.5).then_inc(s_ev, 1)

        @block.vector
        def _(dve):
            link = Link(dve, s_lf)
            link(dve.memset(m0[:, 0:SEQ], 0.0))
            dve.wait_ge(s_m0, 16)
            link(dve.tensor_copy(m0[:, SEQ:].rearrange("p (b t) -> p b t", t=TS), m0s[:, :].unsqueeze(2).to_broadcast((MH, NB, TS))))
            dve.wait_ge(s_ln, 1)
            link(dve.scalar_tensor_tensor(lf[:, :], m.gate_rows[:, 1, :], 0.0, t1[:, :], ALU.min, ALU.subtract))
            link(dve.tensor_tensor_scan(bsum[:, :], m.seg_mul[:, :], lf[:, :], 0.0, ALU.mult, ALU.add))
            link(dve.tensor_tensor(r, m.gate_rows[:, 0, :], bsum[:, :], ALU.subtract))
            link(dve.tensor_tensor_scan(mrow[:, :], m.seg_add[:, :], r, NEG, ALU.add, ALU.max))
            link(dve.tensor_tensor(mrow[:, :], mrow[:, :], m0[:, :], ALU.max))
            link(dve.tensor_scalar(m.grow[:, 0:NTOK], mrow[:, :], -1.0, None, ALU.mult))
            link(dve.tensor_tensor(mt[:, :], bsum[:, :], mrow[:, :], ALU.add))
            link(dve.tensor_tensor(wa[:, :], m0[:, SEQ:], mrow[:, SEQ:], ALU.subtract))
            negm_end = m.grow[:, SEQ:NTOK].rearrange("p (b t) -> p b t", t=TS)[:, :, TS - 1:TS]
            link(dve.tensor_tensor(we[:, :].rearrange("p (b t) -> p b t", t=TS), r[:, SEQ:].rearrange("p (b t) -> p b t", t=TS),
                                   negm_end.to_broadcast((MH, NB, TS)), ALU.add))
            dve.sem_inc(s_mt, 1)
            link.go(dve.tensor_copy(mout[:, 0:1], mt[:, SEQ - 1:SEQ]))
            link(dve.tensor_copy(mout[:, 1:].unsqueeze(2), mt[:, SEQ:].rearrange("p (b t) -> p b t", t=TS)[:, :, TS - 1:TS]))
            dve.sem_inc(s_mo, 1)
            dve.wait_ge(s_wi, 1)
            dve.tensor_copy(m.grow[:, NTOK + 64:NTOK + 64 + NB].unsqueeze(2),
                            m.grow[:, NTOK:NTOK + 64].rearrange("p (b t) -> p b t", t=TS)[:, :, TS - 1:TS])
            dve.wait_ge(s_cols, 1)
            dve.tensor_copy(m.gcol[:, 0:2, :, :], m.bank[3][:, 0:24].rearrange("p (t q h) -> p t q h", q=3, h=MH))
            dve.tensor_copy(m.gcol[0:64, 2, :, :], m.bank[3][0:64, 24:36].rearrange("p (q h) -> p q h", h=MH))


def mlstm_heads(nc, m, a):
    s_c0, s_n0, s_nT, s_n0e = m.sem("C0_in"), m.sem("n0_in"), m.sem("n0_T"), m.sem("n0_ev")
    s_nb, s_s, s_arg, s_w = m.sem("bcast_done"), m.sem("qk_scores"), m.sem("warg"), m.sem("wexp")
    s_nbf, s_pt, s_kw, s_num = m.sem("bcast_read"), m.sem("pt_ready"), m.sem("kw_ready"), m.sem("num_done")
    s_cp, s_cpe, s_cs, s_cse = m.sem("Cp_done"), m.sem("Cp_evicted"), m.sem("Cs_done"), m.sem("Cs_evicted")
    s_h, s_sq, s_numf, s_chain = m.sem("h_ready"), m.sem("h_sq"), m.sem("num_read"), m.sem("heads_dve")
    s_out, s_qm, s_rt, s_hn = m.sem("C_out"), m.sem("qm_zero"), m.sem("hrms_sqrt"), m.sem("hn_ready")
    s_hT, s_hTe, s_rs, s_nc, s_nct, s_nce = (m.sem("hT"), m.sem("hT_ev"), m.sem("hrms_ms"), m.sem("ncol"),
                                             m.sem("ncol_T"), m.sem("ncol_ev"))
    QW = 136
    with ExitStack() as c:
        def sb(name, shape):
            return c.enter_context(nc.sbuf_tensor(name, shape, FP))

        ce = sb("state_ce", [128, NB, MH, VX])
        cp = sb("prompt_c", [128, MH, VX])
        n0 = sb("n0_rows", [NB * MH, DQK])
        ncol = sb("ncols", [128, MH + NB * MH])
        nrow = sb("nrows", [MH + NB * MH, DQK])
        wi = sb("w_intra", [128, 3 * 128])
        wis = sb("w_intra_s", [64, 64])
        pt = sb("pt", [128, 3 * 128])
        pts = sb("pt_s", [64, 128])
        qm = sb("qm", [128, NB * QW])
        dec = sb("decay", [128, NB])
        kw = sb("kw", [128, 2, DQK])
        wem = sb("wend_m", [64, NB])
        kws = sb("kw_s", [64, NB, DQK])
        den = sb("den", [128, NT])
        ht = sb("h_tok", [128, NT, MH, DV])
        junk = sb("h_junk", [128, DV])
        ss = sb("h_ss", [128, NT, MH])
        block = c.enter_context(nc.Block())

        @block.sync
        def _(sp):
            sp.dma_start(n0[:, :], a.state_n[0].rearrange("b h d -> (b h) d")).then_inc(s_n0, 16)
            for b in range(NB):
                sp.dma_start(ce[:, b, :, 0:DV], a.state_C[0, b].rearrange("h d v -> d h v")).then_inc(s_c0, 16)
            for h in range(MH):
                sp.wait_ge(s_cpe, h + 2)
                sp.dma_start(a.new_C_p[0, 0, h], cp[:, h, 0:DV]).then_inc(s_out, 16)
                sp.wait_ge(s_cse, 2 + NB * (h + 1))
                sp.dma_start(a.new_C_s[0, :, h].rearrange("b d v -> d b v"), ce[:, :, h, 0:DV]).then_inc(s_out, 16)
            sp.wait_ge(s_nce, 1)
            sp.dma_start(a.new_n_p[0, 0], nrow[0:MH, :]).then_inc(s_out, 16)
            sp.dma_start(a.new_n_s[0].rearrange("b h d -> (b h) d"), nrow[MH:, :]).then_inc(s_out, 16)
            sp.wait_ge(s_out, 16 * (2 * MH + 2))

        @block.tensor
        def _(pe):
            pe.wait_ge(s_n0, 16)
            pe.transpose(m.bank[5][:, 0:NB * MH], n0[:, :], m.ident[0:NB * MH, 0:NB * MH]).then_inc(s_nT, 1)
            pe.wait_ge(s_n0e, 1)
            pe.wait_ge(s_c0, 16 * NB)
            pe.wait_ge(s_qm, 1)
            for h in range(MH):
                v = [m.v[0:n, t, bass.ds(h, 1), :] for t, n in enumerate(TILE_ROWS)]
                pe.wait_ge(s_nbf, h + 1)
                pe.matmul(m.bank[0][:, 0:392], m.ident[0:MH, bass.ds(h, 1)].to_broadcast((MH, 128)), m.grow[:, :],
                          start=True, stop=True).then_inc(s_nb, 1)
                pe.wait_ge(s_pt, h + 1)
                for o, k0, kn, q0, qn in ((0, 0, 128, 0, 256), (256, 128, 128, 128, 128), (384, 256, 64, 256, 64)):
                    last = pe.matmul(m.bank[1][0:kn, o:o + qn], m.mkT[:, bass.ds(h, 1), k0:k0 + kn],
                                     m.mqT[:, bass.ds(h, 1), q0:q0 + qn], start=True, stop=True)
                last.then_inc(s_s, 1)
                pe.wait_ge(s_pt, h + 2)
                pe.wait_ge(s_numf, 3 * h + 3)
                pe.matmul(m.bank[2][:, 0:VX], pt[:, 0:128], v[0], start=True, stop=True).then_inc(s_num, 1)
                pe.matmul(m.bank[3][:, 0:VX], pt[:, 128:256], v[0], start=True, stop=False)
                pe.matmul(m.bank[3][:, 0:VX], pt[:, 256:384], v[1], start=False, stop=True).then_inc(s_num, 1)
                pe.matmul(m.bank[4][:, 0:VX], pts[:, :], v[2], start=True, stop=False)
                for b in range(NB):
                    last = pe.matmul(m.bank[4][:, 0:VX], qm[:, 128 * b:128 * b + 128], ce[:, b, bass.ds(h, 1), :],
                                     start=False, stop=(b == NB - 1))
                last.then_inc(s_num, 1)
                pe.wait_ge(s_kw, h + 1)
                pe.wait_ge(s_cpe, h + 1)
                for t in range(2):
                    last = pe.matmul(m.bank[5][:, 0:VX], kw[:, t, :], v[t], start=(t == 0), stop=(t == 1))
                last.then_inc(s_cp, 1)
                for b in range(NB):
                    pe.wait_ge(s_cse, NB * h + b + 1)
                    pe.matmul(m.bank[6 + b % 2][:, 0:VX], kws[:, b, :], v[2], start=True, stop=True).then_inc(s_cs, 1)
            pe.wait_ge(s_nc, 1)
            pe.transpose(m.bank[0][0:MH + NB * MH, 0:128], ncol[:, :], m.ident[:, :]).then_inc(s_nct, 1)
            pe.wait_ge(s_hn, 1)
            for k in range(KD):
                if k >= 2:
                    pe.wait_ge(s_hTe, k - 1)
                for t, n in enumerate(TILE_ROWS):
                    last = pe.transpose(m.bank[2 + k % 2][:, t * 128:t * 128 + n],
                                        ht[0:n, t, k // 2, (k % 2) * 128:(k % 2 + 1) * 128], m.ident[0:n, 0:n])
                last.then_inc(s_hT, 1)

        @block.scalar
        def _(act):
            act.sem_inc(s_cpe, 1)
            act.wait_ge(s_nT, 1)
            act.activation(ce[:, :, :, DV:VX].rearrange("p b h o -> p (b h) o"), m.bank[5][:, 0:NB * MH].unsqueeze(2),
                           ACT.Copy).then_inc(s_n0e, 1)
            for h in range(MH):
                act.wait_ge(s_arg, h + 1)
                act.activation(wi[:, :], wi[:, :], ACT.Exp)
                act.activation(wis[:, :], wis[:, :], ACT.Exp).then_inc(s_w, 1)
                act.wait_ge(s_cp, h + 1)
                act.activation(cp[:, bass.ds(h, 1), :], m.bank[5][:, 0:VX], ACT.Copy)
                act.activation(ncol[:, bass.ds(h, 1)], m.bank[5][:, DV:VX], ACT.Copy).then_inc(s_cpe, 1)
                act.wait_ge(s_h, h + 1)
                for t, n in enumerate(TILE_ROWS):
                    if h + t > 0:
                        act.wait_ge(s_sq, NT * h + t)
                    act.activation(junk[0:n, :], ht[0:n, t, bass.ds(h, 1), :], ACT.Square,
                                   accum_out=ss[0:n, t, bass.ds(h, 1)]).then_inc(s_sq, 1)
            act.wait_ge(s_rs, 1)
            act.activation(ss[:, :, :], ss[:, :, :], ACT.Sqrt).then_inc(s_rt, 1)

        @block.vector
        def _(dve):
            link = Link(dve, s_chain)
            dve.sem_inc(s_nbf, 1)
            dve.sem_inc(s_numf, 3)
            dve.sem_inc(s_pt, 1)
            dve.sem_inc(s_cse, 2)
            link.go(dve.memset(ss[:, :, :], 1.0))
            link.go(dve.memset(pts[:, :], 0.0))
            link(dve.memset(qm[:, :], 0.0))
            dve.sem_inc(s_qm, 1)
            for h in range(MH):
                link.loop(h, 25 + NB)
                col = lambda n, t, q: m.gcol[0:n, t, q, bass.ds(h, 1)]
                link(dve.tensor_scalar(wem[:, :], m.seq_onehot[:, :], col(64, 2, 2), None, ALU.mult))
                dve.wait_ge(s_cpe, h + 1)
                for t in range(2):
                    link.go(dve.tensor_scalar(kw[:, t, :], m.mk[:, bass.ds(h, 1), t * DQK:(t + 1) * DQK], col(128, t, 2), None, ALU.mult))
                link(dve.tensor_tensor(kws[:, :, :], m.mk[0:64, bass.ds(h, 1), 2 * DQK:].to_broadcast((64, NB, DQK)),
                                       wem[:, :].unsqueeze(2).to_broadcast((64, NB, DQK)), ALU.mult))
                dve.sem_inc(s_kw, 1)
                dve.wait_ge(s_nb, h + 1)
                nb = m.bank[0]
                link.go(dve.scalar_tensor_tensor(wi[:, 0:128], nb[:, 0:128], col(128, 0, 0), m.causal_st[:, :], ALU.add, ALU.add))
                link.go(dve.tensor_scalar(wi[:, 128:256], nb[:, 128:256], col(128, 0, 0), None, ALU.add))
                link.go(dve.scalar_tensor_tensor(wi[:, 256:384], nb[:, 128:256], col(128, 1, 0), m.causal_st[:, :], ALU.add, ALU.add))
                link(dve.scalar_tensor_tensor(wis[:, :], nb[0:64, 256:320], col(64, 2, 0), m.same_seq[:, :], ALU.add, ALU.add))
                dve.sem_inc(s_arg, 1)
                link.go(dve.tensor_tensor(qm[:, :].rearrange("p (b x) -> p b x", x=QW)[:, :, 0:TS],
                                          m.mqT[:, bass.ds(h, 1), SEQ:].rearrange("p h (b t) -> p (h b) t", t=TS),
                                          nb[:, NTOK:NTOK + 64].rearrange("p (b t) -> p b t", t=TS), ALU.mult))
                link(dve.tensor_copy(dec[:, :], nb[:, NTOK + 64:NTOK + 64 + NB]))
                dve.sem_inc(s_nbf, 1)
                dve.wait_ge(s_w, h + 1)
                dve.wait_ge(s_s, h + 1)
                link.go(dve.tensor_tensor(pt[:, :], m.bank[1][:, 0:384], wi[:, :], ALU.mult))
                link(dve.tensor_tensor(pts[:, 0:64], m.bank[1][0:64, 384:448], wis[:, :], ALU.mult))
                dve.sem_inc(s_pt, 1)
                for t, n in enumerate(TILE_ROWS):
                    dve.wait_ge(s_num, 3 * h + t + 1)
                    ps = m.bank[2 + t]
                    link(dve.scalar_tensor_tensor(den[0:n, t:t + 1], ps[0:n, DV:VX], -1.0, col(n, t, 1), ALU.mult, ALU.max))
                    link(dve.tensor_tensor(den[0:n, t:t + 1], ps[0:n, DV:VX], den[0:n, t:t + 1], ALU.max))
                    link(dve.reciprocal(den[0:n, t:t + 1], den[0:n, t:t + 1]))
                    link(dve.tensor_scalar(ht[0:n, t, bass.ds(h, 1), :], ps[0:n, 0:DV], den[0:n, t:t + 1], None, ALU.mult))
                    dve.sem_inc(s_numf, 1)
                dve.sem_inc(s_h, 1)
                for b in range(NB):
                    dve.wait_ge(s_cs, NB * h + b + 1)
                    st = ce[:, b, bass.ds(h, 1), :]
                    link(dve.scalar_tensor_tensor(st, st, dec[:, b:b + 1], m.bank[6 + b % 2][:, 0:VX], ALU.mult, ALU.add))
                    dve.sem_inc(s_cse, 1)
                link.go(dve.tensor_copy(ncol[:, MH:].rearrange("p (b h) -> p b h", h=MH)[:, :, bass.ds(h, 1)],
                                        ce[:, :, bass.ds(h, 1), DV:VX].rearrange("p b h o -> p b (h o)")))
            link.done(MH)
            link.wait()
            dve.wait_ge(s_cpe, MH + 1)
            dve.sem_inc(s_nc, 1)
            dve.wait_ge(s_sq, 3 * MH)
            link(dve.tensor_scalar(ss[:, :, :], ss[:, :, :], 1.0 / DV, EPS, ALU.mult, ALU.add))
            dve.sem_inc(s_rs, 1)
            dve.wait_ge(s_rt, 1)
            link(dve.reciprocal(ss[:, :, :], ss[:, :, :]))
            for t, n in enumerate(TILE_ROWS):
                for h in range(MH):
                    link.go(dve.tensor_scalar(ht[0:n, t, h, :], ht[0:n, t, h, :], ss[0:n, t, h:h + 1], None, ALU.mult))
            link.wait()
            dve.sem_inc(s_hn, 1)
            dve.wait_ge(s_nct, 1)
            dve.tensor_copy(nrow[:, :], m.bank[0][0:MH + NB * MH, 0:128]).then_inc(s_nce, 1)
            for k in range(KD):
                dve.wait_ge(s_hT, k + 1)
                dve.scalar_tensor_tensor(m.hmT[:, k, :], m.bank[2 + k % 2][:, 0:NTOK], m.par[:, 5, k:k + 1],
                                         m.zf[:, KD + k, :], ALU.mult, ALU.mult).then_inc(s_hTe, 1)


def nsa_prepare(nc, m, a):
    s_w, s_z, s_b, s_g1, s_g2 = m.sem("wcmp_in"), m.sem("wcmp_zero"), m.sem("bcmp_in"), m.sem("gate_out"), m.sem("gate_in")
    s_t, s_te, s_c, s_ce, s_ct, s_cte = (m.sem("kT_done"), m.sem("kT_ev"), m.sem("cmpp_done"), m.sem("cmpp_ev"),
                                         m.sem("cvp_T"), m.sem("cvp_ev"))
    s_out, s_pt = m.sem("kv_out"), m.sem("pages_in")
    gates = nc.dram_tensor("gates_scratch", (NB * TS, 48), FP).ap()
    with ExitStack() as c:
        ccp = c.enter_context(nc.sbuf_tensor("ccp", [128, 2, NC_P], FP))
        block = c.enter_context(nc.Block())

        @block.sync
        def _(sp):
            sp.dma_start(gates, m.ngate[0:64, 2, :]).then_inc(s_g1, 16)
            sp.wait_ge(s_g1, 16)
            for h in range(16):
                sp.dma_start(m.gate_s[h * TS:(h + 1) * TS, :, :],
                             gates.rearrange("(b t) (h r) -> h t b r", t=TS, r=3)[h]).then_inc(s_g2, 16)
            sp.wait_ge(s_g2, 256)

        @block.scalar
        def _(act):
            for g in range(2):
                act.dma_start(m.bcmp[g * HD:(g + 1) * HD, :], a.b_cmp[0].rearrange("c e -> e c"),
                              allow_slow_non_contiguous=True).then_inc(s_b, 16)
            act.wait_ge(s_z, 2)
            for g in range(2):
                for i in range(2):
                    act.dma_start(m.wc[g * HD:(g + 1) * HD, i * CMP:(i + 1) * CMP, g * HD:(g + 1) * HD],
                                  a.w_cmp[0, i].rearrange("r d e -> d r e")).then_inc(s_w, 16)
            for g in range(2):
                act.dma_start(m.bcmp_row[0:1, :].rearrange("p (c g e) -> p g c e", c=2, g=2)[:, g],
                              a.b_cmp.rearrange("l c e -> l c e")).then_inc(s_b, 16)
            act.dma_start(m.pages[:, :], a.page_table.rearrange("(o b) n -> o (b n)", o=1)).then_inc(s_pt, 16)
            kvp = a.new_kv_p.rearrange("o (t p) l c g d -> t p (o l c g d)", p=128)
            wnp = a.new_win_p.rearrange("l o (t p) c g d -> t p (l o c g d)", p=128)
            for t in range(2):
                act.dma_start(kvp[t], m.kv[:, t, 0:512]).then_inc(s_out, 16)
                act.dma_start(wnp[t], m.kv[:, t, 512:KVC]).then_inc(s_out, 16)
            act.dma_start(a.new_kv_s.rearrange("b t l c g d -> (b t) (l c g d)"), m.kv[0:64, 2, 0:512]).then_inc(s_out, 16)
            nws = a.new_win_s[0].rearrange("b w c g d -> b w (c g d)")
            act.dma_start(nws[:, 0:WIN - TS, :], a.cache_win_kv[0].rearrange("b w c g d -> b w (c g d)")[:, TS:, :]).then_inc(s_out, 16)
            for b in range(NB):
                act.dma_start(nws[b, WIN - TS:, :], m.kv[b * TS:(b + 1) * TS, 2, 512:KVC]).then_inc(s_out, 16)
            act.wait_ge(s_out, 16 * (6 + NB))
            act.wait_ge(s_pt, 16)
            act.wait_ge(s_b, 64)
            for i in range(2):
                act.wait_ge(s_c, i + 1)
                act.activation(ccp[:, i, :], m.bank[4 + i][:, 0:NC_P], ACT.Identity, bias=m.bcmp[:, i:i + 1]).then_inc(s_ce, 1)
            act.wait_ge(s_ce, 2)
            act.activation(m.ckp[:, :], ccp[:, 0, :], ACT.Copy)
            act.wait_ge(s_ct, 1)
            act.activation(m.cvp[:, :], m.bank[6][0:NC_P, 0:128], ACT.Copy)

        @block.tensor
        def _(pe):
            for i, off in enumerate((0, 128, 256, 512)):
                for t, n in enumerate(TILE_ROWS):
                    last = pe.transpose(m.bank[i][:, t * 128:t * 128 + n], m.kv[0:n, t, off:off + 128], m.ident[0:n, 0:n])
                last.then_inc(s_t, 1)
            pe.wait_ge(s_te, 4)
            pe.wait_ge(s_w, 64)
            for i in range(2):
                for r in range(CMP):
                    last = pe.matmul(m.bank[4 + i][:, 0:NC_P], m.wc[:, i * CMP + r, :],
                                     m.kT[:, i, r:r + CST * (NC_P - 1) + 1:CST], start=(r == 0), stop=(r == CMP - 1))
                last.then_inc(s_c, 1)
            pe.wait_ge(s_ce, 2)
            pe.transpose(m.bank[6][0:NC_P, 0:128], ccp[:, 1, :], m.ident[:, :]).then_inc(s_ct, 1)

        @block.vector
        def _(dve):
            for i in range(4):
                dve.wait_ge(s_t, i + 1)
                dve.tensor_copy(m.kT[:, i, :], m.bank[i][:, 0:NTOK]).then_inc(s_te, 1)

        @block.gpsimd
        def _(pool):
            pool.memset(m.wc[:, :, :], 0.0).then_inc(s_z, 1)
            pool.memset(m.bcmp_row[:, :], 0.0).then_inc(s_z, 1)
            pool.memset(m.qbd[:, :], 0.0)
            pool.memset(m.key_mask[:, 0:128], 0.0)
            pool.tensor_copy(m.key_mask[:, 128:256], m.causal_tk[:, :])


def nsa_prompt(nc, m, a):
    s_q, s_sc, s_msk = m.sem("np_q"), m.sem("np_scores"), m.sem("np_masked")
    s_nm, s_ex, s_dg, s_tp = m.sem("np_negmax"), m.sem("np_exp"), m.sem("np_diag"), m.sem("np_T")
    s_ea, s_ed, s_pv, s_oe = m.sem("np_ev_act"), m.sem("np_ev_dve"), m.sem("np_pv"), m.sem("np_out")
    s_chain = m.sem("np_dve")
    FIRST, PER = 7, 18
    with ExitStack() as c:
        def sb(name, shape):
            return c.enter_context(nc.sbuf_tensor(name, shape, FP))

        qs = sb("np_qs", [128, 128])
        s = [sb(f"np_s{p}", [128, 2, 2, SEQ]) for p in range(2)]
        sc = [sb(f"np_sc{p}", [128, 2, NC_P]) for p in range(2)]
        mx = [sb(f"np_mx{p}", [128, 6]) for p in range(2)]
        sm = [sb(f"np_sm{p}", [128, 6]) for p in range(2)]
        dg = sb("np_dg", [128, 6, 128])
        pt = sb("np_pt", [128, 2, 512])
        ptc = sb("np_ptc", [NC_P, 2, 128])
        block = c.enter_context(nc.Block())

        def turns(eng, turn):
            for T in range(2):
                with eng.Fori(0, 3) as i:
                    for p in range(2):
                        turn((T, 2 * i + p, p, 2 * i + (8 * T + p)), (T, 2 * i + (p + 1), 1 - p, 2 * i + (8 * T + p + 1)))
                turn((T, 6, 0, 8 * T + 6), (T, 7, 1, 8 * T + 7))
                turn((T, 7, 1, 8 * T + 7), (1, 0, 0, 8) if T == 0 else None)

        first = (0, 0, 0, 0)

        @block.gpsimd
        def _(pool):
            def queries(T, u, p, U):
                pool.tensor_copy(qs[:, :], m.zf[:, bass.ds(u + 32, 1), T * 128:(T + 1) * 128]).then_inc(s_q, 1)

            def turn(this, after):
                if after:
                    pool.wait_ge(s_sc, this[3] + 1)
                    queries(*after)
            queries(*first)
            turns(pool, turn)

        @block.tensor
        def _(pe):
            def scores(T, u, p, U):
                nk = 128 * (T + 1)
                pe.wait_ge(s_q, U + 1)
                if not isinstance(U, int) or U > 0:
                    pe.wait_ge(s_msk, U)
                for g in range(2):
                    q = qs[g * HD:(g + 1) * HD, :]
                    for i, kind in enumerate((2, 3)):
                        pe.matmul(m.bank[g][:, i * nk:(i + 1) * nk], q, m.kT[g * HD:(g + 1) * HD, kind, 0:nk],
                                  start=True, stop=True)
                    last = pe.matmul(m.bank[(2, 7)[g]][:, 0:NC_P], q, m.ckp[g * HD:(g + 1) * HD, :],
                                     start=True, stop=True)
                last.then_inc(s_sc, 1)

            def turn(this, after):
                T, u, p, U = this
                if after:
                    scores(*after)
                pe.wait_ge(s_dg, U + 1)
                pe.wait_ge(s_ea, U + 1)
                pe.wait_ge(s_ed, U + 1)
                for g in range(2):
                    for br in range(2):
                        for ch in range(T + 1):
                            o = (br * (T + 1) + ch) * 128
                            pe.matmul(m.bank[3 + g][:, o:o + 128], s[p][:, g, br, ch * 128:(ch + 1) * 128],
                                      dg[:, 2 * g + br, :], start=True, stop=True)
                    last = pe.matmul(m.bank[5][0:NC_P, g * 128:(g + 1) * 128], sc[p][:, g, :], dg[:, 4 + g, :],
                                     start=True, stop=True)
                last.then_inc(s_tp, 1)
                pe.wait_ge(s_ea, U + 2)
                pe.wait_ge(s_ed, U + 2)
                pe.wait_ge(s_oe, U + 1)
                out = [m.bank[6][g * HD:(g + 1) * HD, 0:128] for g in range(2)]
                for br, off in enumerate((384, 640)):
                    for ch in range(T + 1):
                        o = (br * (T + 1) + ch) * 128
                        for g in range(2):
                            pe.matmul(out[g], m.kv[:, ch, off + g * HD:off + (g + 1) * HD], pt[:, g, o:o + 128],
                                      start=(br + ch == 0), stop=False)
                for g in range(2):
                    last = pe.matmul(out[g], m.cvp[:, g * HD:(g + 1) * HD], ptc[:, g, :], start=False, stop=True)
                last.then_inc(s_pv, 1)

            scores(*first)
            turns(pe, turn)

        @block.scalar
        def _(act):
            act.sem_inc(s_ea, 1)
            act.sem_inc(s_oe, 1)

            def exps(T, u, p, U):
                nk = 128 * (T + 1)
                act.wait_ge(s_nm, U + 1)
                for g in range(2):
                    for br in range(2):
                        act.activation(s[p][:, g, br, 0:nk], s[p][:, g, br, 0:nk], ACT.Exp,
                                       bias=mx[p][:, 2 * g + br:2 * g + br + 1], accum_out=sm[p][:, 2 * g + br:2 * g + br + 1])
                for g in range(2):
                    last = act.activation(sc[p][:, g, :], sc[p][:, g, :], ACT.Exp, bias=mx[p][:, 4 + g:5 + g],
                                          accum_out=sm[p][:, 4 + g:5 + g])
                last.then_inc(s_ex, 1)

            def turn(this, after):
                T, u, p, U = this
                nk = 128 * (T + 1)
                act.wait_ge(s_tp, U + 1)
                act.activation(ptc[:, :, :], m.bank[5][0:NC_P, 0:256].rearrange("p (g t) -> p g t", g=2), ACT.Copy)
                act.activation(pt[:, 0, 0:2 * nk], m.bank[3][:, 0:2 * nk], ACT.Copy).then_inc(s_ea, 1)
                if after:
                    exps(*after)
                act.wait_ge(s_pv, U + 1)
                act.activation(m.hnT[:, bass.ds(u, 1), T * 128:(T + 1) * 128], m.bank[6][:, 0:128], ACT.Copy).then_inc(s_oe, 1)

            exps(*first)
            turns(act, turn)

        @block.vector
        def _(dve):
            link = Link(dve, s_chain)
            dve.sem_inc(s_ed, 1)

            def mask_and_max(T, u, p, U):
                nk = 128 * (T + 1)
                dve.wait_ge(s_sc, U + 1)
                for g in range(2):
                    link.go(dve.tensor_tensor(s[p][:, g, :, 0:nk], m.bank[g][:, 0:2 * nk].rearrange("p (r k) -> p r k", r=2),
                                              m.key_mask[:, SEQ - nk:SEQ].unsqueeze(1).to_broadcast((128, 2, nk)), ALU.add))
                    link.go(dve.tensor_tensor(sc[p][:, g, :], m.bank[(2, 7)[g]][:, 0:NC_P], m.cmp_mask[:, T, :], ALU.add))
                link.wait()
                dve.sem_inc(s_msk, 1)
                link.go(dve.tensor_reduce(mx[p][:, 0:4], s[p][:, :, :, 0:nk], AX.X, ALU.max))
                link(dve.tensor_reduce(mx[p][:, 4:6], sc[p][:, :, :], AX.X, ALU.max))
                link(dve.tensor_scalar(mx[p][:, :], mx[p][:, :], NEG_CLAMP, -1.0, ALU.max, ALU.mult))
                dve.sem_inc(s_nm, 1)

            def turn(this, after):
                T, u, p, U = this
                nk = 128 * (T + 1)
                link.base, link.n = U * PER + FIRST, 0
                dve.wait_ge(s_ex, U + 1)
                link(dve.tensor_scalar(sm[p][:, :], sm[p][:, :], TINY, None, ALU.max))
                link(dve.reciprocal(sm[p][:, :], sm[p][:, :]))
                gate = m.ngate[:, T, :].rearrange("p (g j r) -> p g j r", g=2, r=3)
                link.go(dve.tensor_tensor(sm[p][:, 0:4].rearrange("p (g r) -> p g r", g=2), sm[p][:, 0:4].rearrange("p (g r) -> p g r", g=2),
                                          gate[:, :, bass.ds(u, 1), 1:3].rearrange("p g j r -> p g (j r)"), ALU.mult))
                link(dve.tensor_tensor(sm[p][:, 4:6], sm[p][:, 4:6],
                                       gate[:, :, bass.ds(u, 1), 0:1].rearrange("p g j r -> p g (j r)").rearrange("p g r -> p (g r)"), ALU.mult))
                for i in range(6):
                    link.go(dve.tensor_scalar(dg[:, i, :], m.ident[:, :], sm[p][:, i:i + 1], None, ALU.mult))
                link.wait()
                dve.sem_inc(s_dg, 1)
                if after:
                    mask_and_max(*after)
                dve.wait_ge(s_tp, U + 1)
                link(dve.tensor_copy(pt[:, 1, 0:2 * nk], m.bank[4][:, 0:2 * nk]))
                dve.sem_inc(s_ed, 1)
                assert not after or link.n == PER, link.n

            mask_and_max(*first)
            turns(dve, turn)


def nsa_sample(nc, m, a):
    s_pa = [m.sem(f"pages_k_slot{p}") for p in range(2)]
    s_pb = [m.sem(f"pages_v_slot{p}") for p in range(2)]
    s_q, s_t, s_te, s_c, s_ce, s_ct = m.sem("ns_q"), m.sem("ns_T"), m.sem("ns_T_ev"), m.sem("ns_cmp"), m.sem("ns_cmp_ev"), m.sem("ns_ckT")
    s_sc, s_pc, s_imp = m.sem("ns_scores"), m.sem("ns_pcmp"), m.sem("ns_imp")
    s_cm, s_ec, s_nm, s_ex = m.sem("ns_cmax"), m.sem("ns_cexp"), m.sem("ns_negmax"), m.sem("ns_exp")
    s_dg, s_p, s_pe_, s_pv, s_o = m.sem("ns_diag"), m.sem("ns_pT"), m.sem("ns_pT_ev"), m.sem("ns_pv"), m.sem("ns_out")
    s_chain, s_pd = m.sem("ns_dve"), m.sem("ns_pT_ev_dve")
    NS1, NS2, NS3, NS4 = PAST, PAST + 64, PAST + 64 + WIN, PAST + 64 + WIN + 64
    PER = 25
    with ExitStack() as c:
        def sb(name, shape):
            return c.enter_context(nc.sbuf_tensor(name, shape, FP))

        pa = [sb(f"ns_pa{p}", [128, NPG, 384]) for p in range(2)]
        pb = [sb(f"ns_pb{p}", [128, NPG, 128]) for p in range(2)]
        wk = [sb(f"ns_wk{p}", [128, WIN // 128, 128]) for p in range(2)]
        wv = [sb(f"ns_wv{p}", [128, WIN // 128, 128]) for p in range(2)]
        kT = sb("ns_kT", [128, 3 * PAST + WIN])
        cc = [sb(f"ns_cc{p}", [128, 128]) for p in range(2)]
        ck = sb("ns_ck", [128, NC_S])
        s = sb("ns_s", [128, NS4])
        pc = sb("ns_pc", [128, NC_S])
        pen = sb("ns_pen", [128, 16])
        imp = sb("ns_imp", [128, 14])
        st = sb("ns_st", [128, 8])
        dg = sb("ns_dg", [128, 3, 128])
        pt = sb("ns_pt", [128, 15, 128])
        block = c.enter_context(nc.Block())

        def turns(eng, turn):
            with eng.Fori(0, NB // 2 - 1) as i:
                for p in range(2):
                    turn(2 * i + p, p, True)
            turn(NB - 2, 0, True)
            turn(NB - 1, 1, False)

        @block.sync
        def _(sp):
            def page(b, j):
                return sp.value_load(m.pages[0:1, bass.ds(b * NPG + j, 1)], min_val=0, max_val=a.cache_kv.shape[0] - 1)

            def load(b, p, dst, win, cols, kind, sem):
                sp.dma_start(win[p][:, :, :], a.cache_win_kv[0, bass.ds(b, 1), :, kind].rearrange("b (w r) g d -> r (b w) (g d)", r=128)
                             ).then_inc(sem[p], 16)
                for j in range(NPG):
                    sp.dma_start(dst[p][:, j, :], a.cache_kv[bass.ds(page(b, j), 1)].rearrange("n r l c g d -> r (n l c g d)")[:, cols]
                                 ).then_inc(sem[p], 16)

            def load_k(b, p):
                load(b, p, pa, wk, slice(0, 384), 0, s_pa)

            def load_v(b, p):
                load(b, p, pb, wv, slice(384, 512), 1, s_pb)

            for p in range(2):
                load_k(p, p)
                load_v(p, p)
            with sp.Fori(0, NB // 2 - 1) as i:
                for p in range(2):
                    b = 2 * i + p
                    sp.wait_ge(s_t, 7 * b + 7)
                    load_k(b + 2, p)
                    sp.wait_ge(s_pv, b + 1)
                    load_v(b + 2, p)

        @block.gpsimd
        def _(pool):
            def queries(b):
                for g in range(2):
                    pool.tensor_copy(m.qbd[g * HD:(g + 1) * HD, g * 64:(g + 1) * 64].rearrange("p (h t) -> p h t", t=TS),
                                     m.zf[g * HD:(g + 1) * HD, 32:40, bass.ds(b * TS + SEQ, TS)]).then_inc(s_q, 1)

            def turn(b, p, more):
                if more:
                    pool.wait_ge(s_sc, 2 * b + 2)
                    queries(b + 1)
            queries(0)
            turns(pool, turn)

        @block.tensor
        def _(pe):
            def transposes(b, p, first, last_f):
                if first == 0:
                    pe.wait_ge(s_pa[p], (b - p) * 8 * (NPG + 1) + 16 * (NPG + 1))
                for f in range(first, last_f):
                    pe.wait_ge(s_te, 7 * b + f + 1)
                    for j in range(4):
                        src = (pa[p][:, (f % 2) * 4 + j, (f // 2) * 128:(f // 2 + 1) * 128] if f < 6 else wk[p][:, j, :])
                        last = pe.transpose(m.bank[(7 * p + f) % 2][:, j * 128:(j + 1) * 128], src, m.ident[:, :])
                    last.then_inc(s_t, 1)

            def compress(b):
                pe.wait_ge(s_te, 7 * b + 6)
                rows = lambda i: m.bank[2][(1 - i) * 64:(2 - i) * 64, 0:128]
                for i in range(2):
                    pe.matmul(rows(i), m.ones[:, 0:64], m.bcmp_row[:, i * 128:(i + 1) * 128], start=True, stop=False)
                for r in range(CMP):
                    for i in range(2):
                        last = pe.matmul(rows(i), kT[:, i * PAST + r:i * PAST + r + CST * 63 + 1:CST], m.wc[:, i * CMP + r, :],
                                         start=False, stop=(r == CMP - 1))
                last.then_inc(s_c, 1)

            def transpose_ck(b, p):
                pe.wait_ge(s_ce, 2 * b + 1)
                pe.matmul(m.bank[2][:, 128:192], cc[p][64:128, :], m.ident[64:128, 64:128], start=True, stop=True).then_inc(s_ct, 1)

            def scores(b):
                pe.wait_ge(s_ce, 2 * b + 2)
                pe.wait_ge(s_q, 2 * b + 2)
                q = m.qbd[:, :]
                pe.matmul(m.bank[7][:, 0:NC_S], q, ck[:, :], start=True, stop=True)
                pe.matmul(m.bank[7][:, 64:128], q, m.kT[:, 2, SEQ:], start=True, stop=True)
                pe.matmul(m.bank[7][:, 128:192], q, m.kT[:, 3, SEQ:], start=True, stop=True).then_inc(s_sc, 1)
                pe.wait_ge(s_te, 7 * b + 9)
                pe.matmul(m.bank[4][:, :], q, kT[:, 2 * PAST:2 * PAST + 512], start=True, stop=True)
                pe.matmul(m.bank[5][:, :], q, kT[:, 2 * PAST + 512:3 * PAST], start=True, stop=True)
                pe.matmul(m.bank[6][:, :], q, kT[:, 3 * PAST:], start=True, stop=True).then_inc(s_sc, 1)

            def turn(b, p, more):
                if more:
                    transposes(b + 1, 1 - p, 0, 4)
                pe.wait_ge(s_pc, b + 1)
                pe.wait_ge(s_o, b + 1)
                pe.matmul(m.bank[3][:, 0:NC_S], m.peer[:, :], pc[:, :], start=True, stop=True).then_inc(s_imp, 1)
                if more:
                    transposes(b + 1, 1 - p, 4, 7)
                    compress(b + 1)
                pe.wait_ge(s_dg, b + 1)
                for o in range(8):
                    pe.matmul(m.bank[4 + o // 4][:, (o % 4) * 128:(o % 4 + 1) * 128], s[:, o * 128:(o + 1) * 128], dg[:, 0, :],
                              start=True, stop=True)
                for o in range(4):
                    pe.matmul(m.bank[6][:, o * 128:(o + 1) * 128], s[:, NS2 + o * 128:NS2 + (o + 1) * 128], dg[:, 1, :],
                              start=True, stop=True)
                pe.matmul(m.bank[7][0:64, 0:128], s[:, NS1:NS2], dg[:, 0, :], start=True, stop=True)
                pe.matmul(m.bank[7][0:64, 128:256], s[:, NS3:NS4], dg[:, 1, :], start=True, stop=True)
                pe.matmul(m.bank[7][0:NC_S, 256:384], pc[:, :], dg[:, 2, :], start=True, stop=True).then_inc(s_p, 1)
                if more:
                    transpose_ck(b + 1, 1 - p)
                pe.wait_ge(s_pb[p], (b - p) * 8 * (NPG + 1) + 16 * (NPG + 1))
                pe.wait_ge(s_pe_, b + 1)
                pe.wait_ge(s_pd, b + 1)
                out = m.bank[3][:, 128:256]
                pe.matmul(out, cc[p][0:NC_S, :], pt[0:NC_S, 14, :], start=True, stop=False)
                for o in range(8):
                    pe.matmul(out, pb[p][:, o, :], pt[:, o, :], start=False, stop=False)
                for o in range(4):
                    pe.matmul(out, wv[p][:, o, :], pt[:, 8 + o, :], start=False, stop=False)
                pe.matmul(out, m.kv[0:64, 2, 384:512], pt[0:64, 12, :], start=False, stop=False)
                pe.matmul(out, m.kv[0:64, 2, 640:768], pt[0:64, 13, :], start=False, stop=True).then_inc(s_pv, 1)
                if more:
                    scores(b + 1)

            transposes(0, 0, 0, 7)
            compress(0)
            transpose_ck(0, 0)
            scores(0)
            turns(pe, turn)

        @block.scalar
        def _(act):
            def take_T(b, p, first, last_f):
                for f in range(first, last_f):
                    act.wait_ge(s_t, 7 * b + f + 1)
                    act.activation(kT[:, f * 512:(f + 1) * 512], m.bank[(7 * p + f) % 2][:, :], ACT.Copy).then_inc(s_te, 1)

            def take_c(b, p):
                act.wait_ge(s_c, b + 1)
                act.activation(cc[p][:, :], m.bank[2][:, 0:128], ACT.Copy).then_inc(s_ce, 1)
                act.wait_ge(s_ct, b + 1)
                act.activation(ck[:, :], m.bank[2][:, 128:128 + NC_S], ACT.Copy).then_inc(s_ce, 1)

            def turn(b, p, more):
                act.wait_ge(s_cm, b + 1)
                act.activation(pc[:, :], m.bank[7][:, 0:NC_S], ACT.Exp, bias=st[:, 0:1], accum_out=st[:, 1:2]).then_inc(s_ec, 1)
                if more:
                    take_T(b + 1, 1 - p, 0, 7)
                act.wait_ge(s_nm, b + 1)
                act.activation(s[:, 0:NS2], s[:, 0:NS2], ACT.Exp, bias=st[:, 2:3], accum_out=st[:, 4:5])
                act.activation(s[:, NS2:NS4], s[:, NS2:NS4], ACT.Exp, bias=st[:, 3:4], accum_out=st[:, 5:6]).then_inc(s_ex, 1)
                if more:
                    act.wait_ge(s_c, b + 2)
                    act.activation(cc[1 - p][:, :], m.bank[2][:, 0:128], ACT.Copy).then_inc(s_ce, 1)
                act.wait_ge(s_p, b + 1)
                act.activation(pt[:, 0:4, :].rearrange("p o c -> p (o c)"), m.bank[4][:, :], ACT.Copy)
                act.activation(pt[:, 4:8, :].rearrange("p o c -> p (o c)"), m.bank[5][:, :], ACT.Copy).then_inc(s_pe_, 1)
                if more:
                    act.wait_ge(s_ct, b + 2)
                    act.activation(ck[:, :], m.bank[2][:, 128:128 + NC_S], ACT.Copy).then_inc(s_ce, 1)
                act.wait_ge(s_pv, b + 1)
                for g in range(2):
                    last = act.activation(m.hnT[g * HD:(g + 1) * HD, :, bass.ds(b * TS + SEQ, TS)],
                                          m.bank[3][g * HD:(g + 1) * HD, 128 + g * 64:128 + (g + 1) * 64].rearrange("p (h t) -> p h t", t=TS), ACT.Copy)
                last.then_inc(s_o, 1)

            act.sem_inc(s_te, 2)
            act.sem_inc(s_o, 1)
            take_T(0, 0, 0, 7)
            take_c(0, 0)
            turns(act, turn)

        @block.vector
        def _(dve):
            link = Link(dve, s_chain)

            def turn(b, p, more):
                link.base, link.n = b * PER, 0
                dve.wait_ge(s_sc, 2 * b + 1)
                link(dve.tensor_reduce(st[:, 0:1], m.bank[7][:, 0:NC_S], AX.X, ALU.max))
                link(dve.tensor_scalar(st[:, 0:1], st[:, 0:1], -1.0, None, ALU.mult))
                dve.sem_inc(s_cm, 1)
                dve.wait_ge(s_ec, b + 1)
                link(dve.reciprocal(st[:, 1:2], st[:, 1:2]))
                link(dve.tensor_scalar(pc[:, :], pc[:, :], st[:, 1:2], None, ALU.mult))
                dve.sem_inc(s_pc, 1)
                new = m.new_mask[:, bass.ds(b * 64, 64)]
                link.go(dve.tensor_tensor(s[:, NS1:NS2], m.bank[7][:, 64:128], new, ALU.add))
                link.go(dve.tensor_tensor(s[:, NS3:NS4], m.bank[7][:, 128:192], new, ALU.add))
                dve.wait_ge(s_sc, 2 * b + 2)
                link.go(dve.tensor_tensor(s[:, NS2:NS3], m.bank[6][:, :], m.win_mask[:, :], ALU.add))
                dve.wait_ge(s_imp, b + 1)
                ib = m.bank[3][:, 4:60].rearrange("p (n c) -> p n c", c=4)
                before = m.bank[3][:, 3:59].rearrange("p (n c) -> p n c", c=4)
                link(dve.tensor_reduce(imp[:, :], ib[:, :, 0:3], AX.X, ALU.add))
                for half in (before[:, :, 0:1], ib[:, :, 3:4]):
                    link(dve.scalar_tensor_tensor(imp[:, :], half.rearrange("p n c -> p (n c)"), 0.5, imp[:, :], ALU.mult, ALU.add))
                link(dve.tensor_reduce(st[:, 6:7], imp[:, :], AX.X, ALU.min))
                link(dve.tensor_scalar(imp[:, :], imp[:, :], st[:, 6:7], None, ALU.is_equal))
                link(dve.tensor_tensor(imp[:, :], imp[:, :], m.blk_idx[:, 1:15], ALU.mult))
                link(dve.tensor_reduce(st[:, 7:8], imp[:, :], AX.X, ALU.max))
                link(dve.tensor_scalar(pen[:, :], m.blk_idx[:, :], st[:, 7:8], NEG, ALU.is_equal, ALU.mult))
                for i in range(2):
                    link.go(dve.tensor_tensor(s[:, i * 512:(i + 1) * 512].rearrange("p (n k) -> p n k", k=64),
                                              m.bank[4 + i][:, :].rearrange("p (n k) -> p n k", k=64),
                                              pen[:, i * 8:(i + 1) * 8].unsqueeze(2).to_broadcast((128, 8, 64)), ALU.add))
                link.wait()
                link.go(dve.tensor_reduce(st[:, 2:3], s[:, 0:NS2], AX.X, ALU.max))
                link(dve.tensor_reduce(st[:, 3:4], s[:, NS2:NS4], AX.X, ALU.max))
                link(dve.tensor_scalar(st[:, 2:4], st[:, 2:4], -1.0, None, ALU.mult))
                dve.sem_inc(s_nm, 1)
                dve.wait_ge(s_ex, b + 1)
                link(dve.reciprocal(st[:, 4:6], st[:, 4:6]))
                gate = m.gate_s[:, bass.ds(b, 1), 1:3].rearrange("p b r -> p (b r)")
                link(dve.tensor_tensor(st[:, 4:6], st[:, 4:6], gate, ALU.mult))
                for i in range(2):
                    link.go(dve.tensor_scalar(dg[:, i, :], m.ident[:, :], st[:, 4 + i:5 + i], None, ALU.mult))
                link(dve.tensor_scalar(dg[:, 2, :], m.ident[:, :], m.gate_s[:, bass.ds(b, 1), 0:1].rearrange("p b r -> p (b r)"), None, ALU.mult))
                dve.sem_inc(s_dg, 1)
                dve.wait_ge(s_p, b + 1)
                dve.tensor_copy(pt[:, 8:12, :].rearrange("p o c -> p (o c)"), m.bank[6][:, :])
                dve.tensor_copy(pt[0:64, 12:14, :].rearrange("p o c -> p (o c)"), m.bank[7][0:64, 0:256])
                dve.tensor_copy(pt[0:NC_S, 14, :], m.bank[7][0:NC_S, 256:384]).then_inc(s_pd, 1)
                assert link.n == PER, link.n
            turns(dve, turn)


def merge(nc, m, a):
    s_wm, s_wn, s_wo = m.sem("wbm_in"), m.sem("wbn_in"), m.sem("wout_in")
    s_pe, s_ev, s_chain, s_po, s_x = m.sem("mg_branch"), m.sem("mg_gated"), m.sem("mg_dve"), m.sem("mg_out"), m.sem("mg_added")
    with ExitStack() as c:
        wm = c.enter_context(nc.sbuf_tensor("w_bm", [128, KD, D], FP))
        wn = c.enter_context(nc.sbuf_tensor("w_bn", [128, KD, D], FP))
        wo = c.enter_context(nc.sbuf_tensor("w_o", [128, KD, D], FP))
        t1 = c.enter_context(nc.sbuf_tensor("mg_t1", [128, NTOK], FP))
        mT = m.zf[:, 32:40, :]
        block = c.enter_context(nc.Block())

        @block.sync
        def _(sp):
            sp.dma_start(wm[:, :, :], a.w_branch_m[0].rearrange("(k p) n -> p k n", p=128)).then_inc(s_wm, 16)
            wn_v = a.w_branch_n[0].rearrange("(g j d) n -> g d j n", g=2, d=HD)
            for g in range(2):
                sp.dma_start(wn[g * HD:(g + 1) * HD, :, :], wn_v[g]).then_inc(s_wn, 16)
            sp.dma_start(wo[:, :, :], a.w_out[0].rearrange("(k p) n -> p k n", p=128)).then_inc(s_wo, 16)

        @block.tensor
        def _(pe):
            for f in range(KD):
                for i, (w, h, s_w, n) in enumerate(((wm, m.hmT, s_wm, 16), (wn, m.hnT, s_wn, 32))):
                    if f == 0:
                        pe.wait_ge(s_w, n)
                    if f >= 2:
                        pe.wait_ge(s_ev, f - 1)
                    for k in range(KD):
                        last = pe.matmul(m.bank[2 * i + f % 2][:, 0:NTOK], w[:, k, f * 128:(f + 1) * 128], h[:, k, :],
                                         start=(k == 0), stop=(k == KD - 1))
                last.then_inc(s_pe, 1)
            pe.wait_ge(s_wo, 16)
            pe.wait_ge(s_ev, KD)
            n = 0
            for t, rows in enumerate(TILE_ROWS):
                for h in range(2):
                    if n >= 4:
                        pe.wait_ge(s_x, n - 3)
                    for k in range(KD):
                        last = pe.matmul(m.bank[4 + n % 4][0:rows, :], mT[:, k, t * 128:t * 128 + rows],
                                         wo[:, k, h * 512:(h + 1) * 512], start=(k == 0), stop=(k == KD - 1))
                    last.then_inc(s_po, 1)
                    n += 1

        @block.vector
        def _(dve):
            link = Link(dve, s_chain)
            for f in range(KD):
                dve.wait_ge(s_pe, f + 1)
                link.go(dve.tensor_tensor(mT[:, f, :], m.bank[f % 2][:, 0:NTOK], m.zf[:, 16 + f, :], ALU.mult))
                link(dve.tensor_tensor(t1[:, :], m.bank[2 + f % 2][:, 0:NTOK], m.zf[:, 24 + f, :], ALU.mult))
                dve.tensor_tensor(mT[:, f, :], mT[:, f, :], t1[:, :], ALU.add).then_inc(s_ev, 1)
                dve.wait_ge(s_ev, f + 1)
            n = 0
            for t, rows in enumerate(TILE_ROWS):
                for h in range(2):
                    dve.wait_ge(s_po, n + 1)
                    xs = m.x[0:rows, t, h * 512:(h + 1) * 512]
                    dve.tensor_tensor(xs, xs, m.bank[4 + n % 4][0:rows, :], ALU.add).then_inc(s_x, 1)
                    n += 1


def weight_loads(sp, m, a, e, wait=None):
    for c in range(NCHUNK):
        if wait is not None:
            wait(c)
        if c < 4:
            src = a.w_gu[0, bass.ds(e, 1), c * 256:(c + 1) * 256, :].rearrange("e (j p) n -> p (e j) n", p=128)
            dst = m.wring[:, c, :].rearrange("p (j n) -> p j n", j=2)
        else:
            src = a.w_dn[0, bass.ds(e, 1), (c - 4) * 512:(c - 3) * 512, :].rearrange("e (j p) n -> p (e j) n", p=128)
            dst = m.wring[:, c, :].rearrange("p (j n) -> p j n", j=4)
        sp.dma_start(dst, src).then_inc(m.s_slot[c], 16)


def route(nc, m, a):
    s_g, s_bg, s_w, s_br = m.sem("g2_in"), m.sem("bgu_in"), m.sem("wr_in"), m.sem("br_in")
    s_ms, s_sq, s_xn, s_xT, s_xTe = m.sem("n2_ms"), m.sem("n2_sqrt"), m.sem("xn2_ready"), m.sem("xn2_T"), m.sem("xn2_T_ev")
    s_lg, s_mx, s_ex, s_sel = m.sem("logits"), m.sem("top_max"), m.sem("top_exp"), m.sem("sel_ready")
    s_pos, s_wT, s_c2, s_chain = m.sem("pos_done"), m.sem("wt_T"), m.sem("bdn_in"), m.sem("route_dve")
    with ExitStack() as c:
        def sb(name, shape, dt=FP):
            return c.enter_context(nc.sbuf_tensor(name, shape, dt))

        g2 = sb("g2b", [128, D])
        br = sb("brb", [128, NE])
        wr = sb("w_r", [128, KD, NE])
        xT = sb("xn2T", [128, KD, NTOK])
        junk = sb("junk2", [128, D])
        ss = sb("ss2", [128, NT])
        lg = sb("lg", [128, NT, NE])
        mx = sb("mx8", [128, NT, 8])
        ix = sb("ix8", [128, NT, 8], U32)
        ixf = sb("ixf", [128, NT, 8])
        nm = sb("nmx", [128, NT])
        sm = sb("sm4", [128, NT])
        w4 = sb("w4", [128, NT, 4])
        sel = sb("sel", [128, NT, NE])
        oh = sb("oh", [128, NE])
        cnt = sb("cnt", [128, NE])
        ext = sb("ext", [128, NE])
        cs = sb("cs", [128, NE])
        cse = sb("cse", [128, NE])
        o1 = sb("o1", [128, N_OVER, NE])
        o2 = sb("o2", [128, N_OVER, NE])
        ej = sb("ej", [128, N_OVER])
        bj = sb("bj", [128, N_OVER])
        ef = sb("ef", [1, NITEM + 1])
        block = c.enter_context(nc.Block())

        @block.sync
        def _(sp):
            sp.dma_start(g2[:, :], a.norm2_g.to_broadcast((128, D))).then_inc(s_g, 16)
            sp.dma_start(br[:, :], a.b_router.to_broadcast((128, NE))).then_inc(s_br, 16)
            sp.dma_start(wr[:, :, :], a.w_router[0].rearrange("(k p) e -> p k e", p=128)).then_inc(s_w, 16)
            sp.dma_start(m.bgu[:, :], a.b_gu[0]).then_inc(s_bg, 16)
            sp.dma_start(m.bdn[:, :], a.b_dn[0]).then_inc(s_c2, 16)
            sp.wait_ge(s_bg, 16)
            sp.wait_ge(s_c2, 16)
            weight_loads(sp, m, a, 0)

        @block.tensor
        def _(pe):
            pe.wait_ge(s_xn, NT)
            for k in range(KD):
                if k >= 2:
                    pe.wait_ge(s_xTe, k - 1)
                for t, n in enumerate(TILE_ROWS):
                    last = pe.transpose(m.bank[1 + k % 2][:, t * 128:t * 128 + n], m.xn[0:n, t, k * 128:(k + 1) * 128],
                                        m.ident[0:n, 0:n])
                last.then_inc(s_xT, 1)
            pe.wait_ge(s_xTe, KD)
            pe.wait_ge(s_w, 16)
            for t, n in enumerate(TILE_ROWS):
                for k in range(KD):
                    last = pe.matmul(m.bank[3][0:n, t * NE:(t + 1) * NE], xT[:, k, t * 128:t * 128 + n], wr[:, k, :],
                                     start=(k == 0), stop=(k == KD - 1))
            last.then_inc(s_lg, 1)
            pe.wait_ge(s_sel, 1)
            for t, n in enumerate(TILE_ROWS):
                for u in range(t + 1):
                    nu = TILE_ROWS[u]
                    lhs = m.tri if u == t else m.ones
                    pe.matmul(m.bank[4][0:n, t * NE:(t + 1) * NE], lhs[0:nu, 0:n], sel[0:nu, u, :], start=(u == 0), stop=(u == t))
            for u, nu in enumerate(TILE_ROWS):
                last = pe.matmul(m.bank[4][:, NT * NE:(NT + 1) * NE], m.ones[0:nu, :], sel[0:nu, u, :], start=(u == 0), stop=(u == NT - 1))
            last.then_inc(s_pos, 1)
            for t, n in enumerate(TILE_ROWS):
                last = pe.transpose(m.bank[5][0:NE, t * 128:t * 128 + n], m.wt[0:n, t, 0:NE], m.ident[0:n, 0:n])
            last.then_inc(s_wT, 1)

        @block.scalar
        def _(act):
            act.wait_ge(s_ms, 1)
            act.activation(ss[:, :], ss[:, :], ACT.Sqrt).then_inc(s_sq, 1)
            for t, n in enumerate(TILE_ROWS):
                act.wait_ge(s_mx, t + 1)
                act.activation(w4[0:n, t, :], mx[0:n, t, 0:4], ACT.Exp, bias=nm[0:n, t:t + 1],
                               accum_out=sm[0:n, t:t + 1]).then_inc(s_ex, 1)

        @block.vector
        def _(dve):
            link = Link(dve, s_chain)
            link.go(dve.memset(m.acc[:, :, :], 0.0))
            link.go(dve.memset(m.pos[:, :, :], -1.0))
            link.go(dve.memset(m.wt[:, :, :], 0.0))
            link.go(dve.memset(ef[:, :], 0.0))
            link(dve.memset(ss[:, :], 1.0))
            for t, n in enumerate(TILE_ROWS):
                link(dve.tensor_tensor_reduce(out=junk[0:n, :], in0=m.x[0:n, t, :], in1=m.x[0:n, t, :], scale=1.0,
                                              scalar=0.0, op0=ALU.mult, op1=ALU.add, accum_out=ss[0:n, t:t + 1]))
            link(dve.tensor_scalar(ss[:, :], ss[:, :], 1.0 / D, EPS, ALU.mult, ALU.add))
            dve.sem_inc(s_ms, 1)
            dve.wait_ge(s_sq, 1)
            link(dve.reciprocal(ss[:, :], ss[:, :]))
            dve.wait_ge(s_g, 16)
            for t, n in enumerate(TILE_ROWS):
                dve.scalar_tensor_tensor(m.xn[0:n, t, :], m.x[0:n, t, :], ss[0:n, t:t + 1], g2[0:n, :], ALU.mult,
                                         ALU.mult).then_inc(s_xn, 1)
            for k in range(KD):
                dve.wait_ge(s_xT, k + 1)
                dve.tensor_copy(xT[:, k, :], m.bank[1 + k % 2][:, 0:NTOK]).then_inc(s_xTe, 1)
            dve.wait_ge(s_lg, 1)
            dve.wait_ge(s_br, 16)
            for t, n in enumerate(TILE_ROWS):
                link(dve.tensor_tensor(lg[0:n, t, :], m.bank[3][0:n, t * NE:(t + 1) * NE], br[0:n, :], ALU.add))
                link(dve.max(mx[0:n, t, :], lg[0:n, t, :]))
                link.go(dve.max_index(ix[0:n, t, :], mx[0:n, t, :], lg[0:n, t, :]))
                link(dve.tensor_scalar(nm[0:n, t:t + 1], mx[0:n, t, 0:1], -1.0, None, ALU.mult))
                dve.sem_inc(s_mx, 1)
                link(dve.tensor_copy(ixf[0:n, t, :], ix[0:n, t, :]))
                dve.wait_ge(s_ex, t + 1)
                link(dve.reciprocal(sm[0:n, t:t + 1], sm[0:n, t:t + 1]))
                link(dve.tensor_scalar(w4[0:n, t, :], w4[0:n, t, :], sm[0:n, t:t + 1], None, ALU.mult))
                for k in range(4):
                    if k == 0:
                        link.go(dve.tensor_scalar(sel[0:n, t, :], m.exp_idx[0:n, :], ixf[0:n, t, 0:1], None, ALU.is_equal))
                        link(dve.tensor_scalar(m.wt[0:n, t, 0:NE], m.exp_idx[0:n, :], ixf[0:n, t, 0:1], w4[0:n, t, 0:1],
                                               ALU.is_equal, ALU.mult))
                    else:
                        link.go(dve.scalar_tensor_tensor(sel[0:n, t, :], m.exp_idx[0:n, :], ixf[0:n, t, k:k + 1], sel[0:n, t, :],
                                                         ALU.is_equal, ALU.add))
                        link(dve.tensor_scalar(oh[0:n, :], m.exp_idx[0:n, :], ixf[0:n, t, k:k + 1], w4[0:n, t, k:k + 1],
                                               ALU.is_equal, ALU.mult))
                        link(dve.tensor_tensor(m.wt[0:n, t, 0:NE], m.wt[0:n, t, 0:NE], oh[0:n, :], ALU.add))
            dve.sem_inc(s_sel, 1)
            dve.wait_ge(s_pos, 1)
            for t, n in enumerate(TILE_ROWS):
                link(dve.tensor_tensor(m.pos[0:n, t, 0:NE], m.bank[4][0:n, t * NE:(t + 1) * NE], sel[0:n, t, :], ALU.mult))
                link(dve.tensor_scalar(sel[0:n, t, :], sel[0:n, t, :], 1e6, -1e6, ALU.mult, ALU.add))
                link(dve.tensor_tensor(m.pos[0:n, t, 0:NE], m.pos[0:n, t, 0:NE], sel[0:n, t, :], ALU.add))
            link(dve.tensor_copy(cnt[:, :], m.bank[4][:, NT * NE:(NT + 1) * NE]))
            link(dve.tensor_scalar(ext[:, :], cnt[:, :], float(SLOT), None, ALU.is_gt))
            for k in range(2, NTOK // SLOT):
                link(dve.scalar_tensor_tensor(ext[:, :], cnt[:, :], float(k * SLOT), ext[:, :], ALU.is_gt, ALU.add))
            link(dve.tensor_tensor_scan(cs[:, :], m.ones[:, 0:NE], ext[:, :], 0.0, ALU.mult, ALU.add))
            link(dve.tensor_tensor(cse[:, :], cs[:, :], ext[:, :], ALU.subtract))
            ov = (128, N_OVER, NE)
            wide = lambda t: t.unsqueeze(1).to_broadcast(ov)
            link.go(dve.tensor_tensor(o1[:, :, :], m.over_idx[:, :, :], wide(cse[:, :]), ALU.is_ge))
            link(dve.tensor_tensor(o2[:, :, :], m.over_idx[:, :, :], wide(cs[:, :]), ALU.is_ge))
            link(dve.tensor_tensor(o1[:, :, :], o1[:, :, :], o2[:, :, :], ALU.subtract))
            link(dve.tensor_tensor(o2[:, :, :], o1[:, :, :], wide(m.exp_idx[:, :]), ALU.mult))
            link(dve.tensor_reduce(ej[:, :], o2[:, :, :], AX.X, ALU.add))
            link(dve.tensor_tensor(o2[:, :, :], m.over_idx[:, :, :], wide(cse[:, :]), ALU.subtract))
            link(dve.tensor_scalar(o2[:, :, :], o2[:, :, :], 1.0, None, ALU.add))
            link(dve.tensor_tensor(o2[:, :, :], o2[:, :, :], o1[:, :, :], ALU.mult))
            link(dve.tensor_reduce(bj[:, :], o2[:, :, :], AX.X, ALU.add))
            for t, n in enumerate(TILE_ROWS):
                for dst in (m.pos, m.wt):
                    link(dve.tensor_tensor(o2[0:n, :, :], o1[0:n, :, :], dst[0:n, t, 0:NE].unsqueeze(1).to_broadcast((n, N_OVER, NE)), ALU.mult))
                    link(dve.tensor_reduce(dst[0:n, t, NE:NITEM], o2[0:n, :, :], AX.X, ALU.add))
                link(dve.scalar_tensor_tensor(m.pos[0:n, t, NE:NITEM], bj[0:n, :], -float(SLOT), m.pos[0:n, t, NE:NITEM], ALU.mult, ALU.add))
            link.go(dve.tensor_copy(m.of_expert[:, 0:NE], m.ident[0:NE, 0:NE]))
            link.go(dve.tensor_scalar(m.of_expert[:, NE:NITEM], ej[0:NE, :], m.part_idx[0:NE, 0:1], None, ALU.is_equal))
            link.go(dve.memset(m.of_expert[:, NITEM:NITEM + 1], 0.0))
            link.go(dve.tensor_copy(ef[:, 0:NE], m.exp_idx[0:1, :]))
            link(dve.tensor_copy(ef[:, NE:NITEM], ej[0:1, :]))
            link(dve.tensor_copy(m.etab[:, 0:NITEM + 1], ef[:, :]))
            link(dve.tensor_scalar(ef[:, 0:1], cs[0:1, NE - 1:NE], float(NE), None, ALU.add))
            link(dve.tensor_copy(m.etab[:, NITEM + 1:NITEM + 2], ef[:, 0:1]))
            dve.wait_ge(s_wT, 1)
            dve.tensor_copy(m.wtT[:, :], m.bank[5][0:NE, 0:NTOK])


def experts(nc, m, a):
    s_oh, s_ohw, s_ohe, s_g, s_xg = m.sem("ex_onehot"), m.sem("ex_onehot_w"), m.sem("ex_onehot_e"), m.sem("ex_gathered"), m.sem("ex_x")
    s_xT, s_xe = m.sem("ex_x_T"), m.sem("ex_xT_ready")
    s_used, s_gf, s_tr, s_oht = m.sem("ex_chunk_used"), m.sem("ex_gu_read"), m.sem("ex_scatter_T"), m.sem("ex_scatter_m")
    s_sc, s_acc, s_gm, s_sg = m.sem("ex_scattered"), m.sem("ex_added"), m.sem("ex_gate"), m.sem("ex_sigmoid")
    s_at, s_aT, s_ate, s_ys, s_chain = m.sem("ex_act"), m.sem("ex_act_T"), m.sem("ex_actT_ready"), m.sem("ex_y"), m.sem("ex_dve")
    PER = 4
    H = D // 2
    with ExitStack() as c:
        def sb(name, shape):
            return c.enter_context(nc.sbuf_tensor(name, shape, FP))

        oh = sb("ex_oh", [128, NT, SLOT])
        ohw = sb("ex_ohw", [128, NT, 2 * SLOT])
        ohe = sb("ex_ohe", [NE, SLOT])
        oht = sb("ex_oht", [128, NT * 128])
        xg = sb("ex_xg", [128, H])
        xe = sb("ex_xe", [128, 4, 2, SLOT])
        gt = sb("ex_gt", [128, H])
        up = sb("ex_up", [128, H])
        sg = sb("ex_sg", [128, H])
        at = sb("ex_at", [128, H])
        atT = sb("ex_atT", [128, 4, 2, SLOT])
        ys = sb("ex_ys", [128, H])
        warm = sb("ex_warm", [128, 1])
        block = c.enter_context(nc.Block())

        def n_items(eng):
            return eng.value_load(m.etab[0:1, NITEM + 1:NITEM + 2], min_val=NE, max_val=NITEM)

        @block.sync
        def _(sp):
            nw = n_items(sp)
            with sp.Fori(1, nw) as i:
                e = sp.value_load(m.etab[0:1, bass.ds(i, 1)], min_val=0, max_val=NE - 1)
                weight_loads(sp, m, a, e, wait=lambda ch: sp.wait_ge(s_used, NCHUNK * i + (ch + 1 - NCHUNK)))

        @block.tensor
        def _(pe):
            half = lambda bank, h: m.bank[bank][h * SLOT:(h + 1) * SLOT, :]

            def gather():
                for t, n in enumerate(TILE_ROWS):
                    for h in range(2):
                        last = pe.matmul(half(0, h), oh[0:n, t, :], m.xn[0:n, t, h * H:(h + 1) * H],
                                         start=(t == 0), stop=(t == NT - 1))
                last.then_inc(s_g, 1)

            def transpose(bank, src, sem):
                for k in range(4):
                    last = pe.matmul(m.bank[bank][:, k * 128:(k + 1) * 128], src[:, k * 128:(k + 1) * 128], m.ident[:, :],
                                     start=True, stop=True)
                last.then_inc(sem, 1)

            def scatter(i):
                pe.wait_ge(s_ys, i + 1)
                pe.wait_ge(s_oht, i + 1)
                for t in range(NT):
                    if t != 1:
                        pe.wait_ge(s_acc, 6 * i + (2 if t == 2 else 0) + 6)
                    for h in range(2):
                        pe.matmul(m.bank[(6, 4, 6)[t] + h][:, :], oht[h * SLOT:(h + 1) * SLOT, t * 128:(t + 1) * 128],
                                  ys[h * SLOT:(h + 1) * SLOT, :], start=True, stop=True).then_inc(s_sc, 1)

            nw = n_items(pe)
            pe.wait_ge(s_oh, 1)
            gather()
            pe.wait_ge(s_xg, 1)
            transpose(0, xg, s_xT)
            with pe.Fori(0, nw) as i:
                pe.wait_ge(s_ohe, i + 1)
                pe.wait_ge(s_gf, i + 1)
                for gu in range(2):
                    for h in range(2):
                        pe.matmul(half(2 + gu, h), ohe[:, :], m.bgu[:, gu * FE + h * H:gu * FE + (h + 1) * H], start=True, stop=False)
                pe.wait_ge(s_xe, i + 1)
                for k in range(KD):
                    if k % 2 == 0:
                        pe.wait_ge(m.s_slot[k // 2], 16 * i + 16)
                    for gu in range(2):
                        for h in range(2):
                            o = (k % 2) * 2 * FE + gu * FE + h * H
                            last = pe.matmul(half(2 + gu, h), xe[:, k % 4, k // 4, :], m.wring[:, k // 2, o:o + H],
                                             start=False, stop=(k == KD - 1))
                    if k % 2 == 1:
                        last.then_inc(s_used, 1)
                    if k == 3:
                        scatter(i)
                pe.wait_ge(s_ohw, i + 1)
                for t, n in enumerate(TILE_ROWS):
                    last = pe.matmul(m.bank[1][:, t * 128:t * 128 + n], ohw[0:n, t, :], m.ident[0:n, 0:n], start=True, stop=True)
                last.then_inc(s_tr, 1)
                pe.wait_ge(s_oh, i + 2)
                gather()
                pe.wait_ge(s_at, i + 1)
                pe.wait_ge(s_acc, 6 * i + 10)
                transpose(5, at, s_aT)
                pe.wait_ge(s_xg, i + 2)
                transpose(0, xg, s_xT)
                pe.wait_ge(s_ate, i + 1)
                for k in range(8):
                    if k % 4 == 0:
                        pe.wait_ge(m.s_slot[4 + k // 4], 16 * i + 16)
                    for h in range(2):
                        o = (k % 4) * D + h * H
                        last = pe.matmul(half(4, h), atT[:, k % 4, k // 4, :], m.wring[:, 4 + k // 4, o:o + H],
                                         start=(k == 0), stop=(k == 7))
                    if k % 4 == 3:
                        last.then_inc(s_used, 1)
            scatter(nw)

        @block.scalar
        def _(act):
            def copy(dst, bank, sem):
                act.activation(dst, m.bank[bank][:, :], ACT.Copy).then_inc(sem, 1)

            flat = lambda t: t[:, :, :, :].rearrange("p k h s -> p (k h s)")
            nw = n_items(act)
            act.activation(warm[:, :], m.ones[:, 0:1], ACT.Sigmoid)
            act.wait_ge(s_g, 1)
            copy(xg[:, :], 0, s_xg)
            act.wait_ge(s_xT, 1)
            copy(flat(xe), 0, s_xe)
            with act.Fori(0, nw) as i:
                act.wait_ge(s_tr, i + 1)
                act.wait_ge(s_sc, 6 * i + 6)
                act.activation(oht[:, 0:NTOK], m.bank[1][:, 0:NTOK], ACT.Copy).then_inc(s_oht, 1)
                act.wait_ge(s_gm, i + 1)
                act.activation(sg[:, :], gt[:, :], ACT.Sigmoid, scale=1.702).then_inc(s_sg, 1)
                act.wait_ge(s_g, i + 2)
                copy(xg[:, :], 0, s_xg)
                act.wait_ge(s_aT, i + 1)
                copy(flat(atT), 5, s_ate)
                act.wait_ge(s_xT, i + 2)
                copy(flat(xe), 0, s_xe)
                act.wait_ge(s_used, NCHUNK * i + NCHUNK)
                copy(ys[:, :], 4, s_ys)

        @block.vector
        def _(dve):
            link = Link(dve, s_chain)

            def one_hot(i):
                for t, n in enumerate(TILE_ROWS):
                    last = dve.tensor_scalar(oh[0:n, t, :], m.slot_idx[0:n, 0:SLOT], m.pos[0:n, t, bass.ds(i, 1)], None, ALU.is_equal)
                last.then_inc(s_oh, 1)

            def of_expert(i):
                dve.tensor_copy(ohe[:, :], m.of_expert[:, bass.ds(i, 1)].to_broadcast((NE, SLOT))).then_inc(s_ohe, 1)

            def add_scattered(i):
                for r in range(2 * NT):
                    n = TILE_ROWS[r // 2]
                    part = m.acc[0:n, r // 2, (r % 2) * H:(r % 2 + 1) * H]
                    dve.wait_ge(s_sc, 6 * i + r + 1)
                    dve.tensor_tensor(part, part, m.bank[(6, 4, 6)[r // 2] + r % 2][0:n, :], ALU.add).then_inc(s_acc, 1)

            nw = n_items(dve)
            link.go(dve.memset(ys[:, :], 0.0))
            link(dve.memset(oht[:, :], 0.0))
            dve.sem_inc(s_ys, 1)
            dve.sem_inc(s_oht, 1)
            dve.sem_inc(s_gf, 1)
            dve.sem_inc(s_acc, 6)
            one_hot(0)
            of_expert(0)
            with dve.Fori(0, nw) as i:
                link.base, link.n = i * PER + 2, 0
                dve.wait_ge(s_g, i + 1)
                one_hot(i + 1)
                dve.wait_ge(s_oht, i + 1)
                for t, n in enumerate(TILE_ROWS):
                    last = dve.tensor_scalar(ohw[0:n, t, :], m.slot_idx[0:n, :], m.pos[0:n, t, bass.ds(i, 1)],
                                             m.wt[0:n, t, bass.ds(i, 1)], ALU.is_equal, ALU.mult)
                last.then_inc(s_ohw, 1)
                dve.wait_ge(s_acc, 6 * i + 6)
                add_scattered(i)
                dve.wait_ge(s_used, NCHUNK * i + 4)
                link(dve.tensor_scalar(gt[:, :], m.bank[2][:, :], 7.0, None, ALU.min))
                dve.sem_inc(s_gm, 1)
                link(dve.tensor_scalar(up[:, :], m.bank[3][:, :], 7.0, -7.0, ALU.min, ALU.max))
                dve.sem_inc(s_gf, 1)
                link(dve.scalar_tensor_tensor(up[:, :], up[:, :], 1.0, gt[:, :], ALU.add, ALU.mult))
                dve.wait_ge(s_sg, i + 1)
                link(dve.tensor_tensor(at[:, :], up[:, :], sg[:, :], ALU.mult))
                dve.sem_inc(s_at, 1)
                assert link.n == PER, link.n
                of_expert(i + 1)
            dve.wait_ge(s_acc, 6 * nw + 6)
            add_scattered(nw)


def finish(nc, m, a):
    s_g, s_b, s_ms, s_sq, s_chain, s_y, s_out = (m.sem("gf_in"), m.sem("bdn_sum"), m.sem("fin_ms"), m.sem("fin_sqrt"),
                                                 m.sem("fin_dve"), m.sem("y_ready"), m.sem("y_out"))
    with ExitStack() as c:
        gf = c.enter_context(nc.sbuf_tensor("gf", [128, D], FP))
        junk = c.enter_context(nc.sbuf_tensor("junk3", [128, D], FP))
        ss = c.enter_context(nc.sbuf_tensor("ss3", [128, NT], FP))
        block = c.enter_context(nc.Block())

        @block.sync
        def _(sp):
            sp.dma_start(gf[:, :], a.normf_g.rearrange("(o n) -> o n", o=1).to_broadcast((128, D))).then_inc(s_g, 16)
            sp.wait_ge(s_y, 1)
            sp.dma_start(a.y_prompt[0, 0:128], m.x[:, 0, :]).then_inc(s_out, 16)
            sp.wait_ge(s_y, 2)
            sp.dma_start(a.y_prompt[0, 128:256], m.x[:, 1, :]).then_inc(s_out, 16)
            sp.wait_ge(s_y, 3)
            sp.dma_start(a.y_sample.rearrange("b t d -> (b t) d"), m.x[0:64, 2, :]).then_inc(s_out, 16)
            sp.wait_ge(s_out, 48)

        @block.tensor
        def _(pe):
            for r in range(2 * NT):
                n = TILE_ROWS[r // 2]
                last = pe.matmul(m.bank[r][0:n, :], m.wtT[:, (r // 2) * 128:(r // 2) * 128 + n],
                                 m.bdn[:, (r % 2) * 512:(r % 2 + 1) * 512], start=True, stop=True)
            last.then_inc(s_b, 1)

        @block.scalar
        def _(act):
            act.wait_ge(s_ms, 1)
            act.activation(ss[:, :], ss[:, :], ACT.Sqrt).then_inc(s_sq, 1)

        @block.vector
        def _(dve):
            link = Link(dve, s_chain)
            link(dve.memset(ss[:, :], 1.0))
            for t, n in enumerate(TILE_ROWS):
                link.go(dve.tensor_tensor(m.x[0:n, t, :], m.x[0:n, t, :], m.acc[0:n, t, :], ALU.add))
            link.wait()
            dve.wait_ge(s_b, 1)
            for r in range(2 * NT):
                n = TILE_ROWS[r // 2]
                part = m.x[0:n, r // 2, (r % 2) * 512:(r % 2 + 1) * 512]
                link.go(dve.tensor_tensor(part, part, m.bank[r][0:n, :], ALU.add))
            link.wait()
            for t, n in enumerate(TILE_ROWS):
                link(dve.tensor_tensor_reduce(out=junk[0:n, :], in0=m.x[0:n, t, :], in1=m.x[0:n, t, :], scale=1.0,
                                              scalar=0.0, op0=ALU.mult, op1=ALU.add, accum_out=ss[0:n, t:t + 1]))
            link(dve.tensor_scalar(ss[:, :], ss[:, :], 1.0 / D, EPS, ALU.mult, ALU.add))
            dve.sem_inc(s_ms, 1)
            dve.wait_ge(s_sq, 1)
            link(dve.reciprocal(ss[:, :], ss[:, :]))
            dve.wait_ge(s_g, 16)
            for t, n in enumerate(TILE_ROWS):
                dve.scalar_tensor_tensor(m.x[0:n, t, :], m.x[0:n, t, :], ss[0:n, t:t + 1], gf[0:n, :], ALU.mult,
                                         ALU.mult).then_inc(s_y, 1)


def allocate(nc, m, c):
    def sb(name, shape, dt=FP):
        return c.enter_context(nc.sbuf_tensor(name, shape, dt))

    m.bank = [c.enter_context(nc.psum_tensor(f"bank{i}", [128, 512], FP)) for i in range(8)]
    m.ident = sb("ident", [128, 128])
    m.ones = sb("ones", [128, 128])
    m.tri = sb("tri", [128, 128])
    m.causal_st = sb("causal_st", [128, 128])
    m.causal_tk = sb("causal_tk", [128, 128])
    m.same_seq = sb("same_seq", [64, 64])
    m.seg_mul = sb("seg_mul", [MH, NTOK])
    m.seg_add = sb("seg_add", [MH, NTOK])
    m.seq_onehot = sb("seq_onehot", [64, NB])
    m.cmp_mask = sb("cmp_mask", [128, 2, NC_P])
    m.period = sb("period", [TS, 128])
    m.new8 = sb("new8", [TS, 512])
    m.win8 = sb("win8", [TS, WIN])
    m.new_mask = sb("new_mask", [128, NB * 64])
    m.win_mask = sb("win_mask", [128, WIN])
    m.peer = sb("peer", [128, 128])
    m.blk_idx = sb("blk_idx", [128, 16])
    m.slot_idx = sb("slot_idx", [128, 2 * SLOT])
    m.part_idx = sb("part_idx", [128, 1])
    m.exp_idx = sb("exp_idx", [128, NE])
    m.over_idx = sb("over_idx", [128, N_OVER, NE])
    m.x = sb("x", [128, NT, D])


def allocate_mixers(nc, m, c):
    def sb(name, shape, dt=FP):
        return c.enter_context(nc.sbuf_tensor(name, shape, dt))

    m.par = sb("par", [128, 7, KD])
    m.bias_feat = sb("bias_feat", [128, 40])
    m.zf = sb("zf", [128, 40, NTOK])
    m.kv = sb("kv", [128, NT, KVC])
    m.ngate = sb("ngate", [128, NT, 48])
    m.gate_bias = sb("gate_bias", [MH, 2])
    m.hmT = m.zf[:, 0:KD, :]
    m.hnT = m.zf[:, KD:2 * KD, :]


def allocate_mlstm(nc, m, c):
    def sb(name, shape, dt=FP):
        return c.enter_context(nc.sbuf_tensor(name, shape, dt))

    m.xc = sb("xc", [128, KD, NTOK])
    m.mqT = sb("mqT", [128, MH, NTOK])
    m.mkT = sb("mkT", [128, MH, NTOK])
    m.mk = sb("mk", [128, MH, 3 * DQK])
    m.grow = sb("grow", [MH, NTOK + 64 + NB])
    m.gcol = sb("gcol", [128, NT, 3, MH])


def allocate_nsa(nc, m, c):
    def sb(name, shape, dt=FP):
        return c.enter_context(nc.sbuf_tensor(name, shape, dt))

    m.wc = sb("wc", [128, 2 * CMP, 128])
    m.bcmp = sb("bcmp", [128, 2])
    m.bcmp_row = sb("bcmp_row", [128, 2 * 128])
    m.kT = sb("kT", [128, 4, NTOK])
    m.ckp = sb("ckp", [128, NC_P])
    m.cvp = sb("cvp", [NC_P, 128])
    m.gate_s = sb("gate_s", [128, NB, 3])
    m.pages = sb("pages", [1, NB * NPG], I32)
    m.qbd = sb("qbd", [128, 128])
    m.key_mask = sb("key_mask", [128, SEQ])


def allocate_moe(nc, m, c):
    def sb(name, shape, dt=FP):
        return c.enter_context(nc.sbuf_tensor(name, shape, dt))

    m.wring = sb("wring", [128, NCHUNK, 4096])
    m.s_slot = [m.sem(f"chunk{i}_in") for i in range(NCHUNK)]
    m.xn = sb("xn2", [128, NT, D])
    m.acc = sb("acc", [128, NT, D])
    m.pos = sb("pos", [128, NT, NITEM + 1])
    m.wt = sb("wt", [128, NT, NITEM + 1])
    m.wtT = sb("wtT", [NE, NTOK])
    m.bgu = sb("bgu", [NE, 2 * FE])
    m.of_expert = sb("of_expert", [NE, NITEM + 1])
    m.bdn = sb("bdn", [NE, D])
    m.etab = sb("etab", [1, NITEM + 2], I32)


def hybrid_step(nc, a, stages=31):
    with ExitStack() as c:
        m = Mem()
        done_with = []

        def sem(name):
            done_with.append(nc.alloc_semaphore(name))
            return done_with[-1]

        m.sem = sem
        allocate(nc, m, c)
        with ExitStack() as mix:
            allocate_mixers(nc, m, mix)
            make_consts(nc, m)
            with ExitStack() as cell:
                m.v = cell.enter_context(nc.sbuf_tensor("v", [128, NT, MH, VX], FP))
                m.gate_rows = cell.enter_context(nc.sbuf_tensor("gate_rows", [MH, 2, NTOK], FP))
                with ExitStack() as proj:
                    m.uT = proj.enter_context(nc.sbuf_tensor("uT", [128, KD, NTOK], FP))
                    m.bias_tok = proj.enter_context(nc.sbuf_tensor("bias_tok", [128, D + OFF_BG - OFF_NKV], FP))
                    norm_in(nc, m, a)
                    project(nc, m, a)
                allocate_mlstm(nc, m, cell)
                if stages & 1:
                    conv_silu(nc, m, a)
                    mlstm_gates(nc, m, a)
                    mlstm_heads(nc, m, a)
            nc.clear_and_free_semaphores(done_with)
            with nc.Block():
                pass
            with ExitStack() as attn:
                allocate_nsa(nc, m, attn)
                if stages & 2:
                    nsa_prepare(nc, m, a)
                    nsa_prompt(nc, m, a)
                if stages & 4:
                    nsa_sample(nc, m, a)
            if stages & 8:
                merge(nc, m, a)
        if stages & 8:
            allocate_moe(nc, m, c)
            route(nc, m, a)
        if stages & 16:
            experts(nc, m, a)
            finish(nc, m, a)


_INS = ['x_prompt', 'x_sample', 'cache_kv', 'cache_win_kv', 'state_conv', 'state_C', 'state_n', 'state_m',
        'page_table', 'norm1_g', 'w_in', 'b_in', 'w_conv', 'b_conv', 'w_mq', 'w_mk', 'g_mnorm', 'w_cmp', 'b_cmp',
        'w_branch_m', 'w_branch_n', 'w_out', 'norm2_g', 'w_router', 'b_router', 'w_gu', 'b_gu', 'w_dn', 'b_dn',
        'normf_g']
_OUTS = [('y_prompt', (1, 256, 1024)), ('y_sample', (8, 8, 1024)), ('new_kv_p', (1, 256, 1, 4, 2, 64)),
         ('new_win_p', (1, 1, 256, 2, 2, 64)), ('new_conv_p', (1, 1, 3, 1024)), ('new_C_p', (1, 1, 4, 128, 256)),
         ('new_n_p', (1, 1, 4, 128)), ('new_m_p', (1, 1, 4)), ('new_kv_s', (8, 8, 1, 4, 2, 64)),
         ('new_win_s', (1, 8, 512, 2, 2, 64)), ('new_conv_s', (1, 8, 3, 1024)), ('new_C_s', (1, 8, 4, 128, 256)),
         ('new_n_s', (1, 8, 4, 128)), ('new_m_s', (1, 8, 4))]


class Args:
    pass


def kernel(**inputs):
    import numpy as np
    import concourse.bacc as bacc
    from concourse.bass_utils import run_bass_kernel_spmd

    nc = bacc.Bacc("TRN2", target_bir_lowering=False, num_devices=1)
    arrays, a = {}, Args()
    for name in _INS:
        arr = np.ascontiguousarray(inputs[name])
        arrays[name] = arr
        a.__dict__[name] = nc.dram_tensor(name, arr.shape, mybir.dt.from_np(arr.dtype), kind="ExternalInput").ap()
    for name, shape in _OUTS:
        a.__dict__[name] = nc.dram_tensor(name, shape, FP, kind="ExternalOutput").ap()
    hybrid_step(nc, a)
    r = run_bass_kernel_spmd(nc, [arrays], core_ids=[0])
    return tuple(r.results[0][name] for name, _ in _OUTS)
```

```python
import concourse.bass as bass
from concourse import mybir
from contextlib import ExitStack

FP = mybir.dt.float32
I32 = mybir.dt.int32
U32 = mybir.dt.uint32
ALU = mybir.AluOpType
ACT = mybir.ActivationFunctionType
AX = mybir.AxisListType

D = 1024
SEQ = 256
NB = 8
TS = 8
NTOK = SEQ + NB * TS
KD = D // 128
TILE_ROWS = [128, 128, 64]
NT = len(TILE_ROWS)
EPS = 1e-6
TINY = 1e-30
NEG = -1e30
NEG_CLAMP = -1e29

MH = 4
DV = 256
DQK = 128
VX = DV + 1
HD = 64
KVC = 768
PAST = 1024
PAGE = 128
NPG = PAST // PAGE
WIN = 512
CMP = 32
CST = 16
NC_P = SEQ // CST - 1
NC_S = PAST // CST - 1
NE = 32
FE = 1024
SLOT = 64
N_OVER = 20
NITEM = NE + N_OVER
NCHUNK = 6

OFF_MX, OFF_MV, OFF_MO, OFF_MI, OFF_MF, OFF_NQ = 0, 1024, 2048, 3072, 3076, 3080
OFF_NKV, OFF_NG, OFF_BG = 4104, 4872, 4920


class Link:

    def __init__(self, eng, sem):
        self.eng, self.sem, self.base, self.n = eng, sem, 0, 0

    def go(self, ins):
        ins.then_inc(self.sem, 1)
        self.n += 1

    def wait(self):
        self.eng.wait_ge(self.sem, self.base + self.n)

    def __call__(self, ins):
        self.go(ins)
        self.wait()

    def loop(self, i, per):
        if isinstance(i, int) and i > 0:
            assert self.n == per, (self.n, per)
            self.base, self.n = i * per + self.before, 0
        else:
            self.before, self.per, self.base, self.n = self.n, per, i * per + self.n, 0

    def done(self, turns):
        assert self.n == self.per, (self.n, self.per)
        self.base, self.n = 0, self.before + turns * self.per


class Mem:
    pass


def start(nc, m, a):
    s0, s1, s2, s_id = m.sem("const_fill"), m.sem("const_sel"), m.sem("const_sel2"), m.sem("const_ident")
    s_pe, s_cv = m.sem("const_pe"), m.sem("const_ev")
    s_x, s_p, s_v = m.sem("x_in"), m.sem("params_in"), m.sem("vec_in")
    s_tp, s_ev, s_chain = m.sem("tp_done"), m.sem("tp_evicted"), m.sem("norm1_dve")
    s_ms, s_sq = m.sem("norm1_ms"), m.sem("norm1_sqrt")
    s_xn = m.sem("norm1_scaled")
    xp = a.x_prompt.rearrange("b (t p) d -> p (b t) d", p=128)
    xs = a.x_sample.rearrange("b t d -> (b t) d")
    with ExitStack() as c:
        xn = c.enter_context(nc.sbuf_tensor("xn1", [128, NT, D], FP))
        ss = c.enter_context(nc.sbuf_tensor("ss1", [128, NT], FP))
        prow = c.enter_context(nc.sbuf_tensor("prow", [12, D], FP))
        pcol = c.enter_context(nc.sbuf_tensor("pcol", [128, KD, 12], FP))
        period = c.enter_context(nc.sbuf_tensor("period", [TS, 128], FP))
        new8 = c.enter_context(nc.sbuf_tensor("new8", [TS, 512], FP))
        win8 = c.enter_context(nc.sbuf_tensor("win8", [TS, WIN], FP))
        block = c.enter_context(nc.Block())

        @block.gpsimd
        def _(pool):
            pool.memset(m.ident[:], 0.0).then_inc(s_id, 1)
            pool.wait_ge(s_id, 1)
            pool.affine_select(out=m.ident[:], in_=m.ident[:], pattern=[[-1, 128]], compare_op=ALU.not_equal, fill=1.0,
                               base=0, channel_multiplier=1).then_inc(s_id, 1)
            fills = [(m.ones, 1.0), (m.tri, 1.0), (m.causal_st, 0.0), (m.causal_tk, 0.0),
                     (m.same_seq, 0.0), (m.seg_mul, 1.0), (m.seg_add, 0.0), (m.seq_onehot, 1.0),
                     (m.cmp_mask, 0.0), (period, 1.0), (new8, 0.0), (win8, 0.0)]
            for t, v in fills:
                pool.memset(t[:], v).then_inc(s0, 1)
            pool.iota(m.blk_idx[:], [[1, 16]], base=0, channel_multiplier=0,
                      allow_small_or_imprecise_dtypes=True).then_inc(s0, 1)
            pool.iota(m.slot_idx[:], [[0, 2], [1, SLOT]], base=0, channel_multiplier=0,
                      allow_small_or_imprecise_dtypes=True).then_inc(s0, 1)
            pool.iota(m.exp_idx[:], [[1, NE]], base=0, channel_multiplier=0,
                      allow_small_or_imprecise_dtypes=True).then_inc(s0, 1)
            pool.iota(m.over_idx[:], [[1, N_OVER]], base=0, channel_multiplier=0,
                      allow_small_or_imprecise_dtypes=True).then_inc(s0, 1)
            pool.iota(m.thresholds[:], [[SLOT, NTOK // SLOT - 1]], base=SLOT, channel_multiplier=0,
                      allow_small_or_imprecise_dtypes=True).then_inc(s0, 1)
            pool.iota(m.part_idx[:], [[0, 1]], base=0, channel_multiplier=1,
                      allow_small_or_imprecise_dtypes=True).then_inc(s0, 1)
            pool.wait_ge(s0, len(fills) + 6)

            def sel(t, pattern, base, cm, op, fill, sem=s1):
                pool.affine_select(out=t, in_=t, pattern=pattern, compare_op=op, fill=fill,
                                   base=base, channel_multiplier=cm).then_inc(sem, 1)

            sel(m.tri[:], [[1, 128]], 0, -1, ALU.is_gt, 0.0)
            sel(m.causal_st[:], [[1, 128]], 0, -1, ALU.is_ge, NEG)
            sel(m.causal_tk[:], [[-1, 128]], 0, 1, ALU.is_ge, NEG)
            sel(m.same_seq[:], [[1, 64]], 0, -1, ALU.is_ge, NEG)
            sel(m.seg_mul[:, SEQ:], [[0, NB], [1, TS]], 0, 0, ALU.is_gt, 0.0)
            sel(m.seg_add[:, SEQ:], [[0, NB], [1, TS]], 0, 0, ALU.is_gt, NEG)
            sel(m.seq_onehot[:], [[-TS, NB]], 0, 1, ALU.is_ge, 0.0)
            for t in range(2):
                sel(m.cmp_mask[:, t, :], [[-CST, NC_P]], 128 * t - (CMP - 1), 1, ALU.is_ge, NEG)
            sel(period[:], [[0, 16], [-1, TS]], 0, 1, ALU.is_equal, 0.0)
            sel(new8[:], [[0, NB], [0, NB], [-1, TS]], 0, 1, ALU.is_ge, NEG)
            sel(win8[:], [[1, WIN]], 0, -1, ALU.is_gt, NEG)
            pool.wait_ge(s1, 12)
            sel(m.same_seq[:], [[-TS, NB], [0, TS]], 0, 1, ALU.is_ge, NEG, s2)
            sel(m.seq_onehot[:], [[TS, NB]], TS - 1, -1, ALU.is_ge, 0.0, s2)
            sel(new8[:], [[1, NB], [-1, NB], [0, TS]], 0, 0, ALU.is_equal, NEG, s2)

        @block.sync
        def _(sp):
            sp.dma_start(m.x[:, 0:2, :], xp).then_inc(s_x, 16)
            sp.dma_start(m.x[0:64, 2, :], xs).then_inc(s_x, 16)
            w_v = a.w_in[0].rearrange("(k p) n -> p k n", p=128)
            sp.wait_ge(s_p, 160)
            sp.dma_start(m.w_gates[:, :, :], w_v[:, :, OFF_MI:OFF_NQ]).then_inc(m.s_wg, 16)
            for i, (o, n) in enumerate(win_chunks()[:NSL]):
                sp.dma_start(m.w_slots[:, i, :, 0:n], w_v[:, :, o:o + n]).then_inc(m.s_win[i], 16)

        @block.scalar
        def _(act):
            b_in = a.b_in
            act.dma_start(prow[0:4, :], a.w_conv[0]).then_inc(s_p, 16)
            act.dma_start(prow[4:5, :], a.b_conv).then_inc(s_p, 16)
            act.dma_start(prow[5:6, :], a.g_mnorm.rearrange("l h v -> l (h v)")).then_inc(s_p, 16)
            act.dma_start(prow[6:7, :], a.norm1_g).then_inc(s_p, 16)
            act.dma_start(prow[7:8, :], b_in[:, OFF_MX:OFF_MX + D]).then_inc(s_p, 16)
            act.dma_start(prow[8:9, :], b_in[:, OFF_MO:OFF_MO + D]).then_inc(s_p, 16)
            act.dma_start(prow[9:10, :], b_in[:, OFF_BG:OFF_BG + D]).then_inc(s_p, 16)
            act.dma_start(prow[10:11, :], b_in[:, OFF_BG + D:OFF_BG + 2 * D]).then_inc(s_p, 16)
            for g in range(2):
                act.dma_start(prow[11:12, :].rearrange("p (j g d) -> p g j d", g=2, d=HD)[:, g],
                              b_in[:, OFF_NQ + g * 512:OFF_NQ + (g + 1) * 512].rearrange("l (j d) -> l j d", d=HD)).then_inc(s_p, 16)
            act.dma_start(m.bias_tok[:, 0:D], b_in[:, OFF_MV:OFF_MV + D].to_broadcast((128, D))).then_inc(s_v, 16)
            act.dma_start(m.bias_tok[:, D:], b_in[:, OFF_NKV:OFF_BG].to_broadcast((128, OFF_BG - OFF_NKV))).then_inc(s_v, 16)
            act.dma_start(m.gate_bias[:, 0:1], b_in[:, OFF_MI:OFF_MF].rearrange("l h -> h l")).then_inc(s_v, 16)
            act.dma_start(m.gate_bias[:, 1:2], b_in[:, OFF_MF:OFF_NQ].rearrange("l h -> h l")).then_inc(s_v, 16)
            act.wait_ge(s_ms, 1)
            act.activation(ss[:, :], ss[:, :], ACT.Sqrt).then_inc(s_sq, 1)
            act.wait_ge(s_v, 64)

        @block.vector
        def _(dve):
            link = Link(dve, s_chain)
            link(dve.memset(ss[:, :], 1.0))
            dve.wait_ge(s_x, 32)
            for t, n in enumerate(TILE_ROWS):
                link(dve.tensor_tensor_reduce(out=xn[0:n, t, :], in0=m.x[0:n, t, :], in1=m.x[0:n, t, :], scale=1.0,
                                              scalar=0.0, op0=ALU.mult, op1=ALU.add, accum_out=ss[0:n, t:t + 1]))
            dve.tensor_scalar(ss[:, :], ss[:, :], 1.0 / D, EPS, ALU.mult, ALU.add).then_inc(s_ms, 1)
            dve.wait_ge(s_sq, 1)
            link(dve.reciprocal(ss[:, :], ss[:, :]))
            for t, n in enumerate(TILE_ROWS):
                dve.tensor_scalar(xn[0:n, t, :], m.x[0:n, t, :], ss[0:n, t:t + 1], None, ALU.mult).then_inc(s_xn, 1)
            dve.wait_ge(s_tp, 1)
            link(dve.tensor_copy(pcol[:, :, :], m.bank[0][:, 0:KD * 12].rearrange("p (k r) -> p k r", r=12)))
            dve.tensor_copy(m.par[:, :, :], pcol[:, :, 0:7].rearrange("p k r -> p r k"))
            dve.tensor_copy(m.bias_feat[:, :].rearrange("p (r k) -> p r k", k=KD), pcol[:, :, 7:12].rearrange("p k r -> p r k"))
            for k in range(KD):
                dve.wait_ge(s_tp, 2 + k)
                dve.tensor_scalar(m.uT[:, k, :], m.bank[1 + k % 2][:, 0:NTOK], pcol[:, k, 6:7], None,
                                  ALU.mult).then_inc(s_ev, 1)
            dve.wait_ge(s_pe, 3)
            dve.tensor_copy(m.new_mask[:], m.bank[3][:, :])
            dve.tensor_copy(m.win_mask[:], m.bank[4][:, :])
            dve.tensor_copy(m.peer[:], m.bank[5][:, 0:128]).then_inc(s_cv, 1)
            dve.wait_ge(s_cv, 1)
            dve.memset(m.peer[0:64, 64:128], 0.0)
            dve.memset(m.peer[64:128, 0:64], 0.0)

        @block.tensor
        def _(pe):
            pe.wait_ge(s_id, 2)
            pe.wait_ge(s_p, 160)
            for k in range(KD):
                last = pe.transpose(m.bank[0][:, k * 12:(k + 1) * 12], prow[:, k * 128:(k + 1) * 128], m.ident[0:12, 0:12])
            last.then_inc(s_tp, 1)
            pe.wait_ge(s_xn, NT)
            for k in range(KD):
                if k >= 2:
                    pe.wait_ge(s_ev, k - 1)
                for t, n in enumerate(TILE_ROWS):
                    last = pe.transpose(m.bank[1 + k % 2][:, t * 128:t * 128 + n], xn[0:n, t, k * 128:(k + 1) * 128],
                                        m.ident[0:n, 0:n])
                last.then_inc(s_tp, 1)
            pe.wait_ge(s2, 3)
            pe.matmul(m.bank[3][:, :], period[:], new8[:], start=True, stop=True).then_inc(s_pe, 1)
            pe.matmul(m.bank[4][:, :], period[:], win8[:], start=True, stop=True).then_inc(s_pe, 1)
            pe.matmul(m.bank[5][:, 0:128], period[:], period[:], start=True, stop=True).then_inc(s_pe, 1)


NCH = 8
NSL = 3


def win_chunks():
    feat = [OFF_MX, OFF_MX + 512, OFF_MO, OFF_MO + 512] + [OFF_BG + 512 * i for i in range(4)]
    return [(o, 512) for o in feat] + [(OFF_NQ, 512), (OFF_NQ + 512, 512), (OFF_MV, 512), (OFF_MV + 512, 512),
                                       (OFF_NKV, 512), (OFF_NKV + 512, 304)]


def project(nc, m, a):
    s_w, s_wg, s_pe = m.s_win, m.s_wg, m.sem("proj_done")
    s_ev, s_pt, s_et = m.sem("proj_evicted"), m.sem("ptok_done"), m.sem("ptok_evicted")
    s_pg, s_pq, s_eq = m.sem("pgate_done"), m.sem("pq_done"), m.sem("pq_evicted")
    s_in, s_tp, s_last = m.sem("conv_state_in"), m.sem("conv_state_T"), m.sem("conv_last")
    s_lt, s_le, s_out = m.sem("conv_last_T"), m.sem("conv_last_ev"), m.sem("conv_out")
    s_chain, s_acc, s_sig = m.sem("conv_dve"), m.sem("conv_acc"), m.sem("conv_sig")
    R = NB * 3
    w_v = a.w_in[0].rearrange("(k p) n -> p k n", p=128)
    tok_cols = [(512, 0), (512, 512), (512, 1024), (304, 1536)]
    w, wg = m.w_slots, m.w_gates
    with ExitStack() as c:
        state = c.enter_context(nc.sbuf_tensor("conv_state", [R, D], FP))
        xs = c.enter_context(nc.sbuf_tensor("conv_xs", [128, KD, NB, TS + 3], FP))
        last3 = c.enter_context(nc.sbuf_tensor("conv_last3", [128, KD, R + 3], FP))
        rows3 = c.enter_context(nc.sbuf_tensor("conv_rows", [R + 3, D], FP))
        sig = c.enter_context(nc.sbuf_tensor("conv_sigm", [128, KD // 2, NTOK], FP))
        block = c.enter_context(nc.Block())

        @block.sync
        def _(sp):
            sp.dma_start(state[:, :], a.state_conv[0].rearrange("b r d -> (b r) d")).then_inc(s_in, 16)
            for i, (o, n) in enumerate(win_chunks()):
                before = i - NSL
                if before < 0:
                    continue
                if before >= NCH + 2:
                    sp.wait_ge(s_pt, NT * (before - NCH - 1))
                elif before >= NCH:
                    sp.wait_ge(s_pq, KD)
                else:
                    sp.wait_ge(s_pe, 4 * (before + 1))
                sp.dma_start(w[:, i % NSL, :, 0:n], w_v[:, :, o:o + n]).then_inc(s_w[i % NSL], 16)
            sp.dma_start(m.wq[:, :, :], a.w_mq[0].rearrange("h (c p) d -> p (h c) d", p=128)).then_inc(m.s_wqk, 16)
            sp.dma_start(m.wk[:, :, :], a.w_mk[0].rearrange("h (c p) d -> p (h c) d", p=128)).then_inc(m.s_wqk, 16)
            sp.wait_ge(s_le, 2)
            sp.dma_start(a.new_conv_p[0, 0], rows3[0:3, :]).then_inc(s_out, 16)
            sp.dma_start(a.new_conv_s[0].rearrange("b r d -> (b r) d"), rows3[3:R + 3, :]).then_inc(s_out, 16)
            sp.wait_ge(s_out, 32)

        @block.tensor
        def _(pe):
            pe.wait_ge(s_wg, 16)
            for r in range(2):
                for k in range(KD):
                    last = pe.matmul(m.bank[4 + r][0:MH, 0:NTOK], wg[:, k, MH * r:MH * (r + 1)], m.uT[:, k, :],
                                     start=(k == 0), stop=(k == KD - 1))
            last.then_inc(s_pg, 1)

            def features(chunk, s, turn):
                pe.wait_ge(s_w[s], 16 * turn + 16)
                for j in range(4):
                    pe.wait_ge(s_ev, 4 * chunk + (j + 1))
                    for k in range(KD):
                        last = pe.matmul(m.bank[j][:, 0:NTOK], w[:, s, k, j * 128:(j + 1) * 128], m.uT[:, k, :],
                                         start=(k == 0), stop=(k == KD - 1))
                    last.then_inc(s_pe, 1)

            with pe.Fori(0, NCH // NSL) as i:
                for s in range(NSL):
                    features(NSL * i + s, s, i)
            for chunk in range(NCH // NSL * NSL, NCH):
                features(chunk, chunk % NSL, chunk // NSL)
            pe.wait_ge(s_in, 16)
            for k in range(KD):
                last = pe.transpose(m.bank[6][:, k * R:(k + 1) * R], state[:, k * 128:(k + 1) * 128], m.ident[0:R, 0:R])
            last.then_inc(s_tp, 1)
            for g in range(2):
                pe.wait_ge(s_w[(NCH + g) % NSL], 16 * ((NCH + g) // NSL + 1))
            for j in range(KD):
                pe.wait_ge(s_ev, 4 + 32 - 3 + j) if j < 4 else pe.wait_ge(s_eq, j - 3)
                for k in range(KD):
                    for g in range(2):
                        last = pe.matmul(m.bank[j % 4][g * HD:(g + 1) * HD, 0:NTOK], w[:, (NCH + g) % NSL, k, j * HD:(j + 1) * HD],
                                         m.uT[:, k, :], start=(k == 0), stop=(k == KD - 1))
                last.then_inc(s_pq, 1)
            pe.wait_ge(s_last, 1)
            for k in range(KD):
                last = pe.transpose(m.bank[6 + k // 4][0:R + 3, (k % 4) * 128:(k % 4 + 1) * 128], last3[:, k, :], m.ident[:, :])
                if k % 4 == 3:
                    last.then_inc(s_lt, 1)
            n = 0
            for i, (width, _) in enumerate(tok_cols):
                s = (NCH + 2 + i) % NSL
                pe.wait_ge(s_w[s], 16 * ((NCH + 2 + i) // NSL + 1))
                for t, rows in enumerate(TILE_ROWS):
                    pe.wait_ge(s_eq, n + 5) if n < 4 else pe.wait_ge(s_et, n - 3)
                    for k in range(KD):
                        if t < 2:
                            last = pe.matmul(m.bank[n % 4][:, 0:width], m.uT[:, k, t * 128:(t + 1) * 128],
                                             w[:, s, k, 0:width], start=(k == 0), stop=(k == KD - 1))
                            continue
                        for h, (lo, hi) in enumerate(((0, 256), (256, width))):
                            last = pe.matmul(m.bank[n % 4][h * 64:(h + 1) * 64, 0:hi - lo], m.uT[:, k, SEQ:],
                                             w[:, s, k, lo:hi], start=(k == 0), stop=(k == KD - 1))
                    last.then_inc(s_pt, 1)
                    n += 1

        @block.scalar
        def _(act):
            act.sem_inc(s_ev, 4)
            act.wait_ge(s_pg, 1)
            for r in range(2):
                act.activation(m.gate_rows[:, r, :], m.bank[4 + r][0:MH, 0:NTOK], ACT.Identity, bias=m.gate_bias[:, r:r + 1])
            with act.Fori(0, NCH) as i:
                for j in range(4):
                    act.wait_ge(s_pe, 4 * i + j + 1)
                    act.activation(m.zf[:, bass.ds(4 * i + j, 1), :], m.bank[j][:, 0:NTOK], ACT.Identity,
                                   bias=m.bias_feat[:, bass.ds(4 * i + j, 1)]).then_inc(s_ev, 1)
            for j in range(KD):
                act.wait_ge(s_pq, j + 1)
                act.activation(m.zf[:, 32 + j, :], m.bank[j % 4][:, 0:NTOK], ACT.Identity,
                               bias=m.bias_feat[:, 32 + j:33 + j]).then_inc(s_eq, 1)
            for i in range(2):
                act.wait_ge(s_acc, i + 1)
                act.activation(sig[:, :, :], m.xc[:, 4 * i:4 * i + 4, :], ACT.Sigmoid).then_inc(s_sig, 1)
            act.wait_ge(s_ev, 36)
            act.activation(m.zf[:, 8:32, :], m.zf[:, 8:32, :], ACT.Sigmoid)
            act.wait_ge(s_eq, 8)
            act.activation(m.zf[:, 32:40, :], m.zf[:, 32:40, :], ACT.Copy, scale=HD ** -0.5)
            act.wait_ge(s_et, 12)
            act.activation(m.ngate[:, 0:2, :], m.ngate[:, 0:2, :], ACT.Sigmoid)
            act.activation(m.ngate[0:64, 2, :], m.ngate[0:64, 2, :], ACT.Sigmoid)

        @block.vector
        def _(dve):
            link = Link(dve, s_chain)
            dve.memset(m.v[:, :, :, DV:VX], 1.0)
            dve.wait_ge(s_ev, 4 + KD)
            link.go(dve.tensor_copy(xs[:, :, :, 3:], m.zf[:, 0:KD, SEQ:].rearrange("p k (b t) -> p k b t", t=TS)))
            link(dve.tensor_copy(last3[:, :, 0:3], m.zf[:, 0:KD, SEQ - 3:SEQ]))
            with dve.Fori(0, KD) as k:
                link.loop(k, 4)
                yp = m.xc[:, bass.ds(k, 1), 0:SEQ]
                link(dve.tensor_scalar(yp, m.zf[:, bass.ds(k, 1), 0:SEQ], m.par[:, 3, bass.ds(k, 1)], m.par[:, 4, bass.ds(k, 1)],
                                       ALU.mult, ALU.add))
                for j in range(3):
                    late = m.xc[:, bass.ds(k, 1), 3 - j:SEQ]
                    link(dve.scalar_tensor_tensor(late, m.zf[:, bass.ds(k, 1), 0:SEQ - 3 + j], m.par[:, j, bass.ds(k, 1)], late,
                                                  ALU.mult, ALU.add))
            link.done(KD)
            dve.wait_ge(s_tp, 1)
            link(dve.tensor_copy(xs[:, :, :, 0:3], m.bank[6][:, 0:KD * R].rearrange("p (k b r) -> p k b r", b=NB, r=3)))
            link(dve.tensor_copy(last3[:, :, 3:].rearrange("p k (b r) -> p k b r", r=3), xs[:, :, :, TS:TS + 3]))
            dve.sem_inc(s_last, 1)
            with dve.Fori(0, KD) as k:
                link.loop(k, 4)
                ys = m.xc[:, bass.ds(k, 1), SEQ:].rearrange("p k (b t) -> p (k b) t", t=TS)
                for j in range(4):
                    ins = xs[:, bass.ds(k, 1), :, j:j + TS].rearrange("p k b t -> p (k b) t")
                    if j == 0:
                        link(dve.tensor_scalar(ys, ins, m.par[:, 0, bass.ds(k, 1)], m.par[:, 4, bass.ds(k, 1)], ALU.mult, ALU.add))
                    else:
                        link(dve.scalar_tensor_tensor(ys, ins, m.par[:, j, bass.ds(k, 1)], ys, ALU.mult, ALU.add))
            link.done(KD)
            for i in range(2):
                dve.sem_inc(s_acc, 1)
                dve.wait_ge(s_sig, i + 1)
                half = m.xc[:, 4 * i:4 * i + 4, :]
                link(dve.tensor_tensor(half, half, sig[:, :, :], ALU.mult))
            for i in range(2):
                dve.wait_ge(s_lt, i + 1)
                dve.tensor_copy(rows3[:, i * 512:(i + 1) * 512], m.bank[6 + i][0:R + 3, :]).then_inc(s_le, 1)
            n = 0
            for i, (width, off) in enumerate(tok_cols):
                for t, rows in enumerate(TILE_ROWS):
                    dve.wait_ge(s_pt, n + 1)
                    ps = m.bank[n % 4]
                    bias = m.bias_tok[0:rows, off:off + width]
                    if t == 2:
                        halves = [(ps[h * 64:(h + 1) * 64, 0:hi - lo], m.bias_tok[h * 64:(h + 1) * 64, off + lo:off + hi])
                                  for h, (lo, hi) in enumerate(((0, 256), (256, width)))]
                        dst = ([m.v[0:64, 2, 2 * i + h, 0:DV] for h in range(2)] if i < 2 else
                               [m.kv[0:64, 2, h * 256:(h + 1) * 256] for h in range(2)] if i == 2 else
                               [m.kv[0:64, 2, 512:KVC], m.ngate[0:64, 2, :]])
                        for (src, b), out in zip(halves, dst):
                            last = dve.tensor_tensor(out, src, b, ALU.add)
                        last.then_inc(s_et, 1)
                    elif i < 2:
                        dve.tensor_tensor(m.v[0:rows, t, 2 * i:2 * i + 2, 0:DV],
                                          ps[0:rows, 0:512].rearrange("p (h v) -> p h v", v=DV),
                                          bias.rearrange("p (h v) -> p h v", v=DV), ALU.add).then_inc(s_et, 1)
                    elif i == 2:
                        dve.tensor_tensor(m.kv[0:rows, t, 0:512], ps[0:rows, 0:512], bias, ALU.add).then_inc(s_et, 1)
                    else:
                        dve.tensor_tensor(m.kv[0:rows, t, 512:KVC], ps[0:rows, 0:256], bias[:, 0:256], ALU.add)
                        dve.tensor_tensor(m.ngate[0:rows, t, :], ps[0:rows, 256:304], bias[:, 256:304],
                                          ALU.add).then_inc(s_et, 1)
                    n += 1


def mlstm_gates(nc, m, a):
    s_w, s_m0, s_qk, s_ev = m.s_wqk, m.sem("m0_in"), m.sem("qk_done"), m.sem("qk_evicted")
    s_abs, s_e, s_ln, s_lf = m.sem("g_abs"), m.sem("g_exp"), m.sem("g_ln"), m.sem("g_dve")
    s_mt, s_wi, s_we, s_cols = m.sem("g_mt"), m.sem("g_winter"), m.sem("g_wend"), m.sem("g_cols_T")
    s_mo, s_out = m.sem("g_mout"), m.sem("g_m_stored")
    with ExitStack() as c:
        lf = c.enter_context(nc.sbuf_tensor("g_lf", [MH, NTOK], FP))
        t0 = c.enter_context(nc.sbuf_tensor("g_t0", [MH, NTOK], FP))
        t1 = c.enter_context(nc.sbuf_tensor("g_t1", [MH, NTOK], FP))
        bsum = c.enter_context(nc.sbuf_tensor("g_b", [MH, NTOK], FP))
        mrow = c.enter_context(nc.sbuf_tensor("g_m", [MH, NTOK], FP))
        m0 = c.enter_context(nc.sbuf_tensor("g_m0", [MH, NTOK], FP))
        m0s = c.enter_context(nc.sbuf_tensor("g_m0s", [MH, NB], FP))
        mt = c.enter_context(nc.sbuf_tensor("g_mtrow", [MH, NTOK], FP))
        wa = c.enter_context(nc.sbuf_tensor("g_wa", [MH, 64], FP))
        we = c.enter_context(nc.sbuf_tensor("g_we", [MH, 64], FP))
        crow = c.enter_context(nc.sbuf_tensor("g_crow", [MH, 3, NTOK], FP))
        mout = c.enter_context(nc.sbuf_tensor("g_mo", [MH, 1 + NB], FP))
        block = c.enter_context(nc.Block())
        r = crow[:, 0, :]
        wq, wk = m.wq, m.wk

        @block.sync
        def _(sp):
            sp.dma_start(m0s[:, :], a.state_m[0].rearrange("b h -> h b"), allow_slow_non_contiguous=True).then_inc(s_m0, 16)
            sp.dma_start(m.n0[:, :], a.state_n[0].rearrange("b h d -> (b h) d")).then_inc(m.s_n0, 16)
            for b in range(NB):
                sp.dma_start(m.ce[:, b, :, 0:DV], a.state_C[0, b].rearrange("h d v -> d h v")).then_inc(m.s_c0, 16)
            sp.wait_ge(s_mo, 1)
            sp.dma_start(a.new_m_p[0].rearrange("b h -> h b"), mout[:, 0:1], allow_slow_non_contiguous=True).then_inc(s_out, 16)
            sp.dma_start(a.new_m_s[0].rearrange("b h -> h b"), mout[:, 1:], allow_slow_non_contiguous=True).then_inc(s_out, 16)
            sp.wait_ge(s_out, 32)

        @block.tensor
        def _(pe):
            pe.wait_ge(s_w, 32)
            for h in range(MH):
                pe.wait_ge(s_ev, 3 * h + 1)
                for i in range(2):
                    last = pe.matmul(m.bank[0][:, 0:NTOK], wq[:, bass.ds(2 * h + i, 1), :], m.xc[:, bass.ds(2 * h + i, 1), :],
                                     start=(i == 0), stop=(i == 1))
                last.then_inc(s_qk, 1)
                pe.wait_ge(s_ev, 3 * h + 2)
                for i in range(2):
                    last = pe.matmul(m.bank[1][:, 0:NTOK], wk[:, bass.ds(2 * h + i, 1), :], m.xc[:, bass.ds(2 * h + i, 1), :],
                                     start=(i == 0), stop=(i == 1))
                last.then_inc(s_qk, 1)
                pe.wait_ge(s_ev, 3 * h + 3)
                for t, n in enumerate(TILE_ROWS):
                    for i in range(2):
                        last = pe.matmul(m.bank[2][0:n, t * 128:(t + 1) * 128], m.xc[:, bass.ds(2 * h + i, 1), t * 128:t * 128 + n],
                                         wk[:, bass.ds(2 * h + i, 1), :], start=(i == 0), stop=(i == 1))
                last.then_inc(s_qk, 1)
            pe.wait_ge(s_we, 2)
            pe.wait_ge(s_e, 2)
            for t, n in enumerate(TILE_ROWS):
                for q in range(3):
                    last = pe.transpose(m.bank[3][0:n, (t * 3 + q) * MH:(t * 3 + q + 1) * MH],
                                        crow[:, q, t * 128:t * 128 + n], m.ident[0:MH, 0:MH])
            last.then_inc(s_cols, 1)

        @block.scalar
        def _(act):
            act.sem_inc(s_ev, 3)
            act.activation(t0[:, :], m.gate_rows[:, 1, :], ACT.Abs).then_inc(s_abs, 1)
            act.wait_ge(s_abs, 1)
            act.activation(t0[:, :], t0[:, :], ACT.Exp, scale=-1.0).then_inc(s_e, 1)
            act.wait_ge(s_e, 1)
            act.activation(t1[:, :], t0[:, :], ACT.Ln, bias=1.0).then_inc(s_ln, 1)
            for h in range(MH):
                act.wait_ge(s_qk, 3 * h + 1)
                act.activation(m.mqT[:, bass.ds(h, 1), :], m.bank[0][:, 0:NTOK], ACT.Copy).then_inc(s_ev, 1)
                act.wait_ge(s_qk, 3 * h + 2)
                act.activation(m.mkT[:, bass.ds(h, 1), :], m.bank[1][:, 0:NTOK], ACT.Copy, scale=DQK ** -0.5).then_inc(s_ev, 1)
                act.wait_ge(s_qk, 3 * h + 3)
                act.activation(m.mk[:, bass.ds(h, 1), 0:2 * DQK], m.bank[2][:, 0:2 * DQK], ACT.Copy, scale=DQK ** -0.5)
                act.activation(m.mk[0:64, bass.ds(h, 1), 2 * DQK:], m.bank[2][0:64, 2 * DQK:3 * DQK], ACT.Copy,
                               scale=DQK ** -0.5).then_inc(s_ev, 1)
                if h == 1:
                    act.wait_ge(s_mt, 1)
                    act.activation(crow[:, 1, :], mt[:, :], ACT.Exp, scale=-1.0).then_inc(s_e, 1)
                    act.activation(m.grow[:, NTOK:NTOK + 64], wa[:, :], ACT.Exp).then_inc(s_wi, 1)
                    act.activation(crow[:, 2, 0:SEQ], r[:, 0:SEQ], ACT.Exp, bias=m.grow[:, SEQ - 1:SEQ]).then_inc(s_we, 1)
                    act.activation(crow[:, 2, SEQ:], we[:, :], ACT.Exp).then_inc(s_we, 1)

        @block.vector
        def _(dve):
            link = Link(dve, s_lf)
            link(dve.memset(m0[:, 0:SEQ], 0.0))
            dve.wait_ge(s_m0, 16)
            link(dve.tensor_copy(m0[:, SEQ:].rearrange("p (b t) -> p b t", t=TS), m0s[:, :].unsqueeze(2).to_broadcast((MH, NB, TS))))
            dve.wait_ge(s_ln, 1)
            link(dve.scalar_tensor_tensor(lf[:, :], m.gate_rows[:, 1, :], 0.0, t1[:, :], ALU.min, ALU.subtract))
            link(dve.tensor_tensor_scan(bsum[:, :], m.seg_mul[:, :], lf[:, :], 0.0, ALU.mult, ALU.add))
            link(dve.tensor_tensor(r, m.gate_rows[:, 0, :], bsum[:, :], ALU.subtract))
            link(dve.tensor_tensor_scan(mrow[:, :], m.seg_add[:, :], r, NEG, ALU.add, ALU.max))
            link(dve.tensor_tensor(mrow[:, :], mrow[:, :], m0[:, :], ALU.max))
            link(dve.tensor_scalar(m.grow[:, 0:NTOK], mrow[:, :], -1.0, None, ALU.mult))
            link(dve.tensor_tensor(mt[:, :], bsum[:, :], mrow[:, :], ALU.add))
            link(dve.tensor_tensor(wa[:, :], m0[:, SEQ:], mrow[:, SEQ:], ALU.subtract))
            negm_end = m.grow[:, SEQ:NTOK].rearrange("p (b t) -> p b t", t=TS)[:, :, TS - 1:TS]
            link(dve.tensor_tensor(we[:, :].rearrange("p (b t) -> p b t", t=TS), r[:, SEQ:].rearrange("p (b t) -> p b t", t=TS),
                                   negm_end.to_broadcast((MH, NB, TS)), ALU.add))
            dve.sem_inc(s_mt, 1)
            link.go(dve.tensor_copy(mout[:, 0:1], mt[:, SEQ - 1:SEQ]))
            link(dve.tensor_copy(mout[:, 1:].unsqueeze(2), mt[:, SEQ:].rearrange("p (b t) -> p b t", t=TS)[:, :, TS - 1:TS]))
            dve.sem_inc(s_mo, 1)
            dve.wait_ge(s_wi, 1)
            dve.tensor_copy(m.grow[:, NTOK + 64:NTOK + 64 + NB].unsqueeze(2),
                            m.grow[:, NTOK:NTOK + 64].rearrange("p (b t) -> p b t", t=TS)[:, :, TS - 1:TS])
            dve.wait_ge(s_cols, 1)
            dve.tensor_copy(m.gcol[:, 0:2, :, :], m.bank[3][:, 0:24].rearrange("p (t q h) -> p t q h", q=3, h=MH))
            dve.tensor_copy(m.gcol[0:64, 2, :, :], m.bank[3][0:64, 24:36].rearrange("p (q h) -> p q h", h=MH))


def mlstm_heads(nc, m, a):
    s_c0, s_n0, s_nT, s_n0e = m.s_c0, m.s_n0, m.sem("n0_T"), m.sem("n0_ev")
    s_nb, s_s, s_arg, s_w = m.sem("bcast_done"), m.sem("qk_scores"), m.sem("warg"), m.sem("wexp")
    s_nbf, s_pt, s_kw, s_num = m.sem("bcast_read"), m.sem("pt_ready"), m.sem("kw_ready"), m.sem("num_done")
    s_cp, s_cpe, s_cs, s_cse = m.sem("Cp_done"), m.sem("Cp_evicted"), m.sem("Cs_done"), m.sem("Cs_evicted")
    s_h, s_sq, s_numf, s_chain = m.sem("h_ready"), m.sem("h_sq"), m.sem("num_read"), m.sem("heads_dve")
    s_out, s_qm, s_rt, s_hn = m.sem("C_out"), m.sem("qm_zero"), m.sem("hrms_sqrt"), m.sem("hn_ready")
    s_hT, s_hTe, s_rs, s_nc, s_nct, s_nce = (m.sem("hT"), m.sem("hT_ev"), m.sem("hrms_ms"), m.sem("ncol"),
                                             m.sem("ncol_T"), m.sem("ncol_ev"))
    s_wc, s_cpo = m.sem("wcmp_in"), [m.sem(f"Cp_out{p}") for p in range(2)]
    QW = 136
    with ExitStack() as c:
        def sb(name, shape):
            return c.enter_context(nc.sbuf_tensor(name, shape, FP))

        ce, n0 = m.ce, m.n0
        cp = [sb(f"prompt_c{p}", [128, VX]) for p in range(2)]
        ncol = sb("ncols", [128, MH + NB * MH])
        nrow = sb("nrows", [MH + NB * MH, DQK])
        wi = sb("w_intra", [128, 3 * 128])
        wis = sb("w_intra_s", [64, 64])
        pt = sb("pt", [128, 3 * 128])
        pts = sb("pt_s", [64, 128])
        qm = sb("qm", [128, NB * QW])
        dec = [sb(f"decay{p}", [128, NB]) for p in range(2)]
        wem = sb("wend_m", [64, NB])
        kws = [sb("kw_s0", [64, NB, DQK]), m.reused[0:64, NT * MH * DV:NT * MH * DV + NB * DQK].rearrange("p (b d) -> p b d", d=DQK)]
        den = sb("den", [128, NT])
        ht = m.reused[:, 0:NT * MH * DV].rearrange("p (t h v) -> p t h v", t=NT, h=MH)
        o = NT * MH * DV + NB * DQK
        kw = m.reused[:, o:o + 2 * DQK].rearrange("p (t d) -> p t d", d=DQK)
        junk = m.reused[:, o + 2 * DQK:o + 2 * DQK + DV]
        ss = sb("h_ss", [128, NT, MH])
        block = c.enter_context(nc.Block())

        @block.gpsimd
        def _(pool):
            for g in range(2):
                pool.memset(m.wc[g * HD:(g + 1) * HD, :, (1 - g) * HD:(2 - g) * HD], 0.0)

        @block.sync
        def _(sp):
            for g in range(2):
                for i in range(2):
                    sp.dma_start(m.wc[g * HD:(g + 1) * HD, i * CMP:(i + 1) * CMP, g * HD:(g + 1) * HD],
                                 a.w_cmp[0, i].rearrange("r d e -> d r e")).then_inc(s_wc, 16)
            for h in range(MH):
                sp.wait_ge(s_cpe, h + 1)
                sp.dma_start(a.new_C_p[0, 0, h], cp[h % 2][:, 0:DV]).then_inc(s_cpo[h % 2], 16)
                sp.wait_ge(s_cse, NB * (h + 1))
                sp.dma_start(a.new_C_s[0, :, h].rearrange("b d v -> d b v"), ce[:, :, h, 0:DV]).then_inc(s_out, 16)
            sp.wait_ge(s_nce, 1)
            sp.dma_start(a.new_n_p[0, 0], nrow[0:MH, :]).then_inc(s_out, 16)
            sp.dma_start(a.new_n_s[0].rearrange("b h d -> (b h) d"), nrow[MH:, :]).then_inc(s_out, 16)
            sp.wait_ge(s_out, 16 * (MH + 2))
            for p in range(2):
                sp.wait_ge(s_cpo[p], 16 * MH // 2)
            sp.wait_ge(s_wc, 64)

        @block.tensor
        def _(pe):
            pe.wait_ge(s_n0, 16)
            pe.transpose(m.bank[5][:, 0:NB * MH], n0[:, :], m.ident[0:NB * MH, 0:NB * MH]).then_inc(s_nT, 1)
            pe.wait_ge(s_n0e, 1)
            pe.wait_ge(s_c0, 16 * NB)
            pe.wait_ge(s_qm, 1)

            def scores(h):
                if h > 0:
                    pe.wait_ge(s_nbf, h)
                pe.matmul(m.bank[0][:, 0:392], m.ident[0:MH, h:h + 1].to_broadcast((MH, 128)), m.grow[:, :],
                          start=True, stop=True).then_inc(s_nb, 1)
                if h > 0:
                    pe.wait_ge(s_pt, h)
                for o, k0, kn, q0, qn in ((0, 0, 128, 0, 256), (256, 128, 128, 128, 128), (384, 256, 64, 256, 64)):
                    last = pe.matmul(m.bank[1][0:kn, o:o + qn], m.mkT[:, h, k0:k0 + kn], m.mqT[:, h, q0:q0 + qn], start=True, stop=True)
                last.then_inc(s_s, 1)

            scores(0)
            for h in range(MH):
                v = [m.v[0:n, t, h, :] for t, n in enumerate(TILE_ROWS)]
                pe.wait_ge(s_pt, h + 1)
                if h > 0:
                    pe.wait_ge(s_numf, 3 * h)
                pe.matmul(m.bank[2][:, 0:VX], pt[:, 0:128], v[0], start=True, stop=True).then_inc(s_num, 1)
                pe.matmul(m.bank[3][:, 0:VX], pt[:, 128:256], v[0], start=True, stop=False)
                pe.matmul(m.bank[3][:, 0:VX], pt[:, 256:384], v[1], start=False, stop=True).then_inc(s_num, 1)
                pe.matmul(m.bank[4][:, 0:VX], pts[:, :], v[2], start=True, stop=False)
                for b in range(NB):
                    last = pe.matmul(m.bank[4][:, 0:VX], qm[:, 128 * b:128 * b + 128], ce[:, b, h, :],
                                     start=False, stop=(b == NB - 1))
                last.then_inc(s_num, 1)
                pe.wait_ge(s_kw, h + 1)
                if h > 0:
                    pe.wait_ge(s_cpe, h)
                for t in range(2):
                    last = pe.matmul(m.bank[5][:, 0:VX], kw[:, t, :], v[t], start=(t == 0), stop=(t == 1))
                last.then_inc(s_cp, 1)
                if h + 1 < MH:
                    scores(h + 1)
                for b in range(NB):
                    if NB * h + b >= 2:
                        pe.wait_ge(s_cse, NB * h + b - 1)
                    pe.matmul(m.bank[6 + b % 2][:, 0:VX], kws[h % 2][:, b, :], v[2], start=True, stop=True).then_inc(s_cs, 1)
            pe.wait_ge(s_nc, 1)
            pe.transpose(m.bank[0][0:MH + NB * MH, 0:128], ncol[:, :], m.ident[:, :]).then_inc(s_nct, 1)
            pe.wait_ge(s_hn, 1)
            for k in range(KD):
                if k >= 2:
                    pe.wait_ge(s_hTe, k - 1)
                for t, n in enumerate(TILE_ROWS):
                    last = pe.transpose(m.bank[2 + k % 2][:, t * 128:t * 128 + n],
                                        ht[0:n, t, k // 2, (k % 2) * 128:(k % 2 + 1) * 128], m.ident[0:n, 0:n])
                last.then_inc(s_hT, 1)

        @block.scalar
        def _(act):
            act.wait_ge(s_nT, 1)
            act.activation(ce[:, :, :, DV:VX].rearrange("p b h o -> p (b h) o"), m.bank[5][:, 0:NB * MH].unsqueeze(2),
                           ACT.Copy).then_inc(s_n0e, 1)

            def weights(h):
                act.wait_ge(s_arg, h + 1)
                act.activation(wi[:, :], wi[:, :], ACT.Exp)
                act.activation(wis[:, :], wis[:, :], ACT.Exp).then_inc(s_w, 1)

            weights(0)
            for h in range(MH):
                act.wait_ge(s_cp, h + 1)
                if h >= 2:
                    act.wait_ge(s_cpo[h % 2], 16 * (h // 2))
                act.activation(cp[h % 2][:, :], m.bank[5][:, 0:VX], ACT.Copy)
                act.activation(ncol[:, h:h + 1], m.bank[5][:, DV:VX], ACT.Copy).then_inc(s_cpe, 1)
                if h + 1 < MH:
                    weights(h + 1)
                act.wait_ge(s_h, h + 1)
                for t, n in enumerate(TILE_ROWS):
                    if h + t > 0:
                        act.wait_ge(s_sq, NT * h + t)
                    act.activation(junk[0:n, :], ht[0:n, t, h, :], ACT.Square, accum_out=ss[0:n, t, h:h + 1]).then_inc(s_sq, 1)
            act.wait_ge(s_rs, 1)
            act.activation(ss[:, :, :], ss[:, :, :], ACT.Sqrt).then_inc(s_rt, 1)

        @block.vector
        def _(dve):
            link = Link(dve, s_chain)
            link.go(dve.memset(ss[:, :, :], 1.0))
            link.go(dve.memset(pts[:, :], 0.0))
            link(dve.memset(qm[:, :], 0.0))
            dve.sem_inc(s_qm, 1)

            def gates(h):
                col = lambda n, t, q: m.gcol[0:n, t, q, h:h + 1]
                dve.wait_ge(s_nb, h + 1)
                nb = m.bank[0]
                link.go(dve.scalar_tensor_tensor(wi[:, 0:128], nb[:, 0:128], col(128, 0, 0), m.causal_st[:, :], ALU.add, ALU.add))
                link.go(dve.tensor_scalar(wi[:, 128:256], nb[:, 128:256], col(128, 0, 0), None, ALU.add))
                link.go(dve.scalar_tensor_tensor(wi[:, 256:384], nb[:, 128:256], col(128, 1, 0), m.causal_st[:, :], ALU.add, ALU.add))
                link(dve.scalar_tensor_tensor(wis[:, :], nb[0:64, 256:320], col(64, 2, 0), m.same_seq[:, :], ALU.add, ALU.add))
                dve.sem_inc(s_arg, 1)
                link.go(dve.tensor_tensor(qm[:, :].rearrange("p (b x) -> p b x", x=QW)[:, :, 0:TS],
                                          m.mqT[:, h, SEQ:].rearrange("p (b t) -> p b t", t=TS),
                                          nb[:, NTOK:NTOK + 64].rearrange("p (b t) -> p b t", t=TS), ALU.mult))
                link.go(dve.tensor_copy(dec[h % 2][:, :], nb[:, NTOK + 64:NTOK + 64 + NB]))
                link(dve.tensor_scalar(wem[:, :], m.seq_onehot[:, :], col(64, 2, 2), None, ALU.mult))
                dve.sem_inc(s_nbf, 1)
                if h > 0:
                    dve.wait_ge(s_cp, h)
                for t in range(2):
                    link.go(dve.tensor_scalar(kw[:, t, :], m.mk[:, h, t * DQK:(t + 1) * DQK], col(128, t, 2), None, ALU.mult))
                link(dve.tensor_tensor(kws[h % 2][:, :, :], m.mk[0:64, h:h + 1, 2 * DQK:].to_broadcast((64, NB, DQK)),
                                       wem[:, :].unsqueeze(2).to_broadcast((64, NB, DQK)), ALU.mult))
                dve.sem_inc(s_kw, 1)

            def weigh_scores(h):
                dve.wait_ge(s_w, h + 1)
                dve.wait_ge(s_s, h + 1)
                link.go(dve.tensor_tensor(pt[:, :], m.bank[1][:, 0:384], wi[:, :], ALU.mult))
                link(dve.tensor_tensor(pts[:, 0:64], m.bank[1][0:64, 384:448], wis[:, :], ALU.mult))
                dve.sem_inc(s_pt, 1)

            gates(0)
            weigh_scores(0)
            for h in range(MH):
                for t, n in enumerate(TILE_ROWS):
                    dve.wait_ge(s_num, 3 * h + t + 1)
                    ps = m.bank[2 + t]
                    link(dve.scalar_tensor_tensor(den[0:n, t:t + 1], ps[0:n, DV:VX], -1.0, m.gcol[0:n, t, 1, h:h + 1], ALU.mult, ALU.max))
                    link(dve.tensor_tensor(den[0:n, t:t + 1], ps[0:n, DV:VX], den[0:n, t:t + 1], ALU.max))
                    link(dve.reciprocal(den[0:n, t:t + 1], den[0:n, t:t + 1]))
                    link(dve.tensor_scalar(ht[0:n, t, h, :], ps[0:n, 0:DV], den[0:n, t:t + 1], None, ALU.mult))
                    dve.sem_inc(s_numf, 1)
                dve.sem_inc(s_h, 1)
                if h + 1 < MH:
                    gates(h + 1)
                for b in range(NB):
                    if b == NB // 2 and h + 1 < MH:
                        weigh_scores(h + 1)
                    dve.wait_ge(s_cs, NB * h + b + 1)
                    dve.scalar_tensor_tensor(ce[:, b, h, :], ce[:, b, h, :], dec[h % 2][:, b:b + 1], m.bank[6 + b % 2][:, 0:VX],
                                             ALU.mult, ALU.add).then_inc(s_cse, 1)
                dve.wait_ge(s_cse, NB * (h + 1))
                link.go(dve.tensor_copy(ncol[:, MH:].rearrange("p (b h) -> p b h", h=MH)[:, :, h:h + 1], ce[:, :, h, DV:VX]))
            link.wait()
            dve.wait_ge(s_cpe, MH)
            dve.sem_inc(s_nc, 1)
            dve.wait_ge(s_sq, 3 * MH)
            link(dve.tensor_scalar(ss[:, :, :], ss[:, :, :], 1.0 / DV, EPS, ALU.mult, ALU.add))
            dve.sem_inc(s_rs, 1)
            dve.wait_ge(s_rt, 1)
            link(dve.reciprocal(ss[:, :, :], ss[:, :, :]))
            for t, n in enumerate(TILE_ROWS):
                for h in range(MH):
                    link.go(dve.tensor_scalar(ht[0:n, t, h, :], ht[0:n, t, h, :], ss[0:n, t, h:h + 1], None, ALU.mult))
            link.wait()
            dve.sem_inc(s_hn, 1)
            dve.wait_ge(s_nct, 1)
            dve.tensor_copy(nrow[:, :], m.bank[0][0:MH + NB * MH, 0:128]).then_inc(s_nce, 1)
            for k in range(KD):
                dve.wait_ge(s_hT, k + 1)
                dve.scalar_tensor_tensor(m.hmT[:, k, :], m.bank[2 + k % 2][:, 0:NTOK], m.par[:, 5, k:k + 1],
                                         m.zf[:, KD + k, :], ALU.mult, ALU.mult).then_inc(s_hTe, 1)


def nsa_prepare(nc, m, a):
    s_zr, s_b = m.sem("bcmp_zero"), m.sem("bcmp_in")
    s_t, s_te, s_c, s_ce, s_ct = m.sem("kT_done"), m.sem("kT_ev"), m.sem("cmpp_done"), m.sem("cmpp_ev"), m.sem("ckp_T")
    with ExitStack() as c:
        ccp = c.enter_context(nc.sbuf_tensor("ccp", [128, 128], FP))
        block = c.enter_context(nc.Block())

        @block.sync
        def _(sp):
            sp.dma_start(m.pages[:, :], a.page_table.rearrange("(o b) n -> o (b n)", o=1)).then_inc(m.s_pages, 16)
            sp.wait_ge(m.s_pages, 16)

        @block.scalar
        def _(act):
            act.wait_ge(s_zr, 1)
            for g in range(2):
                act.dma_start(m.bcmp_row[0:1, :].rearrange("p (c g e) -> p g c e", c=2, g=2)[:, g],
                              a.b_cmp.rearrange("l c e -> l c e")).then_inc(s_b, 16)
            act.wait_ge(s_c, 1)
            for i in range(2):
                rows = slice(i * 64, i * 64 + NC_P + 1)
                last = act.activation(ccp[rows, :], m.bank[4][rows, 0:128], ACT.Copy)
            last.then_inc(s_ce, 1)
            act.wait_ge(s_ce, 1)
            act.activation(m.cvp[:, :], ccp[0:NC_P, :], ACT.Copy)
            act.wait_ge(s_ct, 1)
            act.activation(m.ckp[:, :], m.bank[5][:, 0:NC_P], ACT.Copy)

        @block.tensor
        def _(pe):
            for i, off in enumerate((0, 128, 256, 512)):
                for t, n in enumerate(TILE_ROWS):
                    last = pe.transpose(m.bank[i][:, t * 128:t * 128 + n], m.kv[0:n, t, off:off + 128], m.ident[0:n, 0:n])
                last.then_inc(s_t, 1)
            pe.wait_ge(s_te, 4)
            pe.wait_ge(s_b, 32)
            rows = lambda i: m.bank[4][(1 - i) * 64:(1 - i) * 64 + NC_P + 1, 0:128]
            for i in range(2):
                pe.matmul(rows(i), m.ones[:, 0:NC_P + 1], m.bcmp_row[:, i * 128:(i + 1) * 128], start=True, stop=False)
            for r in range(CMP):
                for i in range(2):
                    last = pe.matmul(rows(i), m.kT[:, i, r:r + CST * NC_P + 1:CST], m.wc[:, i * CMP + r, :],
                                     start=False, stop=(r == CMP - 1))
            last.then_inc(s_c, 1)
            pe.wait_ge(s_ce, 1)
            pe.matmul(m.bank[5][:, 0:NC_P + 1], ccp[64:64 + NC_P + 1, :], m.ident[64:64 + NC_P + 1, 64:64 + NC_P + 1],
                      start=True, stop=True).then_inc(s_ct, 1)

        @block.vector
        def _(dve):
            for i in range(4):
                dve.wait_ge(s_t, i + 1)
                dve.tensor_copy(m.kT[:, i, :], m.bank[i][:, 0:NTOK]).then_inc(s_te, 1)

        @block.gpsimd
        def _(pool):
            pool.memset(m.bcmp_row[:, :], 0.0).then_inc(s_zr, 1)
            pool.memset(m.qbd[:, :], 0.0)
            pool.memset(m.key_mask[:, 0:128], 0.0)
            pool.tensor_copy(m.key_mask[:, 128:256], m.causal_tk[:, :])


def sample_loader(sp, m, a):
    def load(b, dst, win, cols, kind, sem):
        sp.dma_start(win[:, :, :], a.cache_win_kv[0, bass.ds(b, 1), :, kind].rearrange("b (w r) g d -> r (b w) (g d)", r=128)
                     ).then_inc(sem, 16)
        for j in range(NPG):
            page = sp.value_load(m.pages[0:1, bass.ds(b * NPG + j, 1)], min_val=0, max_val=a.cache_kv.shape[0] - 1)
            sp.dma_start(dst[:, j, :], a.cache_kv[bass.ds(page, 1)].rearrange("n r l c g d -> r (n l c g d)")[:, cols]
                         ).then_inc(sem, 16)

    def load_k(b, p):
        load(b, m.pages_k[p], m.win_k[p], slice(0, 384), 0, m.s_pa[p])

    def load_v(b, p):
        load(b, m.pages_v[p], m.win_v[p], slice(384, 512), 1, m.s_pb[p])

    return load_k, load_v


def nsa_prompt(nc, m, a):
    s_q, s_sc, s_msk = m.sem("np_q"), m.sem("np_scores"), m.sem("np_masked")
    s_nm, s_ex, s_dg, s_tp = m.sem("np_negmax"), m.sem("np_exp"), m.sem("np_diag"), m.sem("np_T")
    s_ea, s_ed, s_pv, s_oe = m.sem("np_ev_act"), m.sem("np_ev_dve"), m.sem("np_pv"), m.sem("np_out")
    s_chain = m.sem("np_dve")
    s_g1, s_g2, s_out = m.sem("gate_out"), m.sem("gate_in"), m.sem("kv_out")
    gates = nc.dram_tensor("gates_scratch", (NB * TS, 48), FP).ap()
    FIRST, PER = 24, 18
    with ExitStack() as c:
        def sb(name, shape):
            return c.enter_context(nc.sbuf_tensor(name, shape, FP))

        qs = sb("np_qs", [128, 128])
        s = [sb(f"np_s{p}", [128, 2, 2, SEQ]) for p in range(2)]
        sc = [sb(f"np_sc{p}", [128, 2, NC_P]) for p in range(2)]
        mx = [sb(f"np_mx{p}", [128, 6]) for p in range(2)]
        sm = [sb(f"np_sm{p}", [128, 6]) for p in range(2)]
        dg = sb("np_dg", [128, 6, 128])
        pt = sb("np_pt", [128, 2, 512])
        ptc = sb("np_ptc", [NC_P, 2, 128])
        block = c.enter_context(nc.Block())

        def turns(eng, turn):
            at = lambda U: (U // 8, U % 8, U % 2, U) if U < 16 else None
            for T in range(2):
                with eng.Fori(0, 3) as i:
                    for p in range(2):
                        turn(*((T, 2 * i + (p + d), (p + d) % 2, 2 * i + (8 * T + p + d)) for d in range(3)))
                for U in (8 * T + 6, 8 * T + 7):
                    turn(at(U), at(U + 1), at(U + 2))

        first, second = (0, 0, 0, 0), (0, 1, 1, 1)

        @block.sync
        def _(sp):
            load_k, load_v = sample_loader(sp, m, a)
            for p in range(2):
                load_k(p, p)
                load_v(p, p)
            sp.dma_start(gates, m.ngate[0:64, 2, :]).then_inc(s_g1, 16)
            sp.wait_ge(s_g1, 16)
            for h in range(16):
                sp.dma_start(m.gate_s[h * TS:(h + 1) * TS, :, :],
                             gates.rearrange("(b t) (h r) -> h t b r", t=TS, r=3)[h]).then_inc(s_g2, 16)
            kvp = a.new_kv_p.rearrange("o (t p) l c g d -> t p (o l c g d)", p=128)
            wnp = a.new_win_p.rearrange("l o (t p) c g d -> t p (l o c g d)", p=128)
            for t in range(2):
                sp.dma_start(kvp[t], m.kv[:, t, 0:512]).then_inc(s_out, 16)
                sp.dma_start(wnp[t], m.kv[:, t, 512:KVC]).then_inc(s_out, 16)
            sp.dma_start(a.new_kv_s.rearrange("b t l c g d -> (b t) (l c g d)"), m.kv[0:64, 2, 0:512]).then_inc(s_out, 16)
            nws = a.new_win_s[0].rearrange("b w c g d -> b w (c g d)")
            sp.dma_start(nws[:, 0:WIN - TS, :], a.cache_win_kv[0].rearrange("b w c g d -> b w (c g d)")[:, TS:, :]).then_inc(s_out, 16)
            for b in range(NB):
                sp.dma_start(nws[b, WIN - TS:, :], m.kv[b * TS:(b + 1) * TS, 2, 512:KVC]).then_inc(s_out, 16)
            sp.wait_ge(s_g2, 256)
            sp.wait_ge(s_out, 16 * (6 + NB))

        @block.gpsimd
        def _(pool):
            def queries(T, u, p, U):
                pool.tensor_copy(qs[:, :], m.zf[:, bass.ds(u + 32, 1), T * 128:(T + 1) * 128]).then_inc(s_q, 1)

            def turn(this, after, then):
                if then:
                    pool.wait_ge(s_sc, this[3] + 2)
                    queries(*then)
            queries(*first)
            pool.wait_ge(s_sc, 1)
            queries(*second)
            turns(pool, turn)

        @block.tensor
        def _(pe):
            def scores(T, u, p, U):
                nk = 128 * (T + 1)
                pe.wait_ge(s_q, U + 1)
                if not isinstance(U, int) or U > 0:
                    pe.wait_ge(s_msk, U)
                for g in range(2):
                    q = qs[g * HD:(g + 1) * HD, :]
                    for i, kind in enumerate((2, 3)):
                        pe.matmul(m.bank[g][:, i * nk:(i + 1) * nk], q, m.kT[g * HD:(g + 1) * HD, kind, 0:nk],
                                  start=True, stop=True)
                    last = pe.matmul(m.bank[(2, 7)[g]][:, 0:NC_P], q, m.ckp[g * HD:(g + 1) * HD, :],
                                     start=True, stop=True)
                last.then_inc(s_sc, 1)

            def turn(this, after, then):
                T, u, p, U = this
                pe.wait_ge(s_dg, U + 1)
                pe.wait_ge(s_ea, U + 1)
                pe.wait_ge(s_ed, U + 1)
                for g in range(2):
                    for br in range(2):
                        for ch in range(T + 1):
                            o = (br * (T + 1) + ch) * 128
                            pe.matmul(m.bank[3 + g][:, o:o + 128], s[p][:, g, br, ch * 128:(ch + 1) * 128],
                                      dg[:, 2 * g + br, :], start=True, stop=True)
                    last = pe.matmul(m.bank[5][0:NC_P, g * 128:(g + 1) * 128], sc[p][:, g, :], dg[:, 4 + g, :],
                                     start=True, stop=True)
                last.then_inc(s_tp, 1)
                if then:
                    scores(*then)
                pe.wait_ge(s_ea, U + 2)
                pe.wait_ge(s_ed, U + 2)
                pe.wait_ge(s_oe, U + 1)
                out = [m.bank[6][g * HD:(g + 1) * HD, 0:128] for g in range(2)]
                for br, off in enumerate((384, 640)):
                    for ch in range(T + 1):
                        o = (br * (T + 1) + ch) * 128
                        for g in range(2):
                            pe.matmul(out[g], m.kv[:, ch, off + g * HD:off + (g + 1) * HD], pt[:, g, o:o + 128],
                                      start=(br + ch == 0), stop=False)
                for g in range(2):
                    last = pe.matmul(out[g], m.cvp[:, g * HD:(g + 1) * HD], ptc[:, g, :], start=False, stop=True)
                last.then_inc(s_pv, 1)

            scores(*first)
            scores(*second)
            turns(pe, turn)

        @block.scalar
        def _(act):
            act.sem_inc(s_ea, 1)
            act.sem_inc(s_oe, 1)

            def exps(T, u, p, U):
                nk = 128 * (T + 1)
                act.wait_ge(s_nm, U + 1)
                for g in range(2):
                    for br in range(2):
                        act.activation(s[p][:, g, br, 0:nk], s[p][:, g, br, 0:nk], ACT.Exp,
                                       bias=mx[p][:, 2 * g + br:2 * g + br + 1], accum_out=sm[p][:, 2 * g + br:2 * g + br + 1])
                for g in range(2):
                    last = act.activation(sc[p][:, g, :], sc[p][:, g, :], ACT.Exp, bias=mx[p][:, 4 + g:5 + g],
                                          accum_out=sm[p][:, 4 + g:5 + g])
                last.then_inc(s_ex, 1)

            def turn(this, after, then):
                T, u, p, U = this
                nk = 128 * (T + 1)
                act.wait_ge(s_tp, U + 1)
                act.activation(ptc[:, :, :], m.bank[5][0:NC_P, 0:256].rearrange("p (g t) -> p g t", g=2), ACT.Copy)
                act.activation(pt[:, 0, 0:2 * nk], m.bank[3][:, 0:2 * nk], ACT.Copy).then_inc(s_ea, 1)
                if then:
                    exps(*then)
                act.wait_ge(s_pv, U + 1)
                act.activation(m.hnT[:, bass.ds(u, 1), T * 128:(T + 1) * 128], m.bank[6][:, 0:128], ACT.Copy).then_inc(s_oe, 1)

            exps(*first)
            exps(*second)
            turns(act, turn)

        @block.vector
        def _(dve):
            link = Link(dve, s_chain)
            dve.sem_inc(s_ed, 1)

            def mask_and_max(T, u, p, U):
                nk = 128 * (T + 1)
                dve.wait_ge(s_sc, U + 1)
                for g in range(2):
                    link.go(dve.tensor_tensor(s[p][:, g, :, 0:nk], m.bank[g][:, 0:2 * nk].rearrange("p (r k) -> p r k", r=2),
                                              m.key_mask[:, SEQ - nk:SEQ].unsqueeze(1).to_broadcast((128, 2, nk)), ALU.add))
                    link.go(dve.tensor_tensor(sc[p][:, g, :], m.bank[(2, 7)[g]][:, 0:NC_P], m.cmp_mask[:, T, :], ALU.add))
                link.wait()
                dve.sem_inc(s_msk, 1)
                link.go(dve.tensor_reduce(mx[p][:, 0:4], s[p][:, :, :, 0:nk], AX.X, ALU.max))
                link(dve.tensor_reduce(mx[p][:, 4:6], sc[p][:, :, :], AX.X, ALU.max))
                link(dve.tensor_scalar(mx[p][:, :], mx[p][:, :], NEG_CLAMP, -1.0, ALU.max, ALU.mult))
                dve.sem_inc(s_nm, 1)

            def scale(T, u, p, U):
                dve.wait_ge(s_ex, U + 1)
                link(dve.tensor_scalar(sm[p][:, :], sm[p][:, :], TINY, None, ALU.max))
                link(dve.reciprocal(sm[p][:, :], sm[p][:, :]))
                gate = m.ngate[:, T, :].rearrange("p (g j r) -> p g j r", g=2, r=3)
                link.go(dve.tensor_tensor(sm[p][:, 0:4].rearrange("p (g r) -> p g r", g=2), sm[p][:, 0:4].rearrange("p (g r) -> p g r", g=2),
                                          gate[:, :, bass.ds(u, 1), 1:3].rearrange("p g j r -> p g (j r)"), ALU.mult))
                link(dve.tensor_tensor(sm[p][:, 4:6], sm[p][:, 4:6],
                                       gate[:, :, bass.ds(u, 1), 0:1].rearrange("p g j r -> p g (j r)").rearrange("p g r -> p (g r)"), ALU.mult))
                for i in range(6):
                    link.go(dve.tensor_scalar(dg[:, i, :], m.ident[:, :], sm[p][:, i:i + 1], None, ALU.mult))
                link.wait()
                dve.sem_inc(s_dg, 1)

            def turn(this, after, then):
                T, u, p, U = this
                nk = 128 * (T + 1)
                if after:
                    link.base, link.n = U * PER + FIRST, 0
                dve.wait_ge(s_tp, U + 1)
                link(dve.tensor_copy(pt[:, 1, 0:2 * nk], m.bank[4][:, 0:2 * nk]))
                dve.sem_inc(s_ed, 1)
                if after:
                    scale(*after)
                if then:
                    mask_and_max(*then)
                assert not then or link.n == PER, link.n

            mask_and_max(*first)
            mask_and_max(*second)
            scale(*first)
            turns(dve, turn)


def nsa_sample(nc, m, a):
    s_q, s_t, s_te, s_c, s_ce, s_ct = m.sem("ns_q"), m.sem("ns_T"), m.sem("ns_T_ev"), m.sem("ns_cmp"), m.sem("ns_cmp_ev"), m.sem("ns_ckT")
    s_sc, s_pc, s_imp = m.sem("ns_scores"), m.sem("ns_pcmp"), m.sem("ns_imp")
    s_cm, s_ec, s_nm, s_ex = m.sem("ns_cmax"), m.sem("ns_cexp"), m.sem("ns_negmax"), m.sem("ns_exp")
    s_dg, s_p, s_pe_, s_pv, s_o = m.sem("ns_diag"), m.sem("ns_pT"), m.sem("ns_pT_ev"), m.sem("ns_pv"), m.sem("ns_out")
    s_chain, s_pd = m.sem("ns_dve"), m.sem("ns_pT_ev_dve")
    NS1, NS2, NS3, NS4 = PAST, PAST + 64, PAST + 64 + WIN, PAST + 64 + WIN + 64
    PER = 25
    with ExitStack() as c:
        def sb(name, shape):
            return c.enter_context(nc.sbuf_tensor(name, shape, FP))

        pa, pb, wk, wv, s_pa, s_pb = m.pages_k, m.pages_v, m.win_k, m.win_v, m.s_pa, m.s_pb
        kT = sb("ns_kT", [128, 3 * PAST + WIN])
        cc = [sb(f"ns_cc{p}", [128, 128]) for p in range(2)]
        ck = sb("ns_ck", [128, NC_S])
        s = sb("ns_s", [128, NS4])
        pc = sb("ns_pc", [128, NC_S])
        pen = sb("ns_pen", [128, 16])
        imp = sb("ns_imp", [128, 14])
        st = sb("ns_st", [128, 8])
        dg = sb("ns_dg", [128, 3, 128])
        pt = sb("ns_pt", [128, 15, 128])
        block = c.enter_context(nc.Block())

        def turns(eng, turn):
            with eng.Fori(0, NB // 2 - 1) as i:
                for p in range(2):
                    turn(2 * i + p, p, True)
            turn(NB - 2, 0, True)
            turn(NB - 1, 1, False)

        @block.sync
        def _(sp):
            load_k, load_v = sample_loader(sp, m, a)
            load_branch_weights(sp, m, a, m.wb0, 0)
            with sp.Fori(0, NB // 2 - 1) as i:
                for p in range(2):
                    b = 2 * i + p
                    sp.wait_ge(s_t, 7 * b + 7)
                    load_k(b + 2, p)
                    sp.wait_ge(s_pv, b + 1)
                    load_v(b + 2, p)

        @block.gpsimd
        def _(pool):
            def queries(b):
                for g in range(2):
                    pool.tensor_copy(m.qbd[g * HD:(g + 1) * HD, g * 64:(g + 1) * 64].rearrange("p (h t) -> p h t", t=TS),
                                     m.zf[g * HD:(g + 1) * HD, 32:40, bass.ds(b * TS + SEQ, TS)]).then_inc(s_q, 1)

            def turn(b, p, more):
                if more:
                    pool.wait_ge(s_sc, 2 * b + 2)
                    queries(b + 1)
            queries(0)
            turns(pool, turn)

        @block.tensor
        def _(pe):
            def transposes(b, p, first, last_f):
                if first == 0:
                    pe.wait_ge(s_pa[p], (b - p) * 8 * (NPG + 1) + 16 * (NPG + 1))
                for f in range(first, last_f):
                    pe.wait_ge(s_te, 7 * b + f + 1)
                    for j in range(4):
                        src = (pa[p][:, (f % 2) * 4 + j, (f // 2) * 128:(f // 2 + 1) * 128] if f < 6 else wk[p][:, j, :])
                        last = pe.transpose(m.bank[(7 * p + f) % 2][:, j * 128:(j + 1) * 128], src, m.ident[:, :])
                    last.then_inc(s_t, 1)

            def compress(b):
                pe.wait_ge(s_te, 7 * b + 6)
                rows = lambda i: m.bank[2][(1 - i) * 64:(2 - i) * 64, 0:128]
                for i in range(2):
                    pe.matmul(rows(i), m.ones[:, 0:64], m.bcmp_row[:, i * 128:(i + 1) * 128], start=True, stop=False)
                for r in range(CMP):
                    for i in range(2):
                        last = pe.matmul(rows(i), kT[:, i * PAST + r:i * PAST + r + CST * 63 + 1:CST], m.wc[:, i * CMP + r, :],
                                         start=False, stop=(r == CMP - 1))
                last.then_inc(s_c, 1)

            def transpose_ck(b, p):
                pe.wait_ge(s_ce, 2 * b + 1)
                pe.matmul(m.bank[2][:, 128:192], cc[p][64:128, :], m.ident[64:128, 64:128], start=True, stop=True).then_inc(s_ct, 1)

            def scores(b):
                pe.wait_ge(s_ce, 2 * b + 2)
                pe.wait_ge(s_q, 2 * b + 2)
                q = m.qbd[:, :]
                pe.matmul(m.bank[7][:, 0:NC_S], q, ck[:, :], start=True, stop=True)
                pe.matmul(m.bank[7][:, 64:128], q, m.kT[:, 2, SEQ:], start=True, stop=True)
                pe.matmul(m.bank[7][:, 128:192], q, m.kT[:, 3, SEQ:], start=True, stop=True).then_inc(s_sc, 1)
                pe.wait_ge(s_te, 7 * b + 9)
                pe.matmul(m.bank[4][:, :], q, kT[:, 2 * PAST:2 * PAST + 512], start=True, stop=True)
                pe.matmul(m.bank[5][:, :], q, kT[:, 2 * PAST + 512:3 * PAST], start=True, stop=True)
                pe.matmul(m.bank[6][:, :], q, kT[:, 3 * PAST:], start=True, stop=True).then_inc(s_sc, 1)

            def turn(b, p, more):
                if more:
                    transposes(b + 1, 1 - p, 0, 4)
                pe.wait_ge(s_pc, b + 1)
                pe.wait_ge(s_o, b + 1)
                pe.matmul(m.bank[3][:, 0:NC_S], m.peer[:, :], pc[:, :], start=True, stop=True).then_inc(s_imp, 1)
                if more:
                    transposes(b + 1, 1 - p, 4, 7)
                    compress(b + 1)
                pe.wait_ge(s_dg, b + 1)
                for o in range(8):
                    pe.matmul(m.bank[4 + o // 4][:, (o % 4) * 128:(o % 4 + 1) * 128], s[:, o * 128:(o + 1) * 128], dg[:, 0, :],
                              start=True, stop=True)
                for o in range(4):
                    pe.matmul(m.bank[6][:, o * 128:(o + 1) * 128], s[:, NS2 + o * 128:NS2 + (o + 1) * 128], dg[:, 1, :],
                              start=True, stop=True)
                pe.matmul(m.bank[7][0:64, 0:128], s[:, NS1:NS2], dg[:, 0, :], start=True, stop=True)
                pe.matmul(m.bank[7][0:64, 128:256], s[:, NS3:NS4], dg[:, 1, :], start=True, stop=True)
                pe.matmul(m.bank[7][0:NC_S, 256:384], pc[:, :], dg[:, 2, :], start=True, stop=True).then_inc(s_p, 1)
                if more:
                    transpose_ck(b + 1, 1 - p)
                pe.wait_ge(s_pb[p], (b - p) * 8 * (NPG + 1) + 16 * (NPG + 1))
                pe.wait_ge(s_pe_, b + 1)
                pe.wait_ge(s_pd, b + 1)
                out = m.bank[3][:, 128:256]
                pe.matmul(out, cc[p][0:NC_S, :], pt[0:NC_S, 14, :], start=True, stop=False)
                for o in range(8):
                    pe.matmul(out, pb[p][:, o, :], pt[:, o, :], start=False, stop=False)
                for o in range(4):
                    pe.matmul(out, wv[p][:, o, :], pt[:, 8 + o, :], start=False, stop=False)
                pe.matmul(out, m.kv[0:64, 2, 384:512], pt[0:64, 12, :], start=False, stop=False)
                pe.matmul(out, m.kv[0:64, 2, 640:768], pt[0:64, 13, :], start=False, stop=True).then_inc(s_pv, 1)
                if more:
                    scores(b + 1)

            transposes(0, 0, 0, 7)
            compress(0)
            transpose_ck(0, 0)
            scores(0)
            turns(pe, turn)

        @block.scalar
        def _(act):
            def take_T(b, p, first, last_f):
                for f in range(first, last_f):
                    act.wait_ge(s_t, 7 * b + f + 1)
                    act.activation(kT[:, f * 512:(f + 1) * 512], m.bank[(7 * p + f) % 2][:, :], ACT.Copy).then_inc(s_te, 1)

            def take_c(b, p):
                act.wait_ge(s_c, b + 1)
                act.activation(cc[p][:, :], m.bank[2][:, 0:128], ACT.Copy).then_inc(s_ce, 1)
                act.wait_ge(s_ct, b + 1)
                act.activation(ck[:, :], m.bank[2][:, 128:128 + NC_S], ACT.Copy).then_inc(s_ce, 1)

            def turn(b, p, more):
                act.wait_ge(s_cm, b + 1)
                act.activation(pc[:, :], m.bank[7][:, 0:NC_S], ACT.Exp, bias=st[:, 0:1], accum_out=st[:, 1:2]).then_inc(s_ec, 1)
                if more:
                    take_T(b + 1, 1 - p, 0, 7)
                act.wait_ge(s_nm, b + 1)
                act.activation(s[:, 0:NS2], s[:, 0:NS2], ACT.Exp, bias=st[:, 2:3], accum_out=st[:, 4:5])
                act.activation(s[:, NS2:NS4], s[:, NS2:NS4], ACT.Exp, bias=st[:, 3:4], accum_out=st[:, 5:6]).then_inc(s_ex, 1)
                if more:
                    act.wait_ge(s_c, b + 2)
                    act.activation(cc[1 - p][:, :], m.bank[2][:, 0:128], ACT.Copy).then_inc(s_ce, 1)
                act.wait_ge(s_p, b + 1)
                act.activation(pt[:, 0:4, :].rearrange("p o c -> p (o c)"), m.bank[4][:, :], ACT.Copy)
                act.activation(pt[:, 4:8, :].rearrange("p o c -> p (o c)"), m.bank[5][:, :], ACT.Copy).then_inc(s_pe_, 1)
                if more:
                    act.wait_ge(s_ct, b + 2)
                    act.activation(ck[:, :], m.bank[2][:, 128:128 + NC_S], ACT.Copy).then_inc(s_ce, 1)
                act.wait_ge(s_pv, b + 1)
                for g in range(2):
                    last = act.activation(m.hnT[g * HD:(g + 1) * HD, :, bass.ds(b * TS + SEQ, TS)],
                                          m.bank[3][g * HD:(g + 1) * HD, 128 + g * 64:128 + (g + 1) * 64].rearrange("p (h t) -> p h t", t=TS), ACT.Copy)
                last.then_inc(s_o, 1)

            act.sem_inc(s_te, 2)
            act.sem_inc(s_o, 1)
            take_T(0, 0, 0, 7)
            take_c(0, 0)
            turns(act, turn)

        @block.vector
        def _(dve):
            link = Link(dve, s_chain)

            def turn(b, p, more):
                link.base, link.n = b * PER, 0
                dve.wait_ge(s_sc, 2 * b + 1)
                link(dve.tensor_reduce(st[:, 0:1], m.bank[7][:, 0:NC_S], AX.X, ALU.max))
                link(dve.tensor_scalar(st[:, 0:1], st[:, 0:1], -1.0, None, ALU.mult))
                dve.sem_inc(s_cm, 1)
                dve.wait_ge(s_ec, b + 1)
                link(dve.reciprocal(st[:, 1:2], st[:, 1:2]))
                link(dve.tensor_scalar(pc[:, :], pc[:, :], st[:, 1:2], None, ALU.mult))
                dve.sem_inc(s_pc, 1)
                new = m.new_mask[:, bass.ds(b * 64, 64)]
                link.go(dve.tensor_tensor(s[:, NS1:NS2], m.bank[7][:, 64:128], new, ALU.add))
                link.go(dve.tensor_tensor(s[:, NS3:NS4], m.bank[7][:, 128:192], new, ALU.add))
                dve.wait_ge(s_sc, 2 * b + 2)
                link.go(dve.tensor_tensor(s[:, NS2:NS3], m.bank[6][:, :], m.win_mask[:, :], ALU.add))
                dve.wait_ge(s_imp, b + 1)
                ib = m.bank[3][:, 4:60].rearrange("p (n c) -> p n c", c=4)
                before = m.bank[3][:, 3:59].rearrange("p (n c) -> p n c", c=4)
                link(dve.tensor_reduce(imp[:, :], ib[:, :, 0:3], AX.X, ALU.add))
                for half in (before[:, :, 0:1], ib[:, :, 3:4]):
                    link(dve.scalar_tensor_tensor(imp[:, :], half.rearrange("p n c -> p (n c)"), 0.5, imp[:, :], ALU.mult, ALU.add))
                link(dve.tensor_reduce(st[:, 6:7], imp[:, :], AX.X, ALU.min))
                link(dve.tensor_scalar(imp[:, :], imp[:, :], st[:, 6:7], None, ALU.is_equal))
                link(dve.tensor_tensor(imp[:, :], imp[:, :], m.blk_idx[:, 1:15], ALU.mult))
                link(dve.tensor_reduce(st[:, 7:8], imp[:, :], AX.X, ALU.max))
                link(dve.tensor_scalar(pen[:, :], m.blk_idx[:, :], st[:, 7:8], NEG, ALU.is_equal, ALU.mult))
                for i in range(2):
                    link.go(dve.tensor_tensor(s[:, i * 512:(i + 1) * 512].rearrange("p (n k) -> p n k", k=64),
                                              m.bank[4 + i][:, :].rearrange("p (n k) -> p n k", k=64),
                                              pen[:, i * 8:(i + 1) * 8].unsqueeze(2).to_broadcast((128, 8, 64)), ALU.add))
                link.wait()
                link.go(dve.tensor_reduce(st[:, 2:3], s[:, 0:NS2], AX.X, ALU.max))
                link(dve.tensor_reduce(st[:, 3:4], s[:, NS2:NS4], AX.X, ALU.max))
                link(dve.tensor_scalar(st[:, 2:4], st[:, 2:4], -1.0, None, ALU.mult))
                dve.sem_inc(s_nm, 1)
                dve.wait_ge(s_ex, b + 1)
                link(dve.reciprocal(st[:, 4:6], st[:, 4:6]))
                gate = m.gate_s[:, bass.ds(b, 1), 1:3].rearrange("p b r -> p (b r)")
                link(dve.tensor_tensor(st[:, 4:6], st[:, 4:6], gate, ALU.mult))
                for i in range(2):
                    link.go(dve.tensor_scalar(dg[:, i, :], m.ident[:, :], st[:, 4 + i:5 + i], None, ALU.mult))
                link(dve.tensor_scalar(dg[:, 2, :], m.ident[:, :], m.gate_s[:, bass.ds(b, 1), 0:1].rearrange("p b r -> p (b r)"), None, ALU.mult))
                dve.sem_inc(s_dg, 1)
                dve.wait_ge(s_p, b + 1)
                dve.tensor_copy(pt[:, 8:12, :].rearrange("p o c -> p (o c)"), m.bank[6][:, :])
                dve.tensor_copy(pt[0:64, 12:14, :].rearrange("p o c -> p (o c)"), m.bank[7][0:64, 0:256])
                dve.tensor_copy(pt[0:NC_S, 14, :], m.bank[7][0:NC_S, 256:384]).then_inc(s_pd, 1)
                assert link.n == PER, link.n
            turns(dve, turn)


BC = D // 4


def load_branch_weights(sp, m, a, tile, q):
    cols = slice(q * BC, (q + 1) * BC)
    wm_v = a.w_branch_m[0].rearrange("(k p) n -> p k n", p=128)
    wn_v = a.w_branch_n[0].rearrange("(g j d) n -> g d j n", g=2, d=HD)
    sp.dma_start(tile[:, 0, :, :], wm_v[:, :, cols]).then_inc(m.s_wb[q], 16)
    for g in range(2):
        sp.dma_start(tile[g * HD:(g + 1) * HD, 1, :, :], wn_v[g, :, :, cols]).then_inc(m.s_wb[q], 16)


def merge(nc, m, a):
    s_wo = m.sem("wout_in")
    s_ms, s_sq, s_up = m.sem("n2_ms"), m.sem("n2_sqrt"), m.sem("mg_shifted")
    s_g = m.sem("g2_in")
    s_pe, s_ev, s_chain, s_po, s_x = m.sem("mg_branch"), m.sem("mg_gated"), m.sem("mg_dve"), m.sem("mg_out"), m.sem("mg_added")
    with ExitStack() as c:
        wb = [m.wb0] + [c.enter_context(nc.sbuf_tensor(f"w_branch{q}", [128, 2, KD, BC], FP)) for q in range(1, 4)]
        wo = c.enter_context(nc.sbuf_tensor("w_o", [128, KD, D], FP))
        t1 = c.enter_context(nc.sbuf_tensor("mg_t1", [128, NTOK], FP))
        lower = c.enter_context(nc.sbuf_tensor("mg_lower", [64, 512], FP))
        mT = m.zf[:, 32:40, :]
        block = c.enter_context(nc.Block())

        @block.sync
        def _(sp):
            for q in range(1, 4):
                load_branch_weights(sp, m, a, wb[q], q)
            sp.dma_start(m.g2[:, :], a.norm2_g.to_broadcast((128, D))).then_inc(s_g, 16)
            sp.dma_start(m.br[:, :], a.b_router.to_broadcast((128, NE))).then_inc(m.s_br, 16)
            sp.dma_start(m.wr[:, :, :], a.w_router[0].rearrange("(k p) e -> p k e", p=128)).then_inc(m.s_wr, 16)
            sp.dma_start(wo[:, :, :], a.w_out[0].rearrange("(k p) n -> p k n", p=128)).then_inc(s_wo, 16)

        @block.tensor
        def _(pe):
            for f in range(KD):
                for i, h in enumerate((m.hmT, m.hnT)):
                    if f % 2 == 0 and i == 0:
                        pe.wait_ge(m.s_wb[f // 2], 48)
                    if f >= 2:
                        pe.wait_ge(s_ev, f - 1)
                    for k in range(KD):
                        last = pe.matmul(m.bank[2 * i + f % 2][:, 0:NTOK], wb[f // 2][:, i, k, f % 2 * 128:(f % 2 + 1) * 128], h[:, k, :],
                                         start=(k == 0), stop=(k == KD - 1))
                last.then_inc(s_pe, 1)
            pe.wait_ge(s_wo, 16)
            pe.wait_ge(s_ev, KD)
            n = 0
            for t in range(2):
                for h in range(2):
                    for k in range(KD):
                        last = pe.matmul(m.bank[4 + n][:, :], mT[:, k, t * 128:(t + 1) * 128],
                                         wo[:, k, h * 512:(h + 1) * 512], start=(k == 0), stop=(k == KD - 1))
                    last.then_inc(s_po, 1)
                    n += 1
            for k in range(KD):
                for h in range(2):
                    last = pe.matmul(m.bank[0][h * 64:(h + 1) * 64, :], mT[:, k, SEQ:],
                                     wo[:, k, h * 512:(h + 1) * 512], start=(k == 0), stop=(k == KD - 1))
            last.then_inc(s_po, 1)

        @block.scalar
        def _(act):
            def root(t):
                n = TILE_ROWS[t]
                act.wait_ge(s_ms, t + 1)
                act.activation(m.rstd[0:n, t:t + 1], m.rstd[0:n, t:t + 1], ACT.Sqrt).then_inc(s_sq, 1)

            root(0)
            root(1)
            act.wait_ge(s_po, 5)
            act.activation(lower[:, :], m.bank[0][64:128, :], ACT.Copy).then_inc(s_up, 1)
            root(2)

        @block.vector
        def _(dve):
            link = Link(dve, s_chain)
            squares = m.zf[:, 0:4, :].rearrange("p k n -> p (k n)")[:, 0:D]
            for f in range(KD):
                dve.wait_ge(s_pe, f + 1)
                link.go(dve.tensor_tensor(mT[:, f, :], m.bank[f % 2][:, 0:NTOK], m.zf[:, 16 + f, :], ALU.mult))
                link(dve.tensor_tensor(t1[:, :], m.bank[2 + f % 2][:, 0:NTOK], m.zf[:, 24 + f, :], ALU.mult))
                dve.tensor_tensor(mT[:, f, :], mT[:, f, :], t1[:, :], ALU.add).then_inc(s_ev, 1)
                dve.wait_ge(s_ev, f + 1)
            n = 0
            for t, rows in enumerate(TILE_ROWS):
                for h in range(2):
                    xs = m.x[0:rows, t, h * 512:(h + 1) * 512]
                    if t < 2:
                        dve.wait_ge(s_po, n + 1)
                        dve.tensor_tensor(xs, xs, m.bank[4 + n][:, :], ALU.add).then_inc(s_x, 1)
                    elif h == 0:
                        dve.wait_ge(s_po, 5)
                        dve.tensor_tensor(xs, xs, m.bank[0][0:64, :], ALU.add).then_inc(s_x, 1)
                    else:
                        dve.wait_ge(s_up, 1)
                        dve.tensor_tensor(xs, xs, lower[:, :], ALU.add).then_inc(s_x, 1)
                    n += 1
                dve.wait_ge(s_x, n)
                link(dve.tensor_tensor_reduce(out=squares[0:rows, :], in0=m.x[0:rows, t, :], in1=m.x[0:rows, t, :], scale=1.0,
                                              scalar=0.0, op0=ALU.mult, op1=ALU.add, accum_out=m.rstd[0:rows, t:t + 1]))
                rstd = m.rstd[0:rows, t:t + 1]
                link(dve.tensor_scalar(rstd, rstd, 1.0 / D, EPS, ALU.mult, ALU.add))
                dve.sem_inc(s_ms, 1)
                dve.wait_ge(s_sq, t + 1)
                link(dve.reciprocal(rstd, rstd))
                if t == 0:
                    dve.wait_ge(s_g, 16)
                dve.scalar_tensor_tensor(m.xn[0:rows, t, :], m.x[0:rows, t, :], rstd, m.g2[0:rows, :], ALU.mult, ALU.mult)


def weight_loads(sp, m, a, e, wait=None):
    for c in range(NCHUNK):
        if wait is not None:
            wait(c)
        if c < 4:
            src = a.w_gu[0, bass.ds(e, 1), c * 256:(c + 1) * 256, :].rearrange("e (j p) n -> p (e j) n", p=128)
            dst = m.wring[:, c, :].rearrange("p (j n) -> p j n", j=2)
        else:
            src = a.w_dn[0, bass.ds(e, 1), (c - 4) * 512:(c - 3) * 512, :].rearrange("e (j p) n -> p (e j) n", p=128)
            dst = m.wring[:, c, :].rearrange("p (j n) -> p j n", j=4)
        sp.dma_start(dst, src).then_inc(m.s_slot[c], 16)


def route(nc, m, a):
    s_bg, s_w, s_br = m.sem("bgu_in"), m.s_wr, m.s_br
    s_xT, s_xTe, s_z = m.sem("xn2_T"), m.sem("xn2_T_ev"), m.sem("route_zero")
    s_lg, s_mx, s_ex, s_sel = m.sem("logits"), m.sem("top_max"), m.sem("top_exp"), m.sem("sel_ready")
    s_pos, s_pT, s_pTe, s_bdn, s_chain = m.sem("pos_done"), m.sem("pos_T"), m.sem("pos_T_ev"), m.sem("bdn_in"), m.sem("route_dve")
    s_ext, s_cum, s_own, s_over, s_poso, s_wTe = (m.sem("extra_items"), m.sem("extra_cumsum"), m.sem("owner_ready"),
                                                  m.sem("overflow_done"), m.sem("pos_ready"), m.sem("wt_T_ev"))
    s_wt, s_pool = m.sem("wt_ready"), m.sem("route_pool")
    K4 = 4
    UNSEEN = 1e6
    with ExitStack() as c:
        def sb(name, shape, dt=FP):
            return c.enter_context(nc.sbuf_tensor(name, shape, dt))

        br, wr = m.br, m.wr
        wtT = m.oht[0:NE, 0:NTOK]
        xT = sb("xn2T", [128, KD, NTOK])
        lg = sb("lg", [128, NT, NE])
        mx = sb("mx8", [128, NT, 8])
        ix = sb("ix8", [128, NT, 8], U32)
        ixf = sb("ixf", [128, NT, 8])
        sm = sb("sm4", [128, NT])
        w4 = sb("w4", [128, NT, K4])
        eq = sb("eq", [128, NT, NE, K4])
        eqw = sb("eqw", [128, NT, NE, K4])
        sel = sb("sel", [128, NT, NE])
        posT = sb("posT", [NE, NTOK])
        cnt = sb("cnt", [NE, 1])
        over_thr = sb("over_thr", [NE, NTOK // SLOT - 1])
        ext = sb("ext", [NE, 1])
        cse = sb("cse", [NE, 1])
        cs = sb("cs", [NE, 1])
        from_e = sb("from_e", [NE, N_OVER])
        shift = sb("shift", [NE, N_OVER])
        own = m.of_expert[:, NE:NITEM]
        block = c.enter_context(nc.Block())

        @block.sync
        def _(sp):
            sp.dma_start(m.bgu[:, :], a.b_gu[0]).then_inc(s_bg, 16)
            for h in range(2):
                sp.dma_start(m.ys[h * SLOT:h * SLOT + NE, :], a.b_dn[0, :, h * (D // 2):(h + 1) * (D // 2)]).then_inc(s_bdn, 16)
            weight_loads(sp, m, a, 0)
            sp.wait_ge(s_bg, 16)
            sp.wait_ge(s_bdn, 32)

        @block.gpsimd
        def _(pool):
            zeroed = Link(pool, s_pool)
            pool.memset(m.pos[:, :, :], -1.0).then_inc(s_z, 1)
            pool.memset(m.wt[:, :, :], 0.0).then_inc(s_z, 1)
            pool.wait_ge(s_z, 2)
            for h in range(2):
                zeroed(pool.memset(m.ys[h * SLOT + NE:(h + 1) * SLOT, :], 0.0))
                zeroed(pool.memset(m.oht[h * SLOT + NE:(h + 1) * SLOT, 0:NTOK], 0.0))
            zeroed(pool.memset(m.oht[:, NTOK:NT * 128], 0.0))
            for t, n in enumerate(TILE_ROWS):
                pool.tensor_copy(m.acc[0:n, t, :], m.x[0:n, t, :])

        @block.tensor
        def _(pe):
            def logits(k):
                pe.wait_ge(s_xTe, k + 1)
                for t, n in enumerate(TILE_ROWS):
                    last = pe.matmul(m.bank[3][0:n, t * NE:(t + 1) * NE], xT[:, k, t * 128:t * 128 + n], wr[:, k, :],
                                     start=(k == 0 and t == 0), stop=(k == KD - 1), skip_group_check=True)
                return last

            pe.wait_ge(s_w, 16)
            for k in range(KD):
                if k >= 4:
                    pe.wait_ge(s_xTe, k - 3)
                for t, n in enumerate(TILE_ROWS):
                    last = pe.transpose(m.bank[(1, 2, 6, 7)[k % 4]][:, t * 128:t * 128 + n], m.xn[0:n, t, k * 128:(k + 1) * 128],
                                        m.ident[0:n, 0:n])
                last.then_inc(s_xT, 1)
                if k >= 2:
                    logits(k - 2)
            logits(KD - 2)
            logits(KD - 1).then_inc(s_lg, 1)
            pe.wait_ge(s_sel, 1)
            for u, nu in enumerate(TILE_ROWS):
                last = pe.matmul(m.bank[5][0:NE, 0:1], sel[0:nu, u, :], m.ones[0:nu, 0:1], start=(u == 0), stop=(u == NT - 1))
            last.then_inc(s_pos, 1)
            for t, n in enumerate(TILE_ROWS):
                for u in range(t + 1):
                    nu = TILE_ROWS[u]
                    lhs = m.tri if u == t else m.ones
                    last = pe.matmul(m.bank[4][0:n, t * NE:(t + 1) * NE], lhs[0:nu, 0:n], sel[0:nu, u, :], start=(u == 0), stop=(u == t))
            last.then_inc(s_pos, 1)
            pe.wait_ge(s_wt, 1)
            for h in range(2):
                for t, n in enumerate(TILE_ROWS):
                    last = pe.matmul(m.bank[6][h * SLOT:h * SLOT + NE, t * 128:t * 128 + n], m.wt[0:n, t, 0:NE], m.ident[0:n, 0:n],
                                     start=True, stop=True)
            last.then_inc(s_pT, 1)
            pe.wait_ge(s_ext, 1)
            pe.matmul(m.bank[0][0:NE, 0:1], m.tri[0:NE, 0:NE], ext[:, :], start=True, stop=True)
            pe.matmul(m.bank[0][0:1, 32:33], ext[:, :], m.ones[0:NE, 0:1], start=True, stop=True).then_inc(s_cum, 1)
            pe.wait_ge(s_poso, 1)
            for t, n in enumerate(TILE_ROWS):
                last = pe.transpose(m.bank[7][0:NE, t * 128:t * 128 + n], m.pos[0:n, t, 0:NE], m.ident[0:n, 0:n])
            last.then_inc(s_pT, 1)
            pe.wait_ge(s_own, 1)
            pe.matmul(m.bank[1][0:1, 0:N_OVER], m.part_idx[0:NE, 0:1], own, start=True, stop=True)
            pe.wait_ge(s_wTe, 1)
            for t, n in enumerate(TILE_ROWS):
                pe.matmul(m.bank[2][0:n, t * N_OVER:(t + 1) * N_OVER], wtT[:, t * 128:t * 128 + n], own, start=True, stop=True)
            pe.wait_ge(s_pTe, 1)
            for t, n in enumerate(TILE_ROWS):
                out = m.bank[3][0:n, t * N_OVER:(t + 1) * N_OVER]
                pe.matmul(out, posT[:, t * 128:t * 128 + n], own, start=True, stop=False)
                last = pe.matmul(out, m.ones[0:NE, 0:n], shift[:, :], start=False, stop=True)
            last.then_inc(s_over, 1)

        @block.scalar
        def _(act):
            act.wait_ge(s_mx, 1)
            act.activation(w4[:, :, :], w4[:, :, :], ACT.Exp).then_inc(s_ex, 1)
            act.wait_ge(s_pT, 1)
            act.activation(wtT, m.bank[6][0:NE, 0:NTOK], ACT.Copy).then_inc(s_wTe, 1)
            act.wait_ge(s_pT, 2)
            act.activation(posT[:, :], m.bank[7][0:NE, 0:NTOK], ACT.Copy).then_inc(s_pTe, 1)
            act.activation(m.oht[SLOT:SLOT + NE, 0:NTOK], m.bank[6][SLOT:SLOT + NE, 0:NTOK], ACT.Copy)

        @block.vector
        def _(dve):
            link = Link(dve, s_chain)
            link.go(dve.memset(lg[:, :, :], 0.0))
            link.go(dve.tensor_copy(m.of_expert[:, 0:NE], m.ident[0:NE, 0:NE]))
            link.go(dve.memset(m.of_expert[:, NITEM:NITEM + 1], 0.0))
            link.go(dve.memset(m.etab[:, NITEM:NITEM + 1], 0))
            link(dve.tensor_copy(m.etab[:, 0:NE], m.exp_idx[0:1, :]))
            for k in range(KD):
                dve.wait_ge(s_xT, k + 1)
                dve.tensor_copy(xT[:, k, :], m.bank[(1, 2, 6, 7)[k % 4]][:, 0:NTOK]).then_inc(s_xTe, 1)
            dve.wait_ge(s_lg, 1)
            dve.wait_ge(s_br, 16)
            link.go(dve.tensor_tensor(lg[:, 0:2, :], m.bank[3][:, 0:2 * NE].rearrange("p (t e) -> p t e", e=NE),
                                      br[:, :].unsqueeze(1).to_broadcast((128, 2, NE)), ALU.add))
            link(dve.tensor_tensor(lg[0:64, 2, :], m.bank[3][0:64, 2 * NE:3 * NE], br[0:64, :], ALU.add))
            for t in range(NT):
                link.go(dve.max(mx[:, t, :], lg[:, t, :]))
            link.wait()
            link(dve.tensor_tensor(w4[:, :, :], mx[:, :, 0:K4], mx[:, :, 0:1].to_broadcast((128, NT, K4)), ALU.subtract))
            dve.sem_inc(s_mx, 1)
            for t in range(NT):
                link.go(dve.max_index(ix[:, t, :], mx[:, t, :], lg[:, t, :]))
            link.wait()
            link(dve.tensor_copy(ixf[:, :, :], ix[:, :, :]))
            wide = (128, NT, NE, K4)
            link(dve.tensor_tensor(eq[:, :, :, :], m.exp_idx[:, :].unsqueeze(1).unsqueeze(3).to_broadcast(wide),
                                   ixf[:, :, 0:K4].unsqueeze(2).to_broadcast(wide), ALU.is_equal))
            link(dve.tensor_reduce(sel[:, :, :], eq[:, :, :, :], AX.X, ALU.add))
            dve.sem_inc(s_sel, 1)
            dve.wait_ge(s_ex, 1)
            link(dve.tensor_reduce(sm[:, :], w4[:, :, :], AX.X, ALU.add))
            link(dve.reciprocal(sm[:, :], sm[:, :]))
            link(dve.tensor_tensor(w4[:, :, :], w4[:, :, :], sm[:, :].unsqueeze(2).to_broadcast((128, NT, K4)), ALU.mult))
            link(dve.tensor_tensor(eqw[:, :, :, :], eq[:, :, :, :], w4[:, :, :].unsqueeze(2).to_broadcast(wide), ALU.mult))
            dve.wait_ge(s_z, 2)
            link(dve.tensor_reduce(m.wt[:, :, 0:NE], eqw[:, :, :, :], AX.X, ALU.add))
            dve.sem_inc(s_wt, 1)
            dve.wait_ge(s_pos, 1)
            link(dve.tensor_copy(cnt[:, :], m.bank[5][0:NE, 0:1]))
            link(dve.tensor_scalar(over_thr[:, :], m.thresholds[:, :], cnt[:, 0:1], None, ALU.is_lt))
            link(dve.tensor_reduce(ext[:, :], over_thr[:, :], AX.X, ALU.add))
            dve.sem_inc(s_ext, 1)
            dve.wait_ge(s_pos, 2)
            link.go(dve.scalar_tensor_tensor(m.pos[:, 0:2, 0:NE], m.bank[4][:, 0:2 * NE].rearrange("p (t e) -> p t e", e=NE), UNSEEN,
                                             sel[:, 0:2, :], ALU.add, ALU.mult))
            link(dve.scalar_tensor_tensor(m.pos[0:64, 2, 0:NE], m.bank[4][0:64, 2 * NE:3 * NE], UNSEEN, sel[0:64, 2, :], ALU.add, ALU.mult))
            link(dve.tensor_scalar(m.pos[:, :, 0:NE], m.pos[:, :, 0:NE], -UNSEEN, None, ALU.add))
            dve.sem_inc(s_poso, 1)
            dve.wait_ge(s_cum, 1)
            link(dve.tensor_copy(cse[:, :], m.bank[0][0:NE, 0:1]))
            link(dve.tensor_tensor(cs[:, :], cse[:, :], ext[:, :], ALU.add))
            link(dve.tensor_scalar(from_e[:, :], m.over_idx[:, :], cse[:, 0:1], None, ALU.is_ge))
            link(dve.scalar_tensor_tensor(own, m.over_idx[:, :], cs[:, 0:1], from_e[:, :], ALU.is_lt, ALU.mult))
            link(dve.tensor_scalar(shift[:, :], m.over_idx[:, :], cse[:, 0:1], -float(SLOT), ALU.subtract, ALU.mult))
            link(dve.scalar_tensor_tensor(shift[:, :], shift[:, :], -float(SLOT), own, ALU.add, ALU.mult))
            dve.sem_inc(s_own, 1)
            dve.tensor_scalar(m.etab[:, NITEM + 1:NITEM + 2], m.bank[0][0:1, 32:33], float(NE), None, ALU.add)
            dve.wait_ge(s_over, 1)
            dve.tensor_copy(m.etab[:, NE:NITEM], m.bank[1][0:1, 0:N_OVER])
            for dst, bank in ((m.wt, 2), (m.pos, 3)):
                dve.tensor_copy(dst[:, 0:2, NE:NITEM], m.bank[bank][:, 0:2 * N_OVER].rearrange("p (t e) -> p t e", e=N_OVER))
                dve.tensor_copy(dst[0:64, 2, NE:NITEM], m.bank[bank][0:64, 2 * N_OVER:3 * N_OVER])


def experts(nc, m, a):
    s_oh, s_ohw, s_ohe, s_g, s_xg = m.sem("ex_onehot"), m.sem("ex_onehot_w"), m.sem("ex_onehot_e"), m.sem("ex_gathered"), m.sem("ex_x")
    s_xT, s_xe = m.sem("ex_x_T"), m.sem("ex_xT_ready")
    s_used, s_gf, s_tr, s_oht = m.sem("ex_chunk_used"), m.sem("ex_gu_read"), m.sem("ex_scatter_T"), m.sem("ex_scatter_m")
    s_sc, s_acc, s_gm, s_sg = m.sem("ex_scattered"), m.sem("ex_added"), m.sem("ex_gate"), m.sem("ex_sigmoid")
    s_at, s_aT, s_ate, s_ys, s_chain = m.sem("ex_act"), m.sem("ex_act_T"), m.sem("ex_actT_ready"), m.sem("ex_y"), m.sem("ex_dve")
    PER = 4
    H = D // 2
    with ExitStack() as c:
        def sb(name, shape):
            return c.enter_context(nc.sbuf_tensor(name, shape, FP))

        oh = sb("ex_oh", [128, NT, SLOT])
        ohw = sb("ex_ohw", [128, NT, 2 * SLOT])
        ohe = sb("ex_ohe", [NE, SLOT])
        xg = sb("ex_xg", [128, H])
        xe = sb("ex_xe", [128, 4, 2, SLOT])
        gt = sb("ex_gt", [128, H])
        up = sb("ex_up", [128, H])
        sg = sb("ex_sg", [128, H])
        at = sb("ex_at", [128, H])
        atT = sb("ex_atT", [128, 4, 2, SLOT])
        oht, ys = m.oht, m.ys
        warm = sb("ex_warm", [128, 1])
        block = c.enter_context(nc.Block())

        def n_items(eng):
            return eng.value_load(m.etab[0:1, NITEM + 1:NITEM + 2], min_val=NE, max_val=NITEM)

        @block.sync
        def _(sp):
            nw = n_items(sp)
            sp.dma_start(m.gf[:, :], a.normf_g.rearrange("(o n) -> o n", o=1).to_broadcast((128, D))).then_inc(m.s_gf, 16)
            with sp.Fori(1, nw) as i:
                e = sp.value_load(m.etab[0:1, bass.ds(i, 1)], min_val=0, max_val=NE - 1)
                weight_loads(sp, m, a, e, wait=lambda ch: sp.wait_ge(s_used, NCHUNK * i + (ch + 1 - NCHUNK)))

        @block.tensor
        def _(pe):
            half = lambda bank, h: m.bank[bank][h * SLOT:(h + 1) * SLOT, :]

            def gather():
                for t, n in enumerate(TILE_ROWS):
                    for h in range(2):
                        last = pe.matmul(half(0, h), oh[0:n, t, :], m.xn[0:n, t, h * H:(h + 1) * H],
                                         start=(t == 0), stop=(t == NT - 1))
                last.then_inc(s_g, 1)

            def transpose(bank, src, sem):
                for k in range(4):
                    last = pe.matmul(m.bank[bank][:, k * 128:(k + 1) * 128], src[:, k * 128:(k + 1) * 128], m.ident[:, :],
                                     start=True, stop=True)
                last.then_inc(sem, 1)

            def scatter(i):
                pe.wait_ge(s_ys, i + 1)
                pe.wait_ge(s_oht, i + 1)
                for t in range(NT):
                    if t != 1:
                        pe.wait_ge(s_acc, 6 * i + (2 if t == 2 else 0) + 6)
                    for h in range(2):
                        pe.matmul(m.bank[(6, 4, 6)[t] + h][:, :], oht[h * SLOT:(h + 1) * SLOT, t * 128:(t + 1) * 128],
                                  ys[h * SLOT:(h + 1) * SLOT, :], start=True, stop=True).then_inc(s_sc, 1)

            nw = n_items(pe)
            pe.wait_ge(s_oh, 1)
            gather()
            pe.wait_ge(s_xg, 1)
            transpose(0, xg, s_xT)
            with pe.Fori(0, nw) as i:
                pe.wait_ge(s_ohe, i + 1)
                pe.wait_ge(s_gf, i + 1)
                for gu in range(2):
                    for h in range(2):
                        pe.matmul(half(2 + gu, h), ohe[:, :], m.bgu[:, gu * FE + h * H:gu * FE + (h + 1) * H], start=True, stop=False)
                pe.wait_ge(s_xe, i + 1)
                for k in range(KD):
                    if k % 2 == 0:
                        pe.wait_ge(m.s_slot[k // 2], 16 * i + 16)
                    for gu in range(2):
                        for h in range(2):
                            o = (k % 2) * 2 * FE + gu * FE + h * H
                            last = pe.matmul(half(2 + gu, h), xe[:, k % 4, k // 4, :], m.wring[:, k // 2, o:o + H],
                                             start=False, stop=(k == KD - 1))
                    if k % 2 == 1:
                        last.then_inc(s_used, 1)
                    if k == 3:
                        scatter(i)
                pe.wait_ge(s_ohw, i + 1)
                for t, n in enumerate(TILE_ROWS):
                    last = pe.matmul(m.bank[1][:, t * 128:t * 128 + n], ohw[0:n, t, :], m.ident[0:n, 0:n], start=True, stop=True)
                last.then_inc(s_tr, 1)
                pe.wait_ge(s_oh, i + 2)
                gather()
                pe.wait_ge(s_at, i + 1)
                pe.wait_ge(s_acc, 6 * i + 10)
                transpose(5, at, s_aT)
                pe.wait_ge(s_xg, i + 2)
                transpose(0, xg, s_xT)
                pe.wait_ge(s_ate, i + 1)
                for k in range(8):
                    if k % 4 == 0:
                        pe.wait_ge(m.s_slot[4 + k // 4], 16 * i + 16)
                    for h in range(2):
                        o = (k % 4) * D + h * H
                        last = pe.matmul(half(4, h), atT[:, k % 4, k // 4, :], m.wring[:, 4 + k // 4, o:o + H],
                                         start=(k == 0), stop=(k == 7))
                    if k % 4 == 3:
                        last.then_inc(s_used, 1)
            scatter(nw)

        @block.scalar
        def _(act):
            def copy(dst, bank, sem):
                act.activation(dst, m.bank[bank][:, :], ACT.Copy).then_inc(sem, 1)

            flat = lambda t: t[:, :, :, :].rearrange("p k h s -> p (k h s)")
            nw = n_items(act)
            act.activation(warm[:, :], m.ones[:, 0:1], ACT.Sigmoid)
            act.wait_ge(s_g, 1)
            copy(xg[:, :], 0, s_xg)
            act.wait_ge(s_xT, 1)
            copy(flat(xe), 0, s_xe)
            with act.Fori(0, nw) as i:
                act.wait_ge(s_tr, i + 1)
                act.wait_ge(s_sc, 6 * i + 6)
                act.activation(oht[:, 0:NTOK], m.bank[1][:, 0:NTOK], ACT.Copy).then_inc(s_oht, 1)
                act.wait_ge(s_gm, i + 1)
                act.activation(sg[:, :], gt[:, :], ACT.Sigmoid, scale=1.702).then_inc(s_sg, 1)
                act.wait_ge(s_g, i + 2)
                copy(xg[:, :], 0, s_xg)
                act.wait_ge(s_aT, i + 1)
                copy(flat(atT), 5, s_ate)
                act.wait_ge(s_xT, i + 2)
                copy(flat(xe), 0, s_xe)
                act.wait_ge(s_used, NCHUNK * i + NCHUNK)
                copy(ys[:, :], 4, s_ys)

        @block.vector
        def _(dve):
            link = Link(dve, s_chain)

            def one_hot(i):
                for t, n in enumerate(TILE_ROWS):
                    last = dve.tensor_scalar(oh[0:n, t, :], m.slot_idx[0:n, 0:SLOT], m.pos[0:n, t, bass.ds(i, 1)], None, ALU.is_equal)
                last.then_inc(s_oh, 1)

            def of_expert(i):
                dve.tensor_copy(ohe[:, :], m.of_expert[:, bass.ds(i, 1)].to_broadcast((NE, SLOT))).then_inc(s_ohe, 1)

            def add_scattered(i):
                for r in range(2 * NT):
                    n = TILE_ROWS[r // 2]
                    part = m.acc[0:n, r // 2, (r % 2) * H:(r % 2 + 1) * H]
                    dve.wait_ge(s_sc, 6 * i + r + 1)
                    dve.tensor_tensor(part, part, m.bank[(6, 4, 6)[r // 2] + r % 2][0:n, :], ALU.add).then_inc(s_acc, 1)

            nw = n_items(dve)
            dve.sem_inc(s_gf, 1)
            dve.sem_inc(s_acc, 6)
            dve.sem_inc(s_ys, 1)
            dve.sem_inc(s_oht, 1)
            one_hot(0)
            of_expert(0)
            with dve.Fori(0, nw) as i:
                link.base, link.n = i * PER, 0
                dve.wait_ge(s_g, i + 1)
                one_hot(i + 1)
                dve.wait_ge(s_oht, i + 1)
                for t, n in enumerate(TILE_ROWS):
                    last = dve.tensor_scalar(ohw[0:n, t, :], m.slot_idx[0:n, :], m.pos[0:n, t, bass.ds(i, 1)],
                                             m.wt[0:n, t, bass.ds(i, 1)], ALU.is_equal, ALU.mult)
                last.then_inc(s_ohw, 1)
                dve.wait_ge(s_acc, 6 * i + 6)
                add_scattered(i)
                dve.wait_ge(s_used, NCHUNK * i + 4)
                link(dve.tensor_scalar(gt[:, :], m.bank[2][:, :], 7.0, None, ALU.min))
                dve.sem_inc(s_gm, 1)
                link(dve.tensor_scalar(up[:, :], m.bank[3][:, :], 7.0, -7.0, ALU.min, ALU.max))
                dve.sem_inc(s_gf, 1)
                link(dve.scalar_tensor_tensor(up[:, :], up[:, :], 1.0, gt[:, :], ALU.add, ALU.mult))
                dve.wait_ge(s_sg, i + 1)
                link(dve.tensor_tensor(at[:, :], up[:, :], sg[:, :], ALU.mult))
                dve.sem_inc(s_at, 1)
                assert link.n == PER, link.n
                of_expert(i + 1)
            dve.wait_ge(s_acc, 6 * nw + 6)
            add_scattered(nw)


def finish(nc, m, a):
    s_sum, s_ms, s_sq, s_chain, s_y, s_out = (m.sem("fin_squares"), m.sem("fin_ms"), m.sem("fin_sqrt"),
                                              m.sem("fin_dve"), m.sem("y_ready"), m.sem("y_out"))
    y = [a.y_prompt[0, 0:128], a.y_prompt[0, 128:256], a.y_sample.rearrange("b t d -> (b t) d")]
    with ExitStack() as c:
        squares = [c.enter_context(nc.sbuf_tensor(f"fin_squares{i}", [128, D], FP)) for i in range(2)]
        ss = c.enter_context(nc.sbuf_tensor("ss3", [128, NT], FP))
        block = c.enter_context(nc.Block())

        @block.sync
        def _(sp):
            for t, n in enumerate(TILE_ROWS):
                sp.wait_ge(s_y, t + 1)
                sp.dma_start(y[t], m.acc[0:n, t, :]).then_inc(s_out, 16)
            sp.wait_ge(s_out, 16 * NT)

        @block.scalar
        def _(act):
            act.activation(squares[1][:, :], m.acc[:, 1, :], ACT.Square, accum_out=ss[:, 1:2]).then_inc(s_sum, 1)
            act.wait_ge(s_ms, 1)
            act.activation(ss[:, :], ss[:, :], ACT.Sqrt).then_inc(s_sq, 1)

        @block.vector
        def _(dve):
            link = Link(dve, s_chain)
            link(dve.memset(ss[64:128, 2:3], 1.0))
            for t in (0, 2):
                n = TILE_ROWS[t]
                link(dve.tensor_tensor_reduce(out=squares[0][0:n, :], in0=m.acc[0:n, t, :], in1=m.acc[0:n, t, :], scale=1.0,
                                              scalar=0.0, op0=ALU.mult, op1=ALU.add, accum_out=ss[0:n, t:t + 1]))
            dve.wait_ge(s_sum, 1)
            link(dve.tensor_scalar(ss[:, :], ss[:, :], 1.0 / D, EPS, ALU.mult, ALU.add))
            dve.sem_inc(s_ms, 1)
            dve.wait_ge(m.s_gf, 16)
            dve.wait_ge(s_sq, 1)
            link(dve.reciprocal(ss[:, :], ss[:, :]))
            for t, n in enumerate(TILE_ROWS):
                dve.scalar_tensor_tensor(m.acc[0:n, t, :], m.acc[0:n, t, :], ss[0:n, t:t + 1], m.gf[0:n, :], ALU.mult,
                                         ALU.mult).then_inc(s_y, 1)


def allocate(nc, m, c):
    def sb(name, shape, dt=FP):
        return c.enter_context(nc.sbuf_tensor(name, shape, dt))

    m.bank = [c.enter_context(nc.psum_tensor(f"bank{i}", [128, 512], FP)) for i in range(8)]
    m.ident = sb("ident", [128, 128])
    m.ones = sb("ones", [128, 128])
    m.tri = sb("tri", [128, 128])
    m.causal_st = sb("causal_st", [128, 128])
    m.causal_tk = sb("causal_tk", [128, 128])
    m.same_seq = sb("same_seq", [64, 64])
    m.seq_onehot = sb("seq_onehot", [64, NB])
    m.cmp_mask = sb("cmp_mask", [128, 2, NC_P])
    m.new_mask = sb("new_mask", [128, NB * 64])
    m.win_mask = sb("win_mask", [128, WIN])
    m.peer = sb("peer", [128, 128])
    m.blk_idx = sb("blk_idx", [128, 16])
    m.slot_idx = sb("slot_idx", [128, 2 * SLOT])
    m.part_idx = sb("part_idx", [128, 1])
    m.exp_idx = sb("exp_idx", [128, NE])
    m.over_idx = sb("over_idx", [NE, N_OVER])
    m.thresholds = sb("thresholds", [NE, NTOK // SLOT - 1])
    m.rstd = sb("rstd2", [128, NT])
    m.x = sb("x", [128, NT, D])


def allocate_mixers(nc, m, c):
    def sb(name, shape, dt=FP):
        return c.enter_context(nc.sbuf_tensor(name, shape, dt))

    m.par = sb("par", [128, 7, KD])
    m.bias_feat = sb("bias_feat", [128, 40])
    m.zf = sb("zf", [128, 40, NTOK])
    m.kv = sb("kv", [128, NT, KVC])
    m.ngate = sb("ngate", [128, NT, 48])
    m.gate_bias = sb("gate_bias", [MH, 2])
    m.hmT = m.zf[:, 0:KD, :]
    m.hnT = m.zf[:, KD:2 * KD, :]


def allocate_projection(nc, m, proj, cell, rows):
    def sb(name, shape, scope):
        return scope.enter_context(nc.sbuf_tensor(name, shape, FP))

    m.v = sb("v", [128, NT, MH, VX], cell)
    right = lambda name, shape: rows.enter_context(nc.sbuf_tensor(name, shape, FP, side="right"))
    m.gate_rows = right("gate_rows", [MH, 2, NTOK])
    m.seg_mul = right("seg_mul", [MH, NTOK])
    m.seg_add = right("seg_add", [MH, NTOK])
    m.reused = sb("reused", [128, KD * NTOK + 4 * MH * DQK], cell)
    o = KD * NTOK
    m.xc = m.reused[:, 0:o].rearrange("p (k n) -> p k n", n=NTOK)
    m.wq = m.reused[:, o:o + 2 * MH * DQK].rearrange("p (i d) -> p i d", d=DQK)
    m.wk = m.reused[:, o + 2 * MH * DQK:].rearrange("p (i d) -> p i d", d=DQK)
    m.uT = sb("uT", [128, KD, NTOK], proj)
    m.bias_tok = sb("bias_tok", [128, D + OFF_BG - OFF_NKV], proj)
    m.w_slots = sb("w_slots", [128, NSL, KD, 512], proj)
    m.w_gates = sb("w_gates", [128, KD, 8], proj)
    m.s_win = [m.sem(f"win_slot{i}") for i in range(NSL)]
    m.s_wg, m.s_wqk = m.sem("wgate_in"), m.sem("wqk_in")


def allocate_mlstm(nc, m, c):
    def sb(name, shape, dt=FP):
        return c.enter_context(nc.sbuf_tensor(name, shape, dt))

    m.ce = sb("state_ce", [128, NB, MH, VX])
    m.n0 = sb("n0_rows", [NB * MH, DQK])
    m.s_c0, m.s_n0 = m.sem("C0_in"), m.sem("n0_in")
    m.mqT = sb("mqT", [128, MH, NTOK])
    m.mkT = sb("mkT", [128, MH, NTOK])
    m.mk = sb("mk", [128, MH, 3 * DQK])
    m.grow = sb("grow", [MH, NTOK + 64 + NB])
    m.gcol = sb("gcol", [128, NT, 3, MH])


def allocate_nsa(nc, m, c):
    def sb(name, shape, dt=FP):
        return c.enter_context(nc.sbuf_tensor(name, shape, dt))

    m.pages_k = [sb(f"ns_pa{p}", [128, NPG, 384]) for p in range(2)]
    m.pages_v = [sb(f"ns_pb{p}", [128, NPG, 128]) for p in range(2)]
    m.win_k = [sb(f"ns_wk{p}", [128, WIN // 128, 128]) for p in range(2)]
    m.win_v = [sb(f"ns_wv{p}", [128, WIN // 128, 128]) for p in range(2)]
    m.s_pa = [m.sem(f"pages_k_slot{p}") for p in range(2)]
    m.s_pb = [m.sem(f"pages_v_slot{p}") for p in range(2)]
    m.s_pages = m.sem("pages_in")
    m.bcmp_row = sb("bcmp_row", [128, 2 * 128])
    m.kT = sb("kT", [128, 4, NTOK])
    m.ckp = sb("ckp", [128, NC_P])
    m.cvp = sb("cvp", [NC_P, 128])
    m.gate_s = sb("gate_s", [128, NB, 3])
    m.pages = sb("pages", [1, NB * NPG], I32)
    m.qbd = sb("qbd", [128, 128])
    m.key_mask = sb("key_mask", [128, SEQ])


def allocate_router(nc, m, c):
    def sb(name, shape):
        return c.enter_context(nc.sbuf_tensor(name, shape, FP, side="right"))

    m.xn = sb("xn2", [128, NT, D])
    m.g2 = sb("g2b", [128, D])
    m.br = sb("brb", [128, NE])
    m.wr = sb("w_r", [128, KD, NE])
    m.s_br, m.s_wr = m.sem("br_in"), m.sem("wr_in")


def allocate_moe(nc, m, c):
    def sb(name, shape, dt=FP):
        return c.enter_context(nc.sbuf_tensor(name, shape, dt))

    m.wring = sb("wring", [128, NCHUNK, 4096])
    m.s_slot = [m.sem(f"chunk{i}_in") for i in range(NCHUNK)]
    m.acc = sb("acc", [128, NT, D])
    m.pos = sb("pos", [128, NT, NITEM + 1])
    m.wt = sb("wt", [128, NT, NITEM + 1])
    m.bgu = sb("bgu", [NE, 2 * FE])
    m.of_expert = sb("of_expert", [NE, NITEM + 1])
    m.ys = sb("ex_ys", [128, D // 2])
    m.oht = sb("ex_oht", [128, NT * 128])
    m.gf = sb("gf", [128, D])
    m.s_gf = m.sem("gf_in")
    m.etab = sb("etab", [1, NITEM + 2], I32)


def hybrid_step(nc, a):
    with ExitStack() as c:
        m = Mem()
        done_with = []

        def sem(name):
            done_with.append(nc.alloc_semaphore(name))
            return done_with[-1]

        m.sem = sem
        allocate(nc, m, c)
        with ExitStack() as mix:
            allocate_mixers(nc, m, mix)
            compress = mix.enter_context(ExitStack())
            with ExitStack() as cell:
                with ExitStack() as rows:
                    with ExitStack() as proj:
                        allocate_projection(nc, m, proj, cell, rows)
                        start(nc, m, a)
                        project(nc, m, a)
                    allocate_mlstm(nc, m, cell)
                    mlstm_gates(nc, m, a)
                m.wc = compress.enter_context(nc.sbuf_tensor("wc", [128, 2 * CMP, 128], FP, side="right"))
                mlstm_heads(nc, m, a)
            nc.clear_and_free_semaphores(done_with)
            with nc.Block():
                pass
            m.wb0 = mix.enter_context(nc.sbuf_tensor("w_branch0", [128, 2, KD, BC], FP))
            m.s_wb = [m.sem(f"w_branch{q}_in") for q in range(4)]
            with ExitStack() as attn:
                allocate_nsa(nc, m, attn)
                nsa_prepare(nc, m, a)
                nsa_prompt(nc, m, a)
                nsa_sample(nc, m, a)
            compress.close()
            allocate_router(nc, m, c)
            merge(nc, m, a)
        allocate_moe(nc, m, c)
        route(nc, m, a)
        experts(nc, m, a)
        finish(nc, m, a)


_INS = ['x_prompt', 'x_sample', 'cache_kv', 'cache_win_kv', 'state_conv', 'state_C', 'state_n', 'state_m',
        'page_table', 'norm1_g', 'w_in', 'b_in', 'w_conv', 'b_conv', 'w_mq', 'w_mk', 'g_mnorm', 'w_cmp', 'b_cmp',
        'w_branch_m', 'w_branch_n', 'w_out', 'norm2_g', 'w_router', 'b_router', 'w_gu', 'b_gu', 'w_dn', 'b_dn',
        'normf_g']
_OUTS = [('y_prompt', (1, 256, 1024)), ('y_sample', (8, 8, 1024)), ('new_kv_p', (1, 256, 1, 4, 2, 64)),
         ('new_win_p', (1, 1, 256, 2, 2, 64)), ('new_conv_p', (1, 1, 3, 1024)), ('new_C_p', (1, 1, 4, 128, 256)),
         ('new_n_p', (1, 1, 4, 128)), ('new_m_p', (1, 1, 4)), ('new_kv_s', (8, 8, 1, 4, 2, 64)),
         ('new_win_s', (1, 8, 512, 2, 2, 64)), ('new_conv_s', (1, 8, 3, 1024)), ('new_C_s', (1, 8, 4, 128, 256)),
         ('new_n_s', (1, 8, 4, 128)), ('new_m_s', (1, 8, 4))]


class Args:
    pass


def kernel(**inputs):
    import numpy as np
    import concourse.bacc as bacc
    from concourse.bass_utils import run_bass_kernel_spmd

    nc = bacc.Bacc("TRN2", target_bir_lowering=False, num_devices=1)
    arrays, a = {}, Args()
    for name in _INS:
        arr = np.ascontiguousarray(inputs[name])
        arrays[name] = arr
        a.__dict__[name] = nc.dram_tensor(name, arr.shape, mybir.dt.from_np(arr.dtype), kind="ExternalInput").ap()
    for name, shape in _OUTS:
        a.__dict__[name] = nc.dram_tensor(name, shape, FP, kind="ExternalOutput").ap()
    hybrid_step(nc, a)
    r = run_bass_kernel_spmd(nc, [arrays], core_ids=[0])
    return tuple(r.results[0][name] for name, _ in _OUTS)
```
